# Optimizing a Trainium2 kernel written in Bass

```python
import jax, jax.numpy as jnp
from jax import lax
import numpy as np
import math
import jax
import jax.numpy as jnp

D_MODEL = 1024
BATCH = 1
SEQ = 256
DEPTH = 1

CONV_DIM = 512
CONV_WIDTH = 31
GLA_HEADS = 4
GLA_DK = 128
GLA_DV = 256
GLA_LOWRANK = 16
GLA_TAU = 16.0
GLA_CHUNK = 64
QK_DIM = GLA_HEADS * GLA_DK
V_DIM = GLA_HEADS * GLA_DV
N_BRANCH = 2
N_GROUPS = 4
EXPERTS_PER_GROUP = 8
N_EXPERTS = N_GROUPS * EXPERTS_PER_GROUP
TOP_K = 2
D_EXPERT = 512
EPS = 1e-6
N_MOD = 6
IN_SIZES = (2 * CONV_DIM, QK_DIM, QK_DIM, V_DIM, V_DIM, GLA_LOWRANK, N_BRANCH * D_MODEL)
IN_DIM = 2 * CONV_DIM + 2 * QK_DIM + 2 * V_DIM + GLA_LOWRANK + N_BRANCH * D_MODEL


def rmsnorm(x, g):
    x32 = x.astype(jnp.float32)
    y = x32 * lax.rsqrt(jnp.mean(x32 * x32, axis=-1, keepdims=True) + EPS)
    return (y * g.astype(jnp.float32)).astype(x.dtype)

def layernorm(x, g, b):
    x32 = x.astype(jnp.float32)
    mu = jnp.mean(x32, axis=-1, keepdims=True)
    xc = x32 - mu
    var = jnp.mean(xc * xc, axis=-1, keepdims=True)
    y = xc * lax.rsqrt(var + EPS) * g.astype(jnp.float32) + b.astype(jnp.float32)
    return y.astype(x.dtype)

def modulate(x, shift, scale):
    return x * (1.0 + scale[:, None, :]) + shift[:, None, :]

def conv_module(u, w_dw, b_dw, ln_g, ln_b, w_pw, b_pw):
    a, gt = jnp.split(u, 2, axis=-1)
    z = a * jax.nn.sigmoid(gt)
    z = lax.conv_general_dilated(
        z, w_dw, window_strides=(1,), padding=[(CONV_WIDTH - 1, 0)],
        dimension_numbers=("NWC", "WIO", "NWC"), feature_group_count=CONV_DIM) + b_dw
    z = jax.nn.silu(layernorm(z, ln_g, ln_b))
    return z @ w_pw + b_pw

def gla_chunked(q, k, v, logg):
    B, S, H, _ = q.shape
    n_chunks = S // GLA_CHUNK

    def to_chunks(t):
        return t.reshape(B, n_chunks, GLA_CHUNK, H, t.shape[-1]).transpose(1, 0, 3, 2, 4)

    causal = jnp.tril(jnp.ones((GLA_CHUNK, GLA_CHUNK), dtype=bool))[:, :, None]

    def step(state, inp):
        qc, kc, vc, gc = inp
        b = jnp.cumsum(gc, axis=2)
        o_inter = jnp.einsum("bhcd,bhde->bhce", qc * jnp.exp(b), state)
        diff = b[:, :, :, None, :] - b[:, :, None, :, :]
        decay = jnp.exp(jnp.where(causal, diff, -jnp.inf))
        attn = jnp.einsum("bhid,bhijd,bhjd->bhij", qc, decay, kc)
        o_intra = jnp.einsum("bhij,bhje->bhie", attn, vc)
        b_last = b[:, :, -1:, :]
        new_state = (jnp.exp(b_last[:, :, 0, :])[..., None] * state
                     + jnp.einsum("bhcd,bhce->bhde", kc * jnp.exp(b_last - b), vc))
        return new_state, o_inter + o_intra

    state0 = jnp.zeros((B, H, q.shape[-1], v.shape[-1]), jnp.float32)
    _, outs = lax.scan(step, state0, (to_chunks(q), to_chunks(k), to_chunks(v), to_chunks(logg)))
    return outs.transpose(1, 0, 3, 2, 4).reshape(B, S, H, v.shape[-1])

def hybrid_mixer(u, w_in, w_dw, b_dw, g_conv_ln, b_conv_ln, w_conv_pw, b_conv_pw,
                 w_a2, b_a2, g_gla_norm, w_gla_o, w_out):
    B, S, _ = u.shape
    proj = u @ w_in
    offs = np.cumsum(IN_SIZES)[:-1].tolist()
    p_conv, q, k, v, r, a1, gates = jnp.split(proj, offs, axis=-1)
    y_conv = conv_module(p_conv, w_dw, b_dw, g_conv_ln, b_conv_ln, w_conv_pw, b_conv_pw)
    q = q.reshape(B, S, GLA_HEADS, GLA_DK).astype(jnp.float32) * (GLA_DK ** -0.5)
    k = k.reshape(B, S, GLA_HEADS, GLA_DK).astype(jnp.float32)
    v = v.reshape(B, S, GLA_HEADS, GLA_DV).astype(jnp.float32)
    logg = jax.nn.log_sigmoid((a1 @ w_a2 + b_a2).astype(jnp.float32)) / GLA_TAU
    logg = logg.reshape(B, S, GLA_HEADS, GLA_DK)
    o = gla_chunked(q, k, v, logg)
    o = rmsnorm(o, g_gla_norm.reshape(GLA_HEADS, GLA_DV)).reshape(B, S, V_DIM).astype(u.dtype)
    y_gla = (o * jax.nn.silu(r)) @ w_gla_o
    gt = jax.nn.sigmoid(gates).reshape(B, S, N_BRANCH, D_MODEL)
    merged = gt[:, :, 0, :] * y_conv + gt[:, :, 1, :] * y_gla
    return merged @ w_out

def hierarchical_moe(h, w_rg, b_rg, w_re, b_re, w1, w3, w2):
    B, S, D = h.shape
    t = h.reshape(B * S, D)
    lg = (t @ w_rg + b_rg).astype(jnp.float32)
    pg = jax.nn.softmax(lg, axis=-1)
    _, gsel = lax.top_k(lg, 1)
    wg = jnp.take_along_axis(pg, gsel, axis=1)
    le = (t @ w_re + b_re).astype(jnp.float32).reshape(-1, N_GROUPS, EXPERTS_PER_GROUP)
    le_sel = jnp.take_along_axis(le, gsel[:, :, None], axis=1)[:, 0, :]
    top_v, top_i = lax.top_k(le_sel, TOP_K)
    w = jax.nn.softmax(top_v, axis=-1) * wg
    eid = gsel * EXPERTS_PER_GROUP + top_i
    comb = jnp.einsum("tk,tke->te", w, jax.nn.one_hot(eid, N_EXPERTS, dtype=jnp.float32))
    y = jnp.zeros((B * S, D), jnp.float32)
    for e in range(N_EXPERTS):
        hid = jax.nn.silu(t @ w1[e]) * (t @ w3[e])
        y = y + comb[:, e:e + 1] * (hid @ w2[e]).astype(jnp.float32)
    return y.astype(h.dtype).reshape(B, S, D)

def first_inputs(seed: int = 0) -> dict:
    key = jax.random.key(seed)
    ks = jax.random.split(key, 32)
    f32 = jnp.float32
    L, D = DEPTH, D_MODEL

    def nrm(k, shape, scale):
        return jax.random.normal(k, shape, f32) * scale

    def gain(k, shape):
        return 1.0 + 0.05 * jax.random.normal(k, shape, f32)

    return {
        "x": jax.random.normal(ks[0], (BATCH, SEQ, D), f32),
        "c": jax.random.normal(ks[1], (BATCH, D), f32),
        "w_ada": nrm(ks[2], (L, D, N_MOD * D), 0.5 * D ** -0.5),
        "b_ada": nrm(ks[3], (L, N_MOD * D), 0.02),
        "g_norm1": gain(ks[4], (L, D)),
        "w_in": nrm(ks[5], (L, D, IN_DIM), D ** -0.5),
        "w_dw": nrm(ks[6], (L, CONV_WIDTH, 1, CONV_DIM), CONV_WIDTH ** -0.5),
        "b_dw": nrm(ks[7], (L, CONV_DIM), 0.02),
        "g_conv_ln": gain(ks[8], (L, CONV_DIM)),
        "b_conv_ln": nrm(ks[9], (L, CONV_DIM), 0.02),
        "w_conv_pw": nrm(ks[10], (L, CONV_DIM, D), CONV_DIM ** -0.5),
        "b_conv_pw": nrm(ks[11], (L, D), 0.02),
        "w_a2": nrm(ks[12], (L, GLA_LOWRANK, QK_DIM), GLA_LOWRANK ** -0.5),
        "b_a2": nrm(ks[13], (L, QK_DIM), 0.02),
        "g_gla_norm": gain(ks[14], (L, V_DIM)),
        "w_gla_o": nrm(ks[15], (L, V_DIM, D), V_DIM ** -0.5),
        "w_out": nrm(ks[16], (L, D, D), D ** -0.5),
        "g_norm2": gain(ks[17], (L, D)),
        "w_router_g": nrm(ks[18], (L, D, N_GROUPS), D ** -0.5),
        "b_router_g": nrm(ks[19], (L, N_GROUPS), 0.01),
        "w_router_e": nrm(ks[20], (L, D, N_EXPERTS), D ** -0.5),
        "b_router_e": nrm(ks[21], (L, N_EXPERTS), 0.01),
        "w1": nrm(ks[22], (L, N_EXPERTS, D, D_EXPERT), D ** -0.5),
        "w3": nrm(ks[23], (L, N_EXPERTS, D, D_EXPERT), D ** -0.5),
        "w2": nrm(ks[24], (L, N_EXPERTS, D_EXPERT, D), D_EXPERT ** -0.5),
        "w_ada_f": nrm(ks[25], (D, 2 * D), 0.5 * D ** -0.5),
        "b_ada_f": nrm(ks[26], (2 * D,), 0.02),
        "g_final": gain(ks[27], (D,)),
    }

def first_block(x, c, w_ada, b_ada, g_norm1, w_in, w_dw, b_dw, g_conv_ln, b_conv_ln,
              w_conv_pw, b_conv_pw, w_a2, b_a2, g_gla_norm, w_gla_o, w_out, g_norm2,
              w_router_g, b_router_g, w_router_e, b_router_e, w1, w3, w2,
              w_ada_f, b_ada_f, g_final):
    h = x
    c_act = jax.nn.silu(c)
    for l in range(DEPTH):
        mod = c_act @ w_ada[l] + b_ada[l]
        sh1, sc1, ga1, sh2, sc2, ga2 = jnp.split(mod, N_MOD, axis=-1)
        u = modulate(rmsnorm(h, g_norm1[l]), sh1, sc1)
        y = hybrid_mixer(u, w_in[l], w_dw[l], b_dw[l], g_conv_ln[l], b_conv_ln[l],
                         w_conv_pw[l], b_conv_pw[l], w_a2[l], b_a2[l], g_gla_norm[l],
                         w_gla_o[l], w_out[l])
        h = h + ga1[:, None, :] * y
        u2 = modulate(rmsnorm(h, g_norm2[l]), sh2, sc2)
        y2 = hierarchical_moe(u2, w_router_g[l], b_router_g[l], w_router_e[l], b_router_e[l],
                              w1[l], w3[l], w2[l])
        h = h + ga2[:, None, :] * y2
    modf = c_act @ w_ada_f + b_ada_f
    shf, scf = jnp.split(modf, 2, axis=-1)
    return modulate(rmsnorm(h, g_final), shf, scf)


DEPTH_2 = 2

D_MIX = D_MODEL
HEAD_DIM = 64
RWKV_WIDTH = D_MIX // 2
RWKV_HEADS = RWKV_WIDTH // HEAD_DIM
MOBA_WIDTH = D_MIX - RWKV_WIDTH
MOBA_HEADS = MOBA_WIDTH // HEAD_DIM
DECAY_LORA = 64
ICLR_LORA = 64
GATE_LORA = 128
RWKV_PROJ = 3 * RWKV_WIDTH + DECAY_LORA + ICLR_LORA + GATE_LORA
MOBA_PROJ = 3 * MOBA_WIDTH
D_PROJ = RWKV_PROJ + MOBA_PROJ
LNX_EPS = 64e-5
MOBA_BLOCK = 256
MOBA_TOPK = 3
MOBA_Q_CHUNK = 16
REL_BUCKETS = 32
REL_MAX_DISTANCE = 1024
MEM_LEN = 256
XATTN_HEADS = 4
XATTN_HEAD_DIM = D_MODEL // XATTN_HEADS
D_FF = ((8 * D_MODEL // 3 + 127) // 128) * 128
FFN_RES_WEIGHT = 0.5
NORM_EPS = 1e-6


def rms_norm(x, g):
    xf = x.astype(jnp.float32)
    y = xf * lax.rsqrt(jnp.mean(xf * xf, axis=-1, keepdims=True) + NORM_EPS)
    return (y * g.astype(jnp.float32)).astype(x.dtype)

def swiglu_ffn(h, w_in, w_out):
    gate, up = jnp.split(h @ w_in, 2, axis=-1)
    return (jax.nn.silu(gate) * up) @ w_out

def token_shift(z):
    return jnp.pad(z, ((0, 0), (1, 0), (0, 0)))[:, :-1]

def rel_bucket(dist):
    n = jnp.maximum(dist, 0)
    max_exact = REL_BUCKETS // 2
    nf = jnp.maximum(n, 1).astype(jnp.float32)
    large = max_exact + (jnp.log(nf / max_exact) / math.log(REL_MAX_DISTANCE / max_exact)
                         * (REL_BUCKETS - max_exact)).astype(jnp.int32)
    large = jnp.minimum(large, REL_BUCKETS - 1)
    return jnp.where(n < max_exact, n, large)

def rwkv7_time_mix(p, mu, w0, w_up, a0, a_up, g_up, k_k, k_a, r_k, ln_g, ln_b):
    B, S, _ = p.shape
    H, Dh, W = RWKV_HEADS, HEAD_DIM, RWKV_WIDTH
    dt = p.dtype
    f32 = jnp.float32
    p = p + (token_shift(p) - p) * mu
    r, k, v, w_lo, a_lo, g_lo = jnp.split(
        p, [W, 2 * W, 3 * W, 3 * W + DECAY_LORA, 3 * W + DECAY_LORA + ICLR_LORA], axis=-1)
    w_log = -jax.nn.softplus(-(w0 + jnp.tanh(w_lo) @ w_up).astype(f32)) - 0.5
    decay = jnp.exp(-jnp.exp(w_log))
    a = jax.nn.sigmoid(a0 + a_lo @ a_up)
    g = jax.nn.sigmoid(g_lo) @ g_up
    kk = k * k_k
    k = k * (1 + (a - 1) * k_a)
    heads = lambda z: z.reshape(B, S, H, Dh).astype(f32)
    r, k, v, a, decay, kk = (heads(z) for z in (r, k, v, a, decay, kk))
    kk = kk / jnp.maximum(jnp.sqrt(jnp.sum(kk * kk, axis=-1, keepdims=True)), 1e-12)
    b = kk * a

    def step(state, inp):
        r_t, w_t, k_t, v_t, kk_t, b_t = inp
        sa = jnp.einsum('bhij,bhj->bhi', state, -kk_t)
        state = (state * w_t[:, :, None, :] + sa[..., None] * b_t[:, :, None, :]
                 + v_t[..., None] * k_t[:, :, None, :])
        return state, jnp.einsum('bhij,bhj->bhi', state, r_t)

    tm = lambda z: jnp.swapaxes(z, 0, 1)
    state0 = jnp.zeros((B, H, Dh, Dh), f32)
    _, y = lax.scan(step, state0, tuple(tm(z) for z in (r, decay, k, v, kk, b)))
    y = tm(y)
    mean = jnp.mean(y, axis=-1, keepdims=True)
    var = jnp.mean(jnp.square(y - mean), axis=-1, keepdims=True)
    y = ((y - mean) * lax.rsqrt(var + LNX_EPS)).reshape(B, S, W) * ln_g + ln_b
    bonus = jnp.sum(r * k * r_k, axis=-1, keepdims=True) * v
    y = y + bonus.reshape(B, S, W)
    return (y * g).astype(dt)

def moba_attention(q, k, v, rel_bias):
    B, S, _ = q.shape
    H, Dh, BLK, QC = MOBA_HEADS, HEAD_DIM, MOBA_BLOCK, MOBA_Q_CHUNK
    f32 = jnp.float32
    nb = -(-S // BLK)
    pad = nb * BLK - S
    to_heads = lambda z: z.reshape(B, S, H, Dh).transpose(0, 2, 1, 3)
    q = to_heads(q) * (Dh ** -0.5)
    k = jnp.pad(to_heads(k), ((0, 0), (0, 0), (0, pad), (0, 0)))
    v = jnp.pad(to_heads(v), ((0, 0), (0, 0), (0, pad), (0, 0)))
    kb = k.reshape(B, H, nb, BLK, Dh)
    vb = v.reshape(B, H, nb, BLK, Dh)
    k_mean = jnp.mean(kb.astype(f32), axis=3).astype(q.dtype)
    topk = min(MOBA_TOPK, nb)
    n_chunks = S // QC
    qc = q.reshape(B, H, n_chunks, QC, Dh).transpose(2, 0, 1, 3, 4)
    b_ix = jnp.arange(B)[:, None, None, None]
    h_ix = jnp.arange(H)[None, :, None, None]
    blk_ar = jnp.arange(BLK)

    def chunk_fn(args):
        q_c, c = args
        q_start = c * QC
        q_pos = q_start + jnp.arange(QC)
        q_blk = q_start // BLK
        gate = jnp.einsum('bhqd,bhnd->bhqn', q_c, k_mean)
        gate = jnp.where(jnp.arange(nb) < q_blk, gate, -jnp.inf)
        _, idx = lax.top_k(gate, topk)
        valid = idx < q_blk
        k_sel = kb[b_ix, h_ix, idx]
        v_sel = vb[b_ix, h_ix, idx]
        k_pos_sel = idx[..., None] * BLK + blk_ar
        bias_sel = rel_bias[h_ix[..., None], rel_bucket(q_pos[None, None, :, None, None] - k_pos_sel)]
        s_sel = jnp.einsum('bhqd,bhqtkd->bhqtk', q_c, k_sel).astype(f32) + bias_sel.astype(f32)
        s_sel = jnp.where(valid[..., None], s_sel, -jnp.inf)
        k_own = lax.dynamic_index_in_dim(kb, q_blk, axis=2, keepdims=False)
        v_own = lax.dynamic_index_in_dim(vb, q_blk, axis=2, keepdims=False)
        own_pos = q_blk * BLK + blk_ar
        bias_own = rel_bias[:, rel_bucket(q_pos[:, None] - own_pos[None, :])]
        s_own = jnp.einsum('bhqd,bhkd->bhqk', q_c, k_own).astype(f32) + bias_own.astype(f32)[None]
        s_own = jnp.where(own_pos[None, :] <= q_pos[:, None], s_own, -jnp.inf)
        logits = jnp.concatenate([s_sel.reshape(B, H, QC, topk * BLK), s_own], axis=-1)
        probs = jax.nn.softmax(logits, axis=-1).astype(v.dtype)
        p_sel = probs[..., :topk * BLK].reshape(B, H, QC, topk, BLK)
        p_own = probs[..., topk * BLK:]
        return (jnp.einsum('bhqtk,bhqtkd->bhqd', p_sel, v_sel)
                + jnp.einsum('bhqk,bhkd->bhqd', p_own, v_own))

    out = lax.map(chunk_fn, (qc, jnp.arange(n_chunks)))
    return out.transpose(1, 0, 3, 2, 4).reshape(B, S, H * Dh)

def memory_cross_attention(h, mem_n, w_q, w_kv, w_o):
    B, S, D = h.shape
    M = mem_n.shape[1]
    q = (h @ w_q).reshape(B, S, XATTN_HEADS, XATTN_HEAD_DIM)
    k, v = jnp.split(mem_n @ w_kv, 2, axis=-1)
    k = k.reshape(B, M, XATTN_HEADS, XATTN_HEAD_DIM)
    v = v.reshape(B, M, XATTN_HEADS, XATTN_HEAD_DIM)
    logits = jnp.einsum('bshd,bmhd->bhsm', q, k).astype(jnp.float32) * (XATTN_HEAD_DIM ** -0.5)
    probs = jax.nn.softmax(logits, axis=-1).astype(v.dtype)
    o = jnp.einsum('bhsm,bmhd->bshd', probs, v).reshape(B, S, D)
    return o @ w_o

def second_inputs(seed: int = 0) -> dict:
    key = jax.random.key(seed)
    ks = iter(jax.random.split(key, 40))
    f32 = jnp.float32

    def nrm(shape, scale):
        return scale * jax.random.normal(next(ks), shape, f32)

    def dense(fan_in, fan_out):
        return nrm((DEPTH_2, fan_in, fan_out), fan_in ** -0.5)

    def gain(n):
        return 1.0 + nrm((DEPTH_2, n), 0.02)

    W = RWKV_WIDTH
    return {
        "x": nrm((BATCH, SEQ, D_MODEL), 1.0),
        "mem": nrm((BATCH, MEM_LEN, D_MODEL), 1.0),
        "rel_bias": nrm((MOBA_HEADS, REL_BUCKETS), 0.5),
        "final_norm_g": 1.0 + nrm((D_MODEL,), 0.02),
        "ffn1_norm_g": gain(D_MODEL),
        "ffn1_w_in": dense(D_MODEL, 2 * D_FF),
        "ffn1_w_out": dense(D_FF, D_MODEL),
        "mix_norm_g": gain(D_MODEL),
        "w_mix_in": dense(D_MODEL, D_PROJ),
        "w_mix_out": dense(D_MIX, D_MODEL),
        "rwkv_mu": jax.random.uniform(next(ks), (DEPTH_2, RWKV_PROJ), f32),
        "rwkv_w0": jnp.linspace(-6.0, -1.0, W, dtype=f32)[None, :] + nrm((DEPTH_2, W), 0.1),
        "rwkv_w_up": nrm((DEPTH_2, DECAY_LORA, W), 0.5 * DECAY_LORA ** -0.5),
        "rwkv_a0": nrm((DEPTH_2, W), 0.1),
        "rwkv_a_up": dense(ICLR_LORA, W),
        "rwkv_g_up": dense(GATE_LORA, W),
        "rwkv_k_k": 0.85 + nrm((DEPTH_2, W), 0.02),
        "rwkv_k_a": 1.0 + nrm((DEPTH_2, W), 0.02),
        "rwkv_r_k": nrm((DEPTH_2, RWKV_HEADS, HEAD_DIM), 0.1),
        "rwkv_ln_g": gain(W),
        "rwkv_ln_b": nrm((DEPTH_2, W), 0.02),
        "xattn_norm_g": gain(D_MODEL),
        "mem_norm_g": gain(D_MODEL),
        "xattn_w_q": dense(D_MODEL, D_MODEL),
        "xattn_w_kv": dense(D_MODEL, 2 * D_MODEL),
        "xattn_w_o": dense(D_MODEL, D_MODEL),
        "ffn2_norm_g": gain(D_MODEL),
        "ffn2_w_in": dense(D_MODEL, 2 * D_FF),
        "ffn2_w_out": dense(D_FF, D_MODEL),
    }

def second_block(x, mem, rel_bias, final_norm_g, ffn1_norm_g, ffn1_w_in, ffn1_w_out, mix_norm_g,
              w_mix_in, w_mix_out, rwkv_mu, rwkv_w0, rwkv_w_up, rwkv_a0, rwkv_a_up, rwkv_g_up,
              rwkv_k_k, rwkv_k_a, rwkv_r_k, rwkv_ln_g, rwkv_ln_b, xattn_norm_g, mem_norm_g,
              xattn_w_q, xattn_w_kv, xattn_w_o, ffn2_norm_g, ffn2_w_in, ffn2_w_out):
    for l in range(DEPTH_2):
        x = x + FFN_RES_WEIGHT * swiglu_ffn(rms_norm(x, ffn1_norm_g[l]), ffn1_w_in[l], ffn1_w_out[l])
        proj = rms_norm(x, mix_norm_g[l]) @ w_mix_in[l]
        p_rwkv = proj[..., :RWKV_PROJ]
        q_m, k_m, v_m = jnp.split(proj[..., RWKV_PROJ:], 3, axis=-1)
        y_rwkv = rwkv7_time_mix(p_rwkv, rwkv_mu[l], rwkv_w0[l], rwkv_w_up[l], rwkv_a0[l],
                                rwkv_a_up[l], rwkv_g_up[l], rwkv_k_k[l], rwkv_k_a[l], rwkv_r_k[l],
                                rwkv_ln_g[l], rwkv_ln_b[l])
        y_moba = moba_attention(q_m, k_m, v_m, rel_bias)
        x = x + jnp.concatenate([y_rwkv, y_moba], axis=-1) @ w_mix_out[l]
        x = x + memory_cross_attention(rms_norm(x, xattn_norm_g[l]), rms_norm(mem, mem_norm_g[l]),
                                       xattn_w_q[l], xattn_w_kv[l], xattn_w_o[l])
        x = x + FFN_RES_WEIGHT * swiglu_ffn(rms_norm(x, ffn2_norm_g[l]), ffn2_w_in[l], ffn2_w_out[l])
    return rms_norm(x, final_norm_g)


def setup_inputs(seed=0):
    out = dict(first_inputs(seed))
    for name, value in second_inputs(seed + 1).items():
        if name != "x":
            out[name + "_2"] = value
    return out


def reference(
    x, c, w_ada, b_ada, g_norm1, w_in, w_dw, b_dw, g_conv_ln, b_conv_ln, w_conv_pw, b_conv_pw,
    w_a2, b_a2, g_gla_norm, w_gla_o, w_out, g_norm2, w_router_g, b_router_g, w_router_e,
    b_router_e, w1, w3, w2, w_ada_f, b_ada_f, g_final, mem_2, rel_bias_2, final_norm_g_2,
    ffn1_norm_g_2, ffn1_w_in_2, ffn1_w_out_2, mix_norm_g_2, w_mix_in_2, w_mix_out_2, rwkv_mu_2,
    rwkv_w0_2, rwkv_w_up_2, rwkv_a0_2, rwkv_a_up_2, rwkv_g_up_2, rwkv_k_k_2, rwkv_k_a_2,
    rwkv_r_k_2, rwkv_ln_g_2, rwkv_ln_b_2, xattn_norm_g_2, mem_norm_g_2, xattn_w_q_2,
    xattn_w_kv_2, xattn_w_o_2, ffn2_norm_g_2, ffn2_w_in_2, ffn2_w_out_2,
):
    x = first_block(
        x, c, w_ada, b_ada, g_norm1, w_in, w_dw, b_dw, g_conv_ln, b_conv_ln, w_conv_pw,
        b_conv_pw, w_a2, b_a2, g_gla_norm, w_gla_o, w_out, g_norm2, w_router_g, b_router_g,
        w_router_e, b_router_e, w1, w3, w2, w_ada_f, b_ada_f, g_final,
    )
    return second_block(
        x, mem_2, rel_bias_2, final_norm_g_2, ffn1_norm_g_2, ffn1_w_in_2, ffn1_w_out_2,
        mix_norm_g_2, w_mix_in_2, w_mix_out_2, rwkv_mu_2, rwkv_w0_2, rwkv_w_up_2, rwkv_a0_2,
        rwkv_a_up_2, rwkv_g_up_2, rwkv_k_k_2, rwkv_k_a_2, rwkv_r_k_2, rwkv_ln_g_2, rwkv_ln_b_2,
        xattn_norm_g_2, mem_norm_g_2, xattn_w_q_2, xattn_w_kv_2, xattn_w_o_2, ffn2_norm_g_2,
        ffn2_w_in_2, ffn2_w_out_2,
    )


_drawn_inputs = setup_inputs


def setup_inputs(seed=0):
    import zlib

    import numpy as np

    out = dict(_drawn_inputs(seed))
    spreads = {}
    factors = {'g_norm1': 3.083,
     'b_dw': 6.805,
     'g_conv_ln': 5.958,
     'b_conv_ln': 8.0,
     'b_conv_pw': 8.0,
     'b_a2': 8.0,
     'g_gla_norm': 5.902,
     'b_router_g': 8.0,
     'b_router_e': 8.0,
     'final_norm_g_2': 2.861,
     'ffn1_norm_g_2': 4.603,
     'mix_norm_g_2': 3.033,
     'rwkv_a0_2': 3.18,
     'rwkv_k_k_2': 4.798,
     'rwkv_k_a_2': 3.936,
     'rwkv_ln_g_2': 5.639,
     'rwkv_ln_b_2': 6.058,
     'xattn_norm_g_2': 8.0,
     'mem_norm_g_2': 8.0,
     'ffn2_norm_g_2': 5.871}
    for name, (base, spread) in spreads.items():
        noise = np.random.default_rng([zlib.crc32(name.encode()), seed]).standard_normal(out[name].shape)
        drawn = base * np.exp(spread * noise) if base else spread * noise
        out[name] = jnp.asarray(drawn.astype(out[name].dtype))
    for name, factor in factors.items():
        out[name] = (out[name] * factor).astype(out[name].dtype)
    return out
```

```python
import concourse.bass as bass
from concourse import mybir
from contextlib import ExitStack
import numpy as np

F32 = mybir.dt.float32
ALU = mybir.AluOpType
ACT = mybir.ActivationFunctionType
AX = mybir.AxisListType

P = 128
SEQ = 256
D = 1024
KD = D // P
NT = SEQ // P
SLOTS = 4
SLOT = 4096
EPS = 1e-6

CONV_DIM, CONV_WIDTH = 512, 31
GH, GDK, GDV, LOWRANK, TAU = 4, 128, 256, 16, 16.0
NG, EPG, NE, DE = 4, 8, 32, 512
DEPTH_2 = 2
W = 512
HD = 64
NH = 8
RB = 32
XH, XHD = 4, 256
D_FF = 2816
LNX_EPS = 64e-5
NGRP = D_FF // 256
BIG = 1.0e30
VECTOR_STEPS = 87

EYE = 0
LEV = 1
LEVT = 8
UPPER = 15
UPPER_EQ = 16
HEADS = 17
ONES = 18
DESC = 19
LOWER = 20
NCONST = 21


def const_tiles():
    i, j = np.arange(P)[:, None], np.arange(P)[None, :]
    c = np.zeros((P, NCONST, P), np.float32)
    c[:, EYE] = i == j
    for n in range(7):
        s = 1 << n
        lev = (i // (2 * s) == j // (2 * s)) & (i % (2 * s) < s) & (j % (2 * s) >= s)
        c[:, LEV + n] = lev
        c[:, LEVT + n] = lev.T
    c[:, UPPER] = i < j
    c[:, UPPER_EQ] = i <= j
    c[:, HEADS] = i // HD == j // HD
    c[:, ONES] = 1.0
    c[:, DESC] = P - j
    c[:, LOWER] = i > j
    return c


BUCKET_START = list(range(17)) + [21, 27, 35, 46, 59, 77, 99, 128, 166, 216]
NDIST = 3 * P


def bucket_onehot():
    out = np.zeros((RB, NDIST), np.float32)
    for dist in range(SEQ):
        b = max(n for n, start in enumerate(BUCKET_START) if start <= dist)
        out[b, SEQ - 1 - dist] = 1.0
    return out


C1 = {}
_at = 0
for _name, _n in (("c", 8), ("g_norm1", 8), ("sh1", 8), ("sc1", 8), ("sh2", 8), ("sc2", 8), ("b_dw", 4),
                  ("g_conv_ln", 4), ("b_conv_ln", 4), ("b_conv_pw", 8), ("b_a2", 4), ("g_gla_norm", 8),
                  ("g_norm2", 8), ("w_dw", 4 * CONV_WIDTH)):
    C1[_name] = (_at, _at + _n)
    _at += _n
NC1 = _at
C2 = {}
_at = 0
for _name, _n in (("ffn1_g", 8), ("mix_g", 8), ("mu", 14), ("w0", 4), ("a0", 4), ("k_k", 4), ("k_a", 4),
                  ("r_k", 4), ("ln_g", 4), ("ln_b", 4), ("xattn_g", 8), ("mem_g", 8), ("ffn2_g", 8)):
    C2[_name] = (_at, _at + _n)
    _at += _n
NC2 = _at
def column(t, spec, name):
    a, b = spec[name]
    return t[:, a:b]


def piece(j, base=(0,) * SLOTS, turn=0):
    return j % SLOTS, base[j % SLOTS] + j // SLOTS + turn


PIECES1 = ([("ada", n) for n in range(4)] + [("in", n) for n in range(7)] + [("ada", 4), ("in", 7), ("ada", 5)]
           + [("in", 8), ("ada", 6), ("ada", 7), ("in", 9), ("ada", 8), ("ada", 9), ("in", 10), ("ada", 10),
              ("ada", 11), ("in", 11), ("ada", 12), ("ada", 13), ("pw", 0), ("ada", 14), ("ada", 15),
              ("glao", 0), ("glao", 1), ("out", 0), ("out", 1)])
J1 = {key: j for j, key in enumerate(PIECES1)}
J_MOE = len(PIECES1)
N36 = NG + NE
COL_A1 = 2 * CONV_DIM + 2 * GH * GDK + 2 * GH * GDV
COL_GATES = COL_A1 + LOWRANK
PROJ_COLS = [512 * n for n in range(8)] + [COL_GATES + 512 * n for n in range(4)]
U_BLOCK2 = [sum(1 for j in range(J_MOE + 3 * NE) if j % SLOTS == s) for s in range(SLOTS)]


def build(nc, a, out):
    ctx = ExitStack()
    dbg = a.get("debug")
    with ctx:
        def sem(name):
            return ctx.enter_context(nc.semaphore(name))

        def sb(name, shape, where=None):
            return (where or ctx).enter_context(nc.sbuf_tensor(name, [P] + shape, F32))

        bank = [ctx.enter_context(nc.psum_tensor(f"bank{n}", [P, 512], F32)) for n in range(8)]

        x = sb("x", [NT, D])
        xT = sb("xT", [KD, SEQ])
        xs = sb("xs", [NT, D])
        ring = sb("ring", [SLOTS, SLOT])
        K = sb("K", [NCONST, P])
        ones256 = sb("ones256", [SEQ])
        neghalf = sb("neghalf", [8])
        ss = sb("ss", [8])
        ms = sb("ms", [8])
        rstd = sb("rstd", [8])
        eye = K[:, EYE, :]
        ones = K[:, ONES, :]

        w_full = [sem(f"w_full{n}") for n in range(SLOTS)]
        consts_loaded = sem("consts_loaded")
        x_loaded = sem("x_loaded")
        rows_loaded = sem("rows_loaded")
        filled = sem("filled")
        x_ready = sem("x_ready")
        ss_ready = sem("ss_ready")
        ms_ready = sem("ms_ready")
        rstd_ready = sem("rstd_ready")
        xs_act = sem("xs_act")
        xs_dve = sem("xs_dve")
        tr_full = sem("tr_full")
        xT_act = sem("xT_act")
        xT_dve = sem("xT_dve")
        dve_steps = sem("dve_steps")
        act_steps = sem("act_steps")
        out_stored = sem("out_stored")
        sp_passed = sem("sp_passed")
        pool_passed = sem("pool_passed")

        def flat(t):
            return t.rearrange("p a b -> p (a b)")

        def slot_w(s, k, n):
            return ring[:, s, 0:k * n].rearrange("p (k n) -> p k n", k=k)

        class Steps:

            def __init__(self, eng, s):
                self.eng, self.s, self.base, self.n = eng, s, 0, 0

            def __call__(self, ins):
                ins.then_inc(self.s, 1)
                self.n += 1

            def sync(self, back=0):
                self.eng.wait_ge(self.s, self.base + self.n - back)

            def loop(self, count, per, start=0):
                outer = self.base + self.n
                with self.eng.Fori(0, count) as i:
                    self.base, self.n = outer + i * per, 0
                    yield i
                    assert self.n == per, (self.n, per)
                self.base, self.n = outer + count * per, 0

        def norm_sums(act, n, src=None):
            src = x if src is None else src
            for t in range(NT):
                last = nc.scalar.activation(xs[:, t, :], src[:, t, :], ACT.Square, accum_out=ss[:, t:t + 1])
            last.then_inc(ss_ready, 1)
            act.wait_ge(rstd_ready, n + 1)
            nc.scalar.activation(xs[:, 0, :], src[:, 0, :], ACT.Copy, scale=rstd[:, 0:1]).then_inc(xs_act, 1)

        def norm_rstd(pool, n):
            pool.wait_ge(ss_ready, n + 1)
            pool.sem_inc(pool_passed, 1)
            nc.gpsimd.tensor_scalar(ms[:, 0:NT], ss[:, 0:NT], 1.0 / D, EPS, ALU.mult, ALU.add).then_inc(ms_ready, 1)
            pool.wait_ge(ms_ready, n + 1)
            nc.gpsimd.tensor_tensor(rstd[:, 0:NT], ms[:, 0:NT], neghalf[:, 0:NT], ALU.pow).then_inc(rstd_ready, 1)

        def norm_scale(dve, n, src=None):
            src = x if src is None else src
            dve.wait_ge(rstd_ready, n + 1)
            nc.vector.tensor_scalar(xs[:, 1, :], src[:, 1, :], rstd[:, 1:2], None, ALU.mult).then_inc(xs_dve, 1)

        def transposes(pe, q, src):
            for b in range(KD // 2):
                for k in (2 * b, 2 * b + 1):
                    for t in range(NT):
                        last = nc.tensor.transpose(bank[b][:, (k % 2) * SEQ + t * P:(k % 2) * SEQ + (t + 1) * P],
                                                   src[:, t, k * P:(k + 1) * P], eye)
                last.then_inc(tr_full, 1)

        def norm_transposes(pe, n, q):
            pe.wait_ge(xs_act, n + 1)
            pe.wait_ge(xs_dve, n + 1)
            transposes(pe, q, xs)

        def tr_bank(k):
            return bank[k // 2][:, (k % 2) * SEQ:(k % 2 + 1) * SEQ]

        def xT_by_act(act, q, scale, bias=None, dst=None):
            dst = xT if dst is None else dst
            for k in (0, 1, 4, 5):
                act.wait_ge(tr_full, 4 * q + k // 2 + 1)
                if bias is None:
                    last = nc.scalar.activation(dst[:, k, :], tr_bank(k), ACT.Copy, scale=scale[:, k:k + 1])
                else:
                    last = nc.scalar.activation(dst[:, k, :], tr_bank(k), ACT.Identity, scale=scale[:, k:k + 1],
                                                bias=bias[:, k:k + 1])
            last.then_inc(xT_act, 1)

        def xT_by_dve(dve, q, scale, bias=None, dst=None):
            dst = xT if dst is None else dst
            for k in (2, 3, 6, 7):
                dve.wait_ge(tr_full, 4 * q + k // 2 + 1)
                if bias is None:
                    last = nc.vector.tensor_scalar(dst[:, k, :], tr_bank(k), scale[:, k:k + 1], None, ALU.mult)
                else:
                    last = nc.vector.tensor_scalar(dst[:, k, :], tr_bank(k), scale[:, k:k + 1], bias[:, k:k + 1],
                                                   ALU.mult, ALU.add)
            last.then_inc(xT_dve, 1)

        ph1 = ExitStack()
        cols = sb("cols", [NC1], ph1)
        c_act = sb("c_act", [KD], ph1)
        mcol = sb("mcol", [4, KD], ph1)
        acc = sb("acc", [2, 512], ph1)
        rows = sb("rows", [4, D], ph1)
        ga1_row, ga2_row, shf_row, scf_row = (rows[:, n, :] for n in range(4))
        brow = sb("brow", [N36], ph1)
        wr = sb("wr", [KD, N36], ph1)

        mix = ExitStack()
        wa1 = sb("wa1", [KD, LOWRANK], mix)
        wa2 = sb("wa2", [512], mix)
        zpad = sb("zpad", [4, CONV_WIDTH - 1 + SEQ], mix)
        cz = sb("cz", [4, SEQ], mix)
        qT = sb("qT", [GH, SEQ], mix)
        kT = sb("kT", [GH, SEQ], mix)
        cum = sb("cum", [GH, SEQ], mix)
        v = sb("v", [NT, D], mix)
        srT = sb("srT", [KD, SEQ], mix)
        sgT = sb("sgT", [2 * KD, SEQ], mix)
        dec = sb("dec", [GH, SEQ], mix)
        QS = sb("QS", [2, GH, SEQ], mix)
        KS = sb("KS", [2, GH, SEQ], mix)
        AT = sb("AT", [3, GH * P], mix)
        tmp = sb("tmp", [2, 512], mix)
        a1T = tmp[:, 1, 0:SEQ]
        mix.close()

        moe = ExitStack()
        lg = sb("lg", [NT, N36], moe)
        rt = sb("rt", [NT, 128], moe)
        comb = sb("comb", [NT, NE], moe)
        y = sb("y", [NT, D], moe)
        gf_row = sb("gf_row", [D], moe)
        hT = sb("hT", [2, 512], moe)
        sg = sb("sg", [2, 512], moe)
        moe.close()
        ph1.close()

        c_ready = sem("c_ready")
        ada_acc = sem("ada_acc")
        ada_psum = sem("ada_psum")
        ada_taken = sem("ada_taken")
        mod_ready = sem("mod_ready")
        proj_full = sem("proj_full")
        proj_act = sem("proj_act")
        proj_dve = sem("proj_dve")
        conv_ready = sem("conv_ready")
        ln_psum = sem("ln_psum")
        ln_sq = sem("ln_sq")
        ln_var = sem("ln_var")
        ln_rstd = sem("ln_rstd")
        ln_norm = sem("ln_norm")
        zc_ready = sem("zc_ready")
        y_psum = sem("y_psum")
        y_taken = sem("y_taken")
        logit_ready = sem("logit_ready")
        soft_ready = sem("soft_ready")
        dist_ready = sem("dist_ready")
        dec_ready = sem("dec_ready")
        qk_ready = sem("qk_ready")
        att_psum = sem("att_psum")
        att_taken = sem("att_taken")
        off_ready = sem("off_ready")
        o_psum = sem("o_psum")
        o_sq = sem("o_sq")
        o_ms = sem("o_ms")
        o_rstd = sem("o_rstd")
        o_normed = sem("o_normed")
        ogT_ready = sem("ogT_ready")
        merged = sem("merged")
        out_psum = sem("out_psum")
        gf_loaded = sem("gf_loaded")
        router_psum = sem("router_psum")
        gap_ready = sem("gap_ready")
        gap_exp = sem("gap_exp")
        hid_up = sem("hid_up")
        hid_silu = sem("hid_silu")
        hid_h = sem("hid_h")
        hid_down = sem("hid_down")
        moe_taken = sem("moe_taken")

        LEVELS = 8

        G_A, G_GT, G_Q, G_K, G_A1, G_DEC, G_V, G_R, G_GATES, G_N = 0, 2, 4, 6, 8, 9, 11, 15, 19, 27
        NB = 5
        BY_DVE = [0, 1, 6, 7, 9, 10]
        BY_ACT = [g for g in range(G_N) if g not in BY_DVE]

        def taken(pe, g):
            if g in BY_DVE:
                pe.wait_ge(proj_dve, BY_DVE.index(g) + 1)
            else:
                pe.wait_ge(proj_act, BY_ACT.index(g) + 1)
        ph2 = ExitStack()
        lc = sb("lc", [NC2], ph2)
        memT = sb("memT", [KD, SEQ], ph2)
        biasT = sb("biasT", [NH, SEQ], ph2)
        lora = sb("lora", [W], ph2)
        gup = sb("gup", [W], ph2)

        pre = ExitStack()
        mem = sb("mem", [NT, D], pre)
        relT = sb("relT", [NH], pre)
        onehot = sb("onehot", [NDIST], pre)
        bydist = sb("bydist", [NDIST], pre)
        gf2_row = sb("gf2_row", [D], pre)
        pre.close()

        ffn = ExitStack()
        fh = sb("fh", [2, 512], ffn)
        fs = sb("fs", [2, 512], ffn)
        ffn.close()

        mix2 = ExitStack()
        pT = sb("pT", [14, SEQ], mix2)
        lw = sb("lw", [4, SEQ], mix2)
        cw = sb("cw", [4, SEQ], mix2)
        aT = sb("aT", [4, SEQ], mix2)
        kk = sb("kk", [4, SEQ], mix2)
        R2 = sb("R2", [4, P], mix2)
        KK2 = sb("KK2", [4, P], mix2)
        bon = sb("bon", [4, SEQ], mix2)
        gT = sb("gT", [4, SEQ], mix2)
        vt = sb("vt", [NT, W], mix2)
        small = sb("small", [48], mix2)
        moba = ExitStack()
        qm = sb("qm", [4, SEQ], moba)
        km = sb("km", [4, SEQ], moba)
        vm = sb("vm", [NT, W], moba)
        sm = sb("sm", [2, 384], moba)
        pmT = sb("pmT", [2, 384], moba)
        moba.close()
        mats = ExitStack()
        Mrb = sb("Mrb", [3, 512], mats)
        Mrk = sb("Mrk", [3, 512], mats)
        Luk = sb("Luk", [3, 512], mats)
        Noff = sb("Noff", [512], mats)
        Nd = sb("Nd", [2, 512], mats)
        Lt = sb("Lt", [2, 512], mats)
        X = sb("X", [2, 512], mats)
        Y = sb("Y", [2, 512], mats)
        Pm = sb("Pm", [2, 512], mats)
        mats.close()
        mix2.close()
        U = lw[:, :, :].rearrange("p a b -> p (a b)").rearrange("p (c n) -> p c n", c=2)
        E1, E3 = xs[:, 0, :], xs[:, 1, :]

        xat = ExitStack()
        gm = sb("gm", [KD, SEQ], xat)
        qx = sb("qx", [KD, SEQ], xat)
        kx = sb("kx", [KD, SEQ], xat)
        vx = sb("vx", [NT, D], xat)
        sx = sb("sx", [2, 512], xat)
        pxT = sb("pxT", [2, 512], xat)
        xsm = sb("xsm", [16], xat)
        xat.close()
        ph2.close()
        bias_dram = nc.dram_tensor("bias_by_distance", (NH, P, NDIST), F32)

        up_full = [sem(f"up_full{n}") for n in range(SLOTS)]
        mem_loaded = sem("mem_loaded")
        rel_loaded = sem("rel_loaded")
        lc_loaded = sem("lc_loaded")
        bd_psum = sem("bd_psum")
        bd_ready = sem("bd_ready")
        bd_stored = sem("bd_stored")
        bias_loaded = sem("bias_loaded")
        mp_full = sem("mp_full")
        mp_act = sem("mp_act")
        shifted = sem("shifted")
        lo_ready = sem("lo_ready")
        lora_psum = sem("lora_psum")
        lora_act = sem("lora_act")
        kk_sq = sem("kk_sq")
        kk_psum = sem("kk_psum")
        kk_ss = sem("kk_ss")
        kk_rs = sem("kk_rs")
        rk_ready = sem("rk_ready")
        rk_psum = sem("rk_psum")
        dec2_ready = sem("dec2_ready")
        e_ready = sem("e_ready")
        vt_psum = sem("vt_psum")
        vt_ready = sem("vt_ready")
        fac_ready = sem("fac_ready")
        mb_s = sem("mb_s")
        mb_sb = sem("mb_sb")
        mb_max = sem("mb_max")
        mb_e = sem("mb_e")
        mb_p = sem("mb_p")
        mb_t = sem("mb_t")
        mb_tc = sem("mb_tc")
        mb_o = sem("mb_o")
        mb_oc = sem("mb_oc")
        mat_full = sem("mat_full")
        mat_dve = sem("mat_dve")
        mat_act = sem("mat_act")
        inv_init = sem("inv_init")
        inv_p = sem("inv_p")
        inv_pm = sem("inv_pm")
        inv_x = sem("inv_x")
        inv_y = sem("inv_y")
        inv_xs = sem("inv_xs")
        inv_ys = sem("inv_ys")
        u_psum = sem("u_psum")
        u_taken = sem("u_taken")
        yy_psum = sem("yy_psum")
        yy_taken = sem("yy_taken")
        gn_psum = sem("gn_psum")
        gn_xc = sem("gn_xc")
        gn_sq = sem("gn_sq")
        gn_var = sem("gn_var")
        gn_rs = sem("gn_rs")
        gn_norm = sem("gn_norm")
        gn_aff = sem("gn_aff")
        bonus_ready = sem("bonus_ready")
        ycat = sem("ycat")
        mo_psum = sem("mo_psum")
        gm_ready = sem("gm_ready")
        kv_psum = sem("kv_psum")
        kv_act = sem("kv_act")
        xq_psum = sem("xq_psum")
        xq_act = sem("xq_act")
        xa_s = sem("xa_s")
        xa_max = sem("xa_max")
        xa_e = sem("xa_e")
        xa_p = sem("xa_p")
        xa_t = sem("xa_t")
        xa_tc = sem("xa_tc")
        xa_o = sem("xa_o")
        xa_oc = sem("xa_oc")
        xo_psum = sem("xo_psum")
        gf2_loaded = sem("gf2_loaded")

        def wait_piece(eng, j, base=(0,) * SLOTS, turn=0):
            s, u = piece(j, base, turn)
            eng.wait_ge(w_full[s], (u + 1) * 16)
            return s

        def grouped(g):
            n = {**{g: (g // 2, g % 2) for g in range(8)}, **{11: (4, 0), 12: (4, 1), 13: (5, 0), 14: (5, 1)},
                 **{15 + i: (6 + i // 2, i % 2) for i in range(12)}}[g]
            return n

        def level_views(t, s):
            return t.rearrange("p h (b s) -> p (h b) s", s=2 * s)

        def sync1(sp):
            def load(j, src, k, n, base=(0,) * SLOTS, turn=0):
                s, u = piece(j, base, turn)
                sp.dma_start(slot_w(s, k, n), src).then_inc(w_full[s], 16)

            def read(key):
                kind, n = key
                if kind == "ada":
                    sp.wait_ge(ada_acc, n + 1)
                elif kind == "in":
                    sp.wait_ge(proj_full, {4: 13, 5: 15}.get(n, 2 * n + 2 if n < 4 else G_R + 2 * (n - 6) + 2))
                elif kind == "pw":
                    sp.wait_ge(y_psum, 4)
                elif kind == "glao":
                    sp.wait_ge(y_psum, 4 + 2 * (n + 1))
                else:
                    sp.wait_ge(out_psum, 2 * (n + 1))

            sp.dma_start(x[:, :, :], a["x"][0].rearrange("(t p) d -> p t d", p=P)).then_inc(x_loaded, 16)
            sp.dma_start(cols[:, :], a["cols1"]).then_inc(consts_loaded, 16)
            sp.dma_start(K[:, :, :], a["const_tiles"]).then_inc(consts_loaded, 16)
            srcs = {}
            for n in range(12):
                srcs["ada", n] = a["w_ada"][0][:, n * 512:(n + 1) * 512]
                srcs["in", n] = a["w_in"][0][:, PROJ_COLS[n]:PROJ_COLS[n] + 512]
            for n in range(4):
                srcs["ada", 12 + n] = a["w_ada_f"][:, n * 512:(n + 1) * 512]
            for n in range(2):
                srcs["glao", n] = a["w_gla_o"][0][:, n * 512:(n + 1) * 512]
                srcs["out", n] = a["w_out"][0][:, n * 512:(n + 1) * 512]
            for j, key in enumerate(PIECES1):
                if j >= SLOTS:
                    read(PIECES1[j - SLOTS])
                if key[0] == "pw":
                    load(j, a["w_conv_pw"][0].rearrange("(k p) n -> p k n", p=P), CONV_DIM // P, D)
                else:
                    load(j, srcs[key].rearrange("(k p) n -> p k n", p=P), KD, 512)
                if j == 3:
                    sp.dma_start(wa1[:, :, :], a["w_in"][0][:, COL_A1:COL_A1 + LOWRANK].rearrange(
                        "(k p) n -> p k n", p=P)).then_inc(rows_loaded, 16)
                    sp.dma_start(wa2[0:LOWRANK, :], a["w_a2"][0]).then_inc(rows_loaded, 16)
                    sp.dma_start(wr[:, :, 0:NG], a["w_router_g"][0].rearrange(
                        "(k p) n -> p k n", p=P)).then_inc(rows_loaded, 16)
                    sp.dma_start(wr[:, :, NG:N36], a["w_router_e"][0].rearrange(
                        "(k p) n -> p k n", p=P)).then_inc(rows_loaded, 16)
                    sp.dma_start(brow[:, 0:NG], a["b_router_g"][0].partition_broadcast(P)).then_inc(rows_loaded, 16)
                    sp.dma_start(brow[:, NG:N36], a["b_router_e"][0].partition_broadcast(P)).then_inc(rows_loaded, 16)
                    sp.dma_start(ga1_row, a["b_ada"][0][2 * D:3 * D].partition_broadcast(P)).then_inc(rows_loaded, 16)
                    sp.dma_start(ga2_row, a["b_ada"][0][5 * D:6 * D].partition_broadcast(P)).then_inc(rows_loaded, 16)
                    sp.dma_start(rows[:, 2:4, :], a["b_ada_f"].rearrange("(r d) -> r d", r=2).partition_broadcast(P)
                                 ).then_inc(rows_loaded, 16)
            for key in PIECES1[-SLOTS:]:
                read(key)
            def expert_piece(i, p):
                e, (src, k, n) = p // 3, (("w1", KD, DE), ("w3", KD, DE), ("w2", DE // P, D))[p % 3]
                load(J_MOE + p, a[src][0, i * 4 + e].rearrange("(k p) n -> p k n", p=P), k, n, turn=i * 3)

            def expert_read(i, p):
                sp.wait_ge(hid_down if p % 3 == 2 else hid_up, i * 8 + 2 * (p // 3) + 2)

            for p in range(SLOTS):
                expert_piece(0, p)
            with sp.Fori(0, NE // 4 - 1) as i:
                for p in range(SLOTS, 12 + SLOTS):
                    expert_read(i, p - SLOTS)
                    expert_piece(i + p // 12, p % 12)
            for p in range(SLOTS, 12):
                expert_read(NE // 4 - 1, p - SLOTS)
                expert_piece(NE // 4 - 1, p)
        ROWS = 16 * 9

        def pool1(pool):
            nc.gpsimd.memset(ones256[:, :], 1.0).then_inc(filled, 1)
            nc.gpsimd.memset(neghalf[:, :], -0.5).then_inc(filled, 1)
            nc.gpsimd.memset(zpad[:, :, 0:CONV_WIDTH - 1], 0.0).then_inc(filled, 1)
            for t in (QS, KS):
                nc.gpsimd.memset(t[:, :, :, :], 0.0).then_inc(filled, 1)
            pool.wait_ge(filled, 5)
            norm_rstd(pool, 0)
            pool.wait_ge(o_sq, 1)
            nc.gpsimd.tensor_scalar(ms[:, :], ss[:, :], 1.0 / GDV, EPS, ALU.mult, ALU.add).then_inc(o_ms, 1)
            pool.wait_ge(o_ms, 1)
            nc.gpsimd.tensor_tensor(rstd[:, :], ms[:, :], neghalf[:, 0:8], ALU.pow).then_inc(o_rstd, 1)
            norm_rstd(pool, 1)
            norm_rstd(pool, 2)

        def tensor1(pe):
            pe.wait_ge(consts_loaded, 32)

            def ada_mm(i):
                pe.wait_ge(ada_acc, i + 1)
                if i:
                    pe.wait_ge(ada_taken, i)
                if i < 4 or 6 <= i < 10:
                    for c in range(4):
                        last = nc.tensor.matmul(bank[5][:, c:c + 1], acc[:, i % 2, c * P:(c + 1) * P], ones[:, 0:1],
                                                start=True, stop=True)
                else:
                    last = nc.tensor.matmul(bank[5][:, :], ones, acc[:, i % 2, :], start=True, stop=True)
                last.then_inc(ada_psum, 1)

            norm_transposes(pe, 0, 0)
            for i in range(4):
                ada_mm(i)
            pe.wait_ge(xT_act, 1)
            pe.wait_ge(xT_dve, 1)

            def project(g):
                if g >= NB:
                    taken(pe, g - NB)
                b = bank[g % NB]
                if g == G_A1:
                    pe.wait_ge(rows_loaded, ROWS)
                    for k in range(KD):
                        last = nc.tensor.matmul(b[0:LOWRANK, 0:SEQ], wa1[:, k, :], xT[:, k, :],
                                                start=(k == 0), stop=(k == KD - 1))
                elif g in (G_DEC, G_DEC + 1):
                    pe.wait_ge(proj_act, BY_ACT.index(G_A1) + 1)
                    for c in range(2):
                        h = 2 * (g - G_DEC) + c
                        last = nc.tensor.matmul(b[:, c * SEQ:(c + 1) * SEQ], wa2[0:LOWRANK, h * P:(h + 1) * P],
                                                a1T[0:LOWRANK, :], start=True, stop=True)
                else:
                    n, half = grouped(g)
                    j = J1["in", n]
                    s = wait_piece(pe, j)
                    w = slot_w(s, KD, 512)
                    if G_V <= g < G_R:
                        for k in range(KD):
                            last = nc.tensor.matmul(b[:, :], xT[:, k, half * P:(half + 1) * P], w[:, k, :],
                                                    start=(k == 0), stop=(k == KD - 1))
                    else:
                        for c in range(2):
                            m = 2 * half + c
                            for k in range(KD):
                                last = nc.tensor.matmul(b[:, c * SEQ:(c + 1) * SEQ], w[:, k, m * P:(m + 1) * P],
                                                        xT[:, k, :], start=(k == 0), stop=(k == KD - 1))
                last.then_inc(proj_full, 1)

            def level(l):
                if l:
                    pe.wait_ge(qk_ready, l)
                    pe.wait_ge(att_taken, l)
                else:
                    pe.wait_ge(proj_dve, 4)
                    pe.wait_ge(ln_var, 1)
                q, k = (qT, kT) if l == 0 else (QS[:, l % 2], KS[:, l % 2])
                if l < LEVELS:
                    for ch in range(2):
                        for h in range(GH):
                            last = nc.tensor.matmul(bank[6 + ch][:, h * P:(h + 1) * P], k[:, h, ch * P:(ch + 1) * P],
                                                    q[:, h, ch * P:(ch + 1) * P], start=True, stop=True)
                else:
                    for h in range(GH):
                        last = nc.tensor.matmul(bank[6][:, h * P:(h + 1) * P], k[:, h, 0:P], q[:, h, P:SEQ],
                                                start=True, stop=True)
                last.then_inc(att_psum, 1)

            after = {15: [("ln", 0)], 16: [("ln", 1)], 18: [("ada", 4)], 19: [("level", 0)],
                     **{19 + l: [("ada", 4 + l), ("level", l)] for l in range(1, 8)}}
            after[26] += [("ada", 12), ("level", 8), ("ada", 13)]
            for g in range(G_N):
                project(g)
                for kind, n in after.get(g, ()):
                    if kind == "ada":
                        ada_mm(n)
                    elif kind == "level":
                        level(n)
                    else:
                        if n == 0:
                            pe.wait_ge(conv_ready, 1)
                        else:
                            pe.wait_ge(ln_sq, 1)
                        src = cz if n == 0 else dec
                        for k in range(4):
                            last = nc.tensor.matmul(bank[6 + n][:, 0:SEQ], ones, src[:, k, :],
                                                    start=(k == 0), stop=(k == 3))
                        last.then_inc(ln_psum, 1)

            s = wait_piece(pe, J1["pw", 0])
            w = slot_w(s, 4, D)
            pe.wait_ge(zc_ready, 1)
            pe.wait_ge(proj_act, len(BY_ACT))
            for g in range(4):
                for c in range(2):
                    m = 2 * g + c
                    for k in range(4):
                        last = nc.tensor.matmul(bank[g][:, c * SEQ:(c + 1) * SEQ], w[:, k, m * P:(m + 1) * P],
                                                cz[:, k, :], start=(k == 0), stop=(k == 3))
                last.then_inc(y_psum, 1)
            pe.wait_ge(att_taken, LEVELS + 1)
            pe.wait_ge(ada_taken, 14)
            for g in range(4):
                t, hp = g // 2, g % 2
                for c in range(2):
                    h = 2 * hp + c
                    o = bank[4 + g][:, c * GDV:(c + 1) * GDV]
                    vs = slice(h * GDV, (h + 1) * GDV)
                    hs = slice(h * P, (h + 1) * P)
                    if t == 0:
                        last = nc.tensor.matmul(o, AT[:, 0, hs], v[:, 0, vs], start=True, stop=True)
                    else:
                        nc.tensor.matmul(o, AT[:, 2, hs], v[:, 0, vs], start=True, stop=False)
                        last = nc.tensor.matmul(o, AT[:, 1, hs], v[:, 1, vs], start=False, stop=True)
                last.then_inc(o_psum, 1)
            pe.wait_ge(o_normed, 2)
            pe.wait_ge(y_taken, 4)
            transposes(pe, 1, xs)
            for i in (14, 15):
                ada_mm(i)
            pe.wait_ge(ada_taken, 16)
            pe.wait_ge(ogT_ready, 1)
            for g in range(4):
                s = wait_piece(pe, J1["glao", g // 2])
                w = slot_w(s, KD, 512)
                for c in range(2):
                    m = 2 * (g % 2) + c
                    for k in range(KD):
                        last = nc.tensor.matmul(bank[4 + g][:, c * SEQ:(c + 1) * SEQ], w[:, k, m * P:(m + 1) * P],
                                                xT[:, k, :], start=(k == 0), stop=(k == KD - 1))
                last.then_inc(y_psum, 1)
            pe.wait_ge(merged, 1)
            for half in range(2):
                s = wait_piece(pe, J1["out", half])
                w = slot_w(s, KD, 512)
                for t in range(NT):
                    for k in range(KD):
                        last = nc.tensor.matmul(bank[2 * half + t][:, :], sgT[:, k, t * P:(t + 1) * P], w[:, k, :],
                                                start=(k == 0), stop=(k == KD - 1))
                    last.then_inc(out_psum, 1)

        def scalar1(act):
            st = Steps(act, act_steps)
            act.wait_ge(x_loaded, 16)
            norm_sums(act, 0)
            act.wait_ge(consts_loaded, 32)
            nc.scalar.activation(c_act[:, :], column(cols, C1, "c"), ACT.Silu).then_inc(c_ready, 1)
            act.wait_ge(mod_ready, 1)
            xT_by_act(act, 0, mcol[:, 1, :], mcol[:, 0, :])

            def full(g):
                act.wait_ge(proj_full, g + 1)
                return bank[g % NB]

            for p in range(2):
                b = full(G_GT + p)
                nc.scalar.activation(flat(cz[:, 2 * p:2 * p + 2, :]), b[:, :], ACT.Sigmoid).then_inc(proj_act, 1)
            for p in range(2):
                b = full(G_Q + p)
                nc.scalar.activation(flat(qT[:, 2 * p:2 * p + 2, :]), b[:, :], ACT.Copy,
                                     scale=GDK ** -0.5).then_inc(proj_act, 1)
            b = full(G_A1)
            nc.scalar.activation(a1T[0:LOWRANK, :], b[0:LOWRANK, 0:SEQ], ACT.Copy).then_inc(proj_act, 1)
            act.wait_ge(proj_dve, 6)
            act.wait_ge(filled, 5)
            z, t = flat(dec[:, :, :]), flat(QS[:, 0, :, :])
            st(nc.scalar.activation(t, z, ACT.Abs))
            st.sync()
            st(nc.scalar.activation(t, t, ACT.Exp, scale=-1.0))
            st.sync()
            nc.scalar.activation(t, t, ACT.Ln, bias=1.0).then_inc(soft_ready, 1)
            for g in range(G_V, G_R):
                b = full(g)
                half = (g - G_V) // 2
                nc.scalar.activation(v[:, (g - G_V) % 2, half * 512:(half + 1) * 512], b[:, :],
                                     ACT.Copy).then_inc(proj_act, 1)
            for g in range(G_R, G_GATES):
                b = full(g)
                m = 2 * (g - G_R)
                nc.scalar.activation(flat(srT[:, m:m + 2, :]), b[:, :], ACT.Silu).then_inc(proj_act, 1)
                if g == G_R + 1:
                    act.wait_ge(ln_var, 1)
                    nc.scalar.activation(tmp[:, 1, 0:SEQ], tmp[:, 0, 0:SEQ], ACT.Sqrt).then_inc(ln_rstd, 1)
                if g == G_R + 2:
                    act.wait_ge(ln_norm, 1)
                    for k in range(4):
                        last = nc.scalar.activation(cz[:, k, :], cz[:, k, :], ACT.Silu,
                                                    scale=column(cols, C1, "g_conv_ln")[:, k:k + 1],
                                                    bias=column(cols, C1, "b_conv_ln")[:, k:k + 1])
                    last.then_inc(zc_ready, 1)
            for g in range(G_GATES, G_N):
                b = full(g)
                m = 2 * (g - G_GATES)
                nc.scalar.activation(flat(sgT[:, m:m + 2, :]), b[:, :], ACT.Sigmoid).then_inc(proj_act, 1)
                l = g - G_GATES + 1
                act.wait_ge(dist_ready, l)
                nc.scalar.activation(flat(dec[:, :, :]), flat(dec[:, :, :]), ACT.Exp,
                                     scale=1.0 / TAU).then_inc(dec_ready, 1)
            for g in range(4):
                act.wait_ge(o_psum, g + 1)
                for c in range(2):
                    last = nc.scalar.activation(xs[:, g // 2, (2 * (g % 2) + c) * GDV:(2 * (g % 2) + c + 1) * GDV],
                                                bank[4 + g][:, c * GDV:(c + 1) * GDV], ACT.Square,
                                                accum_out=ss[:, 2 * g + c:2 * g + c + 1])
            last.then_inc(o_sq, 1)
            act.wait_ge(o_rstd, 1)
            for h in range(GH):
                last = nc.scalar.activation(xs[:, 0, h * GDV:(h + 1) * GDV],
                                            bank[4 + h // 2][:, (h % 2) * GDV:(h % 2 + 1) * GDV], ACT.Copy,
                                            scale=rstd[:, h:h + 1])
            last.then_inc(o_normed, 1)
            act.wait_ge(x_ready, 1)
            norm_sums(act, 1)
            act.wait_ge(mod_ready, 2)
            xT_by_act(act, 2, mcol[:, 3, :], mcol[:, 2, :])
            return st

        def vector1(dve):
            st = Steps(dve, dve_steps)

            def ada_sum(i):
                s = wait_piece(dve, J1["ada", i])
                w = slot_w(s, KD, 512)
                if i >= 2:
                    dve.wait_ge(ada_psum, i - 1)
                st(nc.vector.tensor_scalar(acc[:, i % 2, :], w[:, 0, :], c_act[:, 0:1], None, ALU.mult))
                for k in range(1, KD):
                    st.sync()
                    ins = nc.vector.scalar_tensor_tensor(out=acc[:, i % 2, :], in0=w[:, k, :],
                                                         scalar=c_act[:, k:k + 1], in1=acc[:, i % 2, :],
                                                         op0=ALU.mult, op1=ALU.add)
                    if k < KD - 1:
                        st(ins)
                    else:
                        ins.then_inc(ada_acc, 1)
                dve.wait_ge(ada_acc, i + 1)

            def ada_take(i):
                dve.wait_ge(ada_psum, i + 1)
                if i < 4 or 6 <= i < 10:
                    n = i if i < 4 else i - 2
                    nc.vector.tensor_copy(mcol[:, n // 2, (n % 2) * 4:(n % 2) * 4 + 4],
                                          bank[5][:, 0:4]).then_inc(ada_taken, 1)
                else:
                    n = {4: 0, 5: 1, 10: 2, 11: 3}.get(i, i - 8)
                    r = rows[:, n // 2, (n % 2) * 512:(n % 2 + 1) * 512]
                    dve.wait_ge(rows_loaded, ROWS)
                    nc.vector.tensor_tensor(r, bank[5][:, :], r, ALU.add).then_inc(ada_taken, 1)

            def modulation(n, shift, scale, gain):
                i = 2 * n
                st(nc.vector.tensor_tensor(mcol[:, i, :], mcol[:, i, :], column(cols, C1, shift), ALU.add))
                st(nc.vector.scalar_tensor_tensor(out=mcol[:, i + 1, :], in0=mcol[:, i + 1, :], scalar=1.0,
                                                  in1=column(cols, C1, scale), op0=ALU.add, op1=ALU.add))
                st.sync()
                nc.vector.tensor_tensor(mcol[:, i + 1, :], mcol[:, i + 1, :], column(cols, C1, gain),
                                        ALU.mult).then_inc(mod_ready, 1)
                dve.wait_ge(mod_ready, n + 1)

            dve.wait_ge(x_loaded, 16)
            norm_scale(dve, 0)
            dve.wait_ge(consts_loaded, 32)
            dve.wait_ge(c_ready, 1)
            for i in range(4):
                ada_sum(i)
                if i:
                    ada_take(i - 1)
            ada_take(3)
            dve.wait_ge(ada_taken, 4)
            modulation(0, "sh1", "sc1", "g_norm1")
            xT_by_dve(dve, 0, mcol[:, 1, :], mcol[:, 0, :])
            dve.wait_ge(filled, 5)
            for p in range(2):
                dve.wait_ge(proj_full, G_A + p + 1)
                dve.wait_ge(proj_act, p + 1)
                nc.vector.tensor_tensor(zpad[:, 2 * p:2 * p + 2, CONV_WIDTH - 1:],
                                        bank[(G_A + p) % NB][:, :].rearrange("p (c t) -> p c t", c=2),
                                        cz[:, 2 * p:2 * p + 2, :], ALU.mult).then_inc(proj_dve, 1)
            for p in range(2):
                dve.wait_ge(proj_full, G_K + p + 1)
                nc.vector.tensor_copy(flat(kT[:, 2 * p:2 * p + 2, :]), bank[(G_K + p) % NB][:, :]).then_inc(proj_dve, 1)
            for p in range(2):
                dve.wait_ge(proj_full, G_DEC + p + 1)
                for c in range(2):
                    h = 2 * p + c
                    last = nc.vector.tensor_scalar(dec[:, h, :], bank[(G_DEC + p) % NB][:, c * SEQ:(c + 1) * SEQ],
                                                   column(cols, C1, "b_a2")[:, h:h + 1], None, ALU.add)
                last.then_inc(proj_dve, 1)
            dve.wait_ge(proj_dve, 6)
            dve.wait_ge(soft_ready, 1)
            st(nc.vector.scalar_tensor_tensor(out=flat(dec[:, :, :]), in0=flat(dec[:, :, :]), scalar=0.0,
                                              in1=flat(QS[:, 0, :, :]), op0=ALU.min, op1=ALU.subtract))
            st.sync()
            for h in range(GH):
                st(nc.vector.tensor_tensor_scan(cum[:, h, :], ones256[:, :], dec[:, h, :], 0.0, ALU.mult, ALU.add))
            wd = column(cols, C1, "w_dw").rearrange("p (k n) -> p k n", k=4)
            for tap in range(CONV_WIDTH):
                for k in range(4):
                    src = zpad[:, k, tap:tap + SEQ]
                    if tap == 0:
                        st(nc.vector.tensor_scalar(cz[:, k, :], src, wd[:, k, 0:1],
                                                   column(cols, C1, "b_dw")[:, k:k + 1], ALU.mult, ALU.add))
                    else:
                        st.sync(back=3)
                        ins = nc.vector.scalar_tensor_tensor(out=cz[:, k, :], in0=src, scalar=wd[:, k, tap:tap + 1],
                                                             in1=cz[:, k, :], op0=ALU.mult, op1=ALU.add)
                        if tap == CONV_WIDTH - 1 and k == 3:
                            ins.then_inc(conv_ready, 1)
                        else:
                            st(ins)
            dve.wait_ge(ln_psum, 1)
            for k in range(4):
                st(nc.vector.scalar_tensor_tensor(out=cz[:, k, :], in0=bank[6][:, 0:SEQ], scalar=-1.0 / CONV_DIM,
                                                  in1=cz[:, k, :], op0=ALU.mult, op1=ALU.add))
            st.sync()
            nc.vector.tensor_tensor(dec[:, :, :], cz[:, :, :], cz[:, :, :], ALU.mult).then_inc(ln_sq, 1)
            dve.wait_ge(ln_psum, 2)
            nc.vector.tensor_scalar(tmp[:, 0, 0:SEQ], bank[7][:, 0:SEQ], 1.0 / CONV_DIM, EPS,
                                    ALU.mult, ALU.add).then_inc(ln_var, 1)
            dve.wait_ge(ln_rstd, 1)
            st(nc.vector.reciprocal(tmp[:, 1, 0:SEQ], tmp[:, 1, 0:SEQ]))
            st.sync()
            for k in range(4):
                last = nc.vector.tensor_tensor(cz[:, k, :], cz[:, k, :], tmp[:, 1, 0:SEQ], ALU.mult)
            last.then_inc(ln_norm, 1)
            dve.wait_ge(ln_norm, 1)

            def distances(l):
                s = 1 << (l - 1)
                c, d = level_views(cum[:, :, :], s), level_views(dec[:, :, :], s)
                nb = GH * SEQ // (2 * s)
                ref = c[:, :, s - 1:s].to_broadcast([P, nb, s])
                st(nc.vector.tensor_tensor(d[:, :, s:2 * s], c[:, :, s:2 * s], ref, ALU.subtract))
                nc.vector.tensor_tensor(d[:, :, 0:s], ref, c[:, :, 0:s], ALU.subtract).then_inc(dist_ready, 1)

            def scaled(l):
                s = 1 << (l - 1)
                d = level_views(dec[:, :, :], s)
                dve.wait_ge(dec_ready, l)
                if l >= 3:
                    dve.wait_ge(att_psum, l - 1)
                q, k = level_views(QS[:, l % 2], s), level_views(KS[:, l % 2], s)
                st(nc.vector.tensor_tensor(q[:, :, s:2 * s], level_views(qT[:, :, :], s)[:, :, s:2 * s],
                                           d[:, :, s:2 * s], ALU.mult))
                st.sync()
                nc.vector.tensor_tensor(k[:, :, 0:s], level_views(kT[:, :, :], s)[:, :, 0:s],
                                        d[:, :, 0:s], ALU.mult).then_inc(qk_ready, 1)
                dve.wait_ge(qk_ready, l)

            def accumulate(l):
                dve.wait_ge(att_psum, l + 1)
                if l == LEVELS:
                    nc.vector.tensor_copy(AT[:, 2, :], bank[6][:, :]).then_inc(att_taken, 1)
                    return
                mask = K[:, EYE if l == 0 else LEV + l - 1, :].unsqueeze(1).to_broadcast([P, GH, P])
                if l:
                    dve.wait_ge(att_taken, l)
                for ch in range(2):
                    ps = bank[6 + ch][:, :].rearrange("p (h t) -> p h t", h=GH)
                    dst = AT[:, ch, :] if l == 0 else tmp[:, ch, :]
                    ins = nc.vector.tensor_tensor(dst.rearrange("p (h t) -> p h t", h=GH), ps, mask, ALU.mult)
                    st(ins) if l or ch == 0 else ins.then_inc(att_taken, 1)
                if l:
                    st.sync()
                    st(nc.vector.tensor_tensor(AT[:, 0, :], AT[:, 0, :], tmp[:, 0, :], ALU.add))
                    nc.vector.tensor_tensor(AT[:, 1, :], AT[:, 1, :], tmp[:, 1, :], ALU.add).then_inc(att_taken, 1)

            ada_at = {1: [4], 2: [5], 3: [6], 4: [7], 5: [8], 6: [9], 7: [10], 8: [11]}
            for l in range(1, LEVELS + 1):
                distances(l)
                for i in ada_at[l]:
                    ada_sum(i)
                    if i > 4:
                        ada_take(i - 1)
                scaled(l)
                accumulate(l - 1)
            for i in (12, 13):
                ada_sum(i)
                ada_take(i - 1)
            accumulate(LEVELS)
            ada_take(13)

            def merge(g, bias):
                m = 2 * (g % 4)
                ps = bank[g][:, :]
                dve.wait_ge(y_psum, g + 1)
                if g < 4:
                    for c in range(2):
                        last = nc.vector.scalar_tensor_tensor(
                            out=sgT[:, m + c, :], in0=ps[:, c * SEQ:(c + 1) * SEQ], scalar=bias[:, m + c:m + c + 1],
                            in1=sgT[:, m + c, :], op0=ALU.add, op1=ALU.mult)
                    last.then_inc(y_taken, 1)
                else:
                    t = tmp[:, g % 2, :]
                    st(nc.vector.tensor_tensor(t, ps, flat(sgT[:, KD + m:KD + m + 2, :]), ALU.mult))
                    st.sync()
                    dst = flat(sgT[:, m:m + 2, :])
                    ins = nc.vector.tensor_tensor(dst, dst, t, ALU.add)
                    st(ins) if g < 7 else ins.then_inc(merged, 1)

            for g in range(4):
                merge(g, column(cols, C1, "b_conv_pw"))
            dve.wait_ge(y_taken, 4)
            dve.wait_ge(o_rstd, 1)
            for h in range(GH):
                last = nc.vector.tensor_scalar(xs[:, 1, h * GDV:(h + 1) * GDV],
                                               bank[6 + h // 2][:, (h % 2) * GDV:(h % 2 + 1) * GDV],
                                               rstd[:, 4 + h:5 + h], None, ALU.mult)
            last.then_inc(o_normed, 1)
            for k in range(KD):
                dve.wait_ge(tr_full, 4 + k // 2 + 1)
                last = nc.vector.scalar_tensor_tensor(out=xT[:, k, :], in0=tr_bank(k),
                                                      scalar=column(cols, C1, "g_gla_norm")[:, k:k + 1],
                                                      in1=srT[:, k, :], op0=ALU.mult, op1=ALU.mult)
            last.then_inc(ogT_ready, 1)
            for i in (14, 15):
                ada_sum(i)
                ada_take(i)
            for g in range(4, 8):
                merge(g, None)
            for g in range(4):
                half, t = g // 2, g % 2
                cs = slice(half * 512, (half + 1) * 512)
                dve.wait_ge(out_psum, g + 1)
                st(nc.vector.tensor_tensor(tmp[:, g % 2, :], bank[g][:, :], ga1_row[:, cs], ALU.mult))
                st.sync()
                ins = nc.vector.tensor_tensor(x[:, t, cs], x[:, t, cs], tmp[:, g % 2, :], ALU.add)
                st(ins) if g < 3 else ins.then_inc(x_ready, 1)
            norm_scale(dve, 1)
            dve.wait_ge(ada_taken, 16)
            modulation(1, "sh2", "sc2", "g_norm2")
            xT_by_dve(dve, 2, mcol[:, 3, :], mcol[:, 2, :])
            return st

        def tensor_moe(pe):
            norm_transposes(pe, 1, 2)
            pe.wait_ge(xT_act, 2)
            pe.wait_ge(xT_dve, 2)
            for t in range(NT):
                for k in range(KD):
                    last = nc.tensor.matmul(bank[4][:, t * 64:t * 64 + N36], xT[:, k, t * P:(t + 1) * P], wr[:, k, :],
                                            start=(k == 0), stop=(k == KD - 1))
            last.then_inc(router_psum, 1)
            with pe.Fori(0, NE // 4) as i:
                def up(g):
                    e, hh = g // 2, g % 2
                    for m in range(2):
                        s = wait_piece(pe, J_MOE + 3 * e + m, turn=i * 3)
                        w = slot_w(s, KD, DE)
                        for c in range(2):
                            f = (2 * hh + c) * P
                            for k in range(KD):
                                last = nc.tensor.matmul(bank[2 * (g % 2) + m][:, c * SEQ:(c + 1) * SEQ],
                                                        w[:, k, f:f + P], xT[:, k, :],
                                                        start=(k == 0), stop=(k == KD - 1))
                    last.then_inc(hid_up, 1)

                def down(g):
                    e, hh = g // 2, g % 2
                    pe.wait_ge(hid_h, i * 8 + g + 1)
                    s = wait_piece(pe, J_MOE + 3 * e + 2, turn=i * 3)
                    w = slot_w(s, DE // P, D)
                    if hh == 0:
                        pe.wait_ge(moe_taken, i * 4 + e + 1)
                    for t in range(NT):
                        for half in range(2):
                            for c in range(2):
                                last = nc.tensor.matmul(bank[4 + 2 * t + half][:, :],
                                                        hT[:, g % 2, c * SEQ + t * P:c * SEQ + (t + 1) * P],
                                                        w[:, 2 * hh + c, half * 512:(half + 1) * 512],
                                                        start=(hh == 0 and c == 0), stop=(hh == 1 and c == 1))
                    last.then_inc(hid_down, 1)

                up(0)
                for g in range(1, 8):
                    up(g)
                    down(g - 1)
                down(7)

        def scalar_moe(act):
            act.wait_ge(x_ready, 1)
            act.dma_start(gf_row[:, :], a["g_final"].partition_broadcast(P)).then_inc(gf_loaded, 16)
            for n in range(2):
                act.wait_ge(gap_ready, n + 1)
                t = rt[:, :, 4:8] if n == 0 else rt[:, :, 64:65]
                nc.scalar.activation(t, t, ACT.Exp).then_inc(gap_exp, 1)
            with act.Fori(0, NE // 4) as i:
                for g in range(8):
                    act.wait_ge(hid_up, i * 8 + g + 1)
                    nc.scalar.activation(sg[:, g % 2, :], bank[2 * (g % 2)][:, :], ACT.Silu).then_inc(hid_silu, 1)
            act.wait_ge(x_ready, 2)
            norm_sums(act, 2)

        def vector_moe(dve, st):
            dve.wait_ge(x_ready, 1)
            dve.wait_ge(router_psum, 1)
            for t in range(NT):
                st(nc.vector.tensor_tensor(lg[:, t, :], bank[4][:, t * 64:t * 64 + N36], brow[:, :], ALU.add))
            nc.vector.memset(y[:, :, :], 0.0).then_inc(moe_taken, 1)
            st.sync()

            def first_max(values, width, top, hot, weight):
                st(nc.vector.tensor_reduce(top, values, AX.X, ALU.max))
                st.sync()
                st(nc.vector.tensor_tensor(hot, values, top.to_broadcast([P, NT, width]), ALU.is_equal))
                st.sync()
                st(nc.vector.tensor_tensor(hot, hot, K[:, DESC, 0:width].unsqueeze(1).to_broadcast([P, NT, width]),
                                           ALU.mult))
                st.sync()
                st(nc.vector.tensor_reduce(weight, hot, AX.X, ALU.max))
                st.sync()
                st(nc.vector.tensor_tensor(hot, hot, weight.to_broadcast([P, NT, width]), ALU.is_equal))
                st.sync()

            gtop, gsum, wt = rt[:, :, 0:1], rt[:, :, 1:2], rt[:, :, 2:3]
            gexp, ghot = rt[:, :, 4:8], rt[:, :, 8:12]
            sel, hot1, hot2, rest = rt[:, :, 16:24], rt[:, :, 24:32], rt[:, :, 32:40], rt[:, :, 40:48]
            top1, top2, gap, tot = rt[:, :, 48:49], rt[:, :, 49:50], rt[:, :, 64:65], rt[:, :, 65:66]
            prod = rt[:, :, 96:128]
            lgr = lg[:, :, 0:NG]
            first_max(lgr, NG, gtop, ghot, wt)
            nc.vector.tensor_tensor(gexp, lgr, gtop.to_broadcast([P, NT, NG]), ALU.subtract).then_inc(gap_ready, 1)
            for t in range(NT):
                st(nc.vector.tensor_tensor(prod[:, t, :].rearrange("p (g e) -> p g e", g=NG),
                                           lg[:, t, NG:N36].rearrange("p (g e) -> p g e", g=NG),
                                           ghot[:, t, :].unsqueeze(2).to_broadcast([P, NG, EPG]), ALU.mult))
            st.sync()
            for t in range(NT):
                st(nc.vector.tensor_reduce(sel[:, t, :], prod[:, t, :].rearrange("p (g e) -> p e g", g=NG),
                                           AX.X, ALU.add))
            st.sync()
            first_max(sel, EPG, top1, hot1, wt)
            st(nc.vector.scalar_tensor_tensor(out=rest, in0=hot1, scalar=-BIG, in1=sel, op0=ALU.mult, op1=ALU.add))
            st.sync()
            first_max(rest, EPG, top2, hot2, wt)
            nc.vector.tensor_tensor(gap, top2, top1, ALU.subtract).then_inc(gap_ready, 1)
            dve.wait_ge(gap_exp, 2)
            st(nc.vector.tensor_reduce(gsum, gexp, AX.X, ALU.add))
            st(nc.vector.tensor_scalar(tot, gap, 1.0, None, ALU.add))
            st.sync()
            st(nc.vector.tensor_tensor(tot, tot, gsum, ALU.mult))
            st.sync()
            st(nc.vector.reciprocal(tot, tot))
            st.sync()
            st(nc.vector.tensor_tensor(gap, gap, tot, ALU.mult))
            st(nc.vector.tensor_tensor(hot1, hot1, tot.to_broadcast([P, NT, EPG]), ALU.mult))
            st.sync()
            st(nc.vector.tensor_tensor(hot2, hot2, gap.to_broadcast([P, NT, EPG]), ALU.mult))
            st.sync()
            st(nc.vector.tensor_tensor(hot1, hot1, hot2, ALU.add))
            st.sync()
            for t in range(NT):
                st(nc.vector.tensor_tensor(comb[:, t, :].rearrange("p (g e) -> p g e", g=NG),
                                           ghot[:, t, :].unsqueeze(2).to_broadcast([P, NG, EPG]),
                                           hot1[:, t, :].unsqueeze(1).to_broadcast([P, NG, EPG]), ALU.mult))
            st.sync()

            for i in st.loop(NE // 4, 12):
                def hidden(g):
                    dve.wait_ge(hid_silu, i * 8 + g + 1)
                    nc.vector.tensor_tensor(hT[:, g % 2, :], sg[:, g % 2, :], bank[2 * (g % 2) + 1][:, :],
                                            ALU.mult).then_inc(hid_h, 1)

                def take(e):
                    dve.wait_ge(hid_down, i * 8 + 2 * e + 2)
                    dve.wait_ge(moe_taken, i * 4 + e + 1)
                    for t in range(NT):
                        for half in range(2):
                            cs = slice(half * 512, (half + 1) * 512)
                            ins = nc.vector.scalar_tensor_tensor(
                                out=y[:, t, cs], in0=bank[4 + 2 * t + half][:, :],
                                scalar=comb[:, t, bass.ds(i * 4 + e, 1)], in1=y[:, t, cs],
                                op0=ALU.mult, op1=ALU.add)
                            if (t, half) == (1, 1):
                                ins.then_inc(moe_taken, 1)
                            else:
                                st(ins)

                hidden(0)
                hidden(1)
                for e in range(3):
                    hidden(2 * e + 2)
                    take(e)
                    hidden(2 * e + 3)
                take(3)
            dve.wait_ge(moe_taken, NE + 1)
            dve.wait_ge(gf_loaded, 16)
            for t in range(NT):
                st(nc.vector.tensor_tensor(y[:, t, :], y[:, t, :], ga2_row, ALU.mult))
            st(nc.vector.scalar_tensor_tensor(out=scf_row, in0=scf_row, scalar=1.0, in1=gf_row[:, :],
                                              op0=ALU.add, op1=ALU.mult))
            st.sync()
            nc.vector.tensor_tensor(x[:, :, :], x[:, :, :], y[:, :, :], ALU.add).then_inc(x_ready, 1)
            dve.wait_ge(x_ready, 2)
            norm_scale(dve, 2)
            dve.wait_ge(xs_act, 3)
            dve.wait_ge(xs_dve, 3)
            for t in range(NT):
                st(nc.vector.tensor_tensor(y[:, t, :], xs[:, t, :], scf_row, ALU.mult))
            st.sync()
            for t in range(NT):
                last = nc.vector.tensor_tensor(x[:, t, :], y[:, t, :], shf_row, ALU.add)
            last.then_inc(x_ready, 1)
            dve.wait_ge(x_ready, 3)
        J_FFN1, J_MIX, J_MIXOUT, J_KV, J_XQ, J_XO, J_FFN2 = 0, 22, 29, 31, 35, 37, 39
        PER_LAYER = 61
        LAYER_USES = [sum(1 for j in range(PER_LAYER) if j % SLOTS == s) for s in range(SLOTS)]
        MP = 13
        KAPPA = float(np.exp(-0.5))
        FB = NGRP
        FF0 = 2 * NE
        MATS = [("B", 0, "KK", 0, "dve", 0), ("B", 1, "KK", 1, "dve", 1), ("KK", 0, "B", 0, "dve", 2),
                ("KK", 1, "B", 1, "dve", 3), ("B", 0, "KK2", 0, "act", 0), ("K", 0, "KK", 0, "dve", 4),
                ("K", 1, "KK", 1, "dve", 5), ("K", 0, "KK2", 0, "act", 1), ("B", 0, "R", 0, "dve", 6),
                ("B", 1, "R", 1, "dve", 7), ("B", 0, "R2", 0, "act", 2), ("K", 0, "R", 0, "dve", 8),
                ("K", 1, "R", 1, "dve", 9), ("K", 0, "R2", 0, "act", 3)]

        def wait_piece2(eng, j, l, turn=0):
            s = j % SLOTS
            eng.wait_ge(w_full[s], (l * LAYER_USES[s] + (U_BLOCK2[s] + j // SLOTS + 1) + turn) * 16)
            return s

        def heads4(t):
            return t.rearrange("p (h t) -> p h t", t=P)

        def sync2(sp):
            def load(s, src, k, n):
                sp.dma_start(slot_w(s, k, n), src).then_inc(w_full[s], 16)

            def ffn_piece(l, name, g, p, s):
                if p == 0:
                    w = a[name + "_w_in_2"][l].rearrange("(k p) n -> p k n", p=P)
                    dst = slot_w(s, KD, 512)
                    sp.dma_start(dst[:, :, 0:256], w[:, :, bass.ds(g * 256, 256)]).then_inc(w_full[s], 16)
                    sp.dma_start(dst[:, :, 256:512], w[:, :, bass.ds(g * 256 + D_FF, 256)]).then_inc(up_full[s], 16)
                else:
                    w = a[name + "_w_out_2"][l][bass.ds(g * 256, 256), :]
                    load(s, w.rearrange("(k p) n -> p k n", p=P), 2, D)

            def ffn(l, n):
                f = l * 2 + n
                name = ("ffn1", "ffn2")[n]
                j0 = (J_FFN1, J_FFN2)[n]
                for p in range(SLOTS):
                    if n == 0:
                        before_layer(l, p)
                    else:
                        read(l, j0 + p - SLOTS)
                    ffn_piece(l, name, p // 2, p % 2, (j0 + p) % SLOTS)
                with sp.Fori(0, 4) as i:
                    for p in range(SLOTS):
                        sp.wait_ge(hid_up if p % 2 == 0 else hid_down, f * FB + i * 2 + (FF0 + p // 2 + 1))
                        sp.sem_inc(sp_passed, 1)
                        ffn_piece(l, name, i * 2 + (2 + p // 2), p % 2, (j0 + p) % SLOTS)
                for p in range(2):
                    sp.wait_ge(hid_up if p % 2 == 0 else hid_down, f * FB + (FF0 + 9))
                    sp.sem_inc(sp_passed, 1)
                    ffn_piece(l, name, 10, p, (j0 + p) % SLOTS)

            def before_layer(l, p):
                if p == 0:
                    sp.wait_ge(hid_down, l * (2 * FB) + FF0)
                    sp.sem_inc(sp_passed, 1)
                elif p == 1:
                    sp.wait_ge(hid_up, l * (2 * FB) + (FF0 - 1))
                    sp.sem_inc(sp_passed, 1)
                    sp.wait_ge(hid_down, l * (2 * FB) + (FF0 - 2))
                    sp.sem_inc(sp_passed, 1)
                elif p == 2:
                    sp.wait_ge(hid_down, l * (2 * FB) + (FF0 - 1))
                    sp.sem_inc(sp_passed, 1)
                else:
                    sp.wait_ge(hid_up, l * (2 * FB) + FF0)
                    sp.sem_inc(sp_passed, 1)

            def read(l, j):
                if j < J_MIX:
                    sp.wait_ge(hid_up if j % 2 == 0 else hid_down, l * (2 * FB) + (FF0 + j // 2 + 1))
                    sp.sem_inc(sp_passed, 1)
                elif j < J_MIXOUT:
                    n = j - J_MIX
                    sp.wait_ge(mp_full, l * MP + (2 * n + 2 if n < 5 else MP))
                    sp.sem_inc(sp_passed, 1)
                elif j < J_KV:
                    sp.wait_ge(mo_psum, l * 4 + 2 * (j - J_MIXOUT + 1))
                    sp.sem_inc(sp_passed, 1)
                elif j < J_XQ:
                    sp.wait_ge(kv_psum, l * 8 + 2 * (j - J_KV + 1))
                    sp.sem_inc(sp_passed, 1)
                elif j < J_XO:
                    sp.wait_ge(xq_psum, l * 4 + 2 * (j - J_XQ + 1))
                    sp.sem_inc(sp_passed, 1)
                else:
                    sp.wait_ge(xo_psum, l * 4 + 2 * (j - J_XO + 1))
                    sp.sem_inc(sp_passed, 1)

            with sp.Fori(0, DEPTH_2) as l:
                ffn(l, 0)
                mid = [(a["w_mix_in_2"], 512 * n, 512 if n < 6 else 256) for n in range(7)]
                mid += [(a["w_mix_out_2"], 512 * n, 512) for n in range(2)]
                mid += [(a["xattn_w_kv_2"], 512 * n, 512) for n in range(4)]
                mid += [(a["xattn_w_q_2"], 512 * n, 512) for n in range(2)]
                mid += [(a["xattn_w_o_2"], 512 * n, 512) for n in range(2)]
                for n, (w, c, width) in enumerate(mid):
                    read(l, J_MIX + n - SLOTS)
                    load((J_MIX + n) % SLOTS, w[l][:, c:c + width].rearrange("(k p) n -> p k n", p=P), KD, width)
                ffn(l, 1)

        def pool2(pool):
            pool.wait_ge(x_ready, 3)
            pool.dma_start(mem[:, :, :], a["mem_2"][0].rearrange("(t p) d -> p t d", p=P)).then_inc(mem_loaded, 16)
            pool.dma_start(relT[0:RB, :], a["rel_bias"]).then_inc(rel_loaded, 16)
            pool.dma_start(onehot[0:RB, :], a["bucket_onehot"]).then_inc(rel_loaded, 16)
            pool.dma_start(lc[:, :], a["cols2"][0]).then_inc(lc_loaded, 16)
            pool.dma_start(lora[0:64, :], a["rwkv_w_up_2"][0]).then_inc(lc_loaded, 16)
            pool.dma_start(lora[64:P, :], a["rwkv_a_up_2"][0]).then_inc(lc_loaded, 16)
            pool.dma_start(gup[:, :], a["rwkv_g_up_2"][0]).then_inc(lc_loaded, 16)
            norm_rstd(pool, 3)
            pool.wait_ge(bd_ready, 1)
            pool.dma_start(bias_dram.ap(), bydist[0:NH, :].unsqueeze(1).to_broadcast([NH, P, NDIST])
                           ).then_inc(bd_stored, 16)
            pool.wait_ge(bd_stored, 16)
            src = bass.AP(bias_dram, P - 1, [[NDIST - 1, P], [P * NDIST, NH], [1, SEQ]])
            pool.dma_start(biasT[:, :, :], src).then_inc(bias_loaded, 16)
            with pool.Fori(0, DEPTH_2) as l:
                norm_rstd(pool, l * 4 + 4)
                norm_rstd(pool, l * 4 + 5)
                norm_rstd(pool, l * 4 + 6)
                norm_rstd(pool, l * 4 + 7)
                pool.wait_ge(x_ready, l * 4 + 7)
                pool.sem_inc(pool_passed, 1)
                nxt = 1
                pool.dma_start(lc[:, :], a["cols2"][nxt]).then_inc(lc_loaded, 16)
                pool.dma_start(lora[0:64, :], a["rwkv_w_up_2"][nxt]).then_inc(lc_loaded, 16)
                pool.dma_start(lora[64:P, :], a["rwkv_a_up_2"][nxt]).then_inc(lc_loaded, 16)
                pool.dma_start(gup[:, :], a["rwkv_g_up_2"][nxt]).then_inc(lc_loaded, 16)
            pool.dma_start(gf2_row[:, :], a["final_norm_g_2"].partition_broadcast(P)).then_inc(gf2_loaded, 16)
            norm_rstd(pool, 12)
            pool.wait_ge(lc_loaded, 3 * 64)

        def tensor2(pe):
            norm_transposes(pe, 3, 3)
            pe.wait_ge(rel_loaded, 32)
            nc.tensor.matmul(bank[4][0:NH, 0:NDIST], relT[0:RB, :], onehot[0:RB, :],
                             start=True, stop=True).then_inc(bd_psum, 1)
            pe.wait_ge(bd_ready, 1)

            def ffn(l, n):
                f = l * 2 + n
                j0 = (J_FFN1, J_FFN2)[n]
                pe.wait_ge(xT_act, l * 4 + (4 + 3 * n))
                pe.wait_ge(xT_dve, l * 4 + (4 + 3 * n))

                def up(g, par, i=None):
                    turn = 0 if i is None else i
                    s = wait_piece2(pe, j0 + 2 * g, l, turn)
                    w = slot_w(s, KD, 512)
                    pe.wait_ge(up_full[s], (l * ((FB + 1) // 2 if par == 0 else FB // 2) + (g // 2 + 1) + turn) * 16)
                    for u in range(2):
                        for c in range(2):
                            for k in range(KD):
                                m = u * 256 + c * P
                                last = nc.tensor.matmul(bank[2 * par + u][:, c * SEQ:(c + 1) * SEQ],
                                                        w[:, k, m:m + P], xT[:, k, :],
                                                        start=(k == 0), stop=(k == KD - 1))
                    last.then_inc(hid_up, 1)

                def down(g, par, i=None, start=False, stop=False):
                    turn = 0 if i is None else i
                    count = f * FB + (FF0 + g + 1) if i is None else f * FB + i * 2 + (FF0 + g + 1)
                    pe.wait_ge(hid_h, count)
                    s = wait_piece2(pe, j0 + 2 * g + 1, l, turn)
                    w = slot_w(s, 2, D)
                    for t in range(NT):
                        for half in range(2):
                            for c in range(2):
                                last = nc.tensor.matmul(bank[4 + 2 * t + half][:, :],
                                                        fh[:, par, c * SEQ + t * P:c * SEQ + (t + 1) * P],
                                                        w[:, c, half * 512:(half + 1) * 512],
                                                        start=(start and c == 0), stop=(stop and c == 1))
                    last.then_inc(hid_down, 1)

                up(0, 0)
                up(1, 1)
                down(0, 0, start=True)
                with pe.Fori(0, 4) as i:
                    up(2, 0, i)
                    down(1, 1, i)
                    up(3, 1, i)
                    down(2, 0, i)
                up(10, 0)
                down(9, 1)
                down(10, 0, stop=True)

            def project(l, m):
                if m >= 8:
                    pe.wait_ge(mp_act, l * MP + (m - 7))
                b = bank[m % 8]
                if m < 11:
                    s = wait_piece2(pe, J_MIX + m // 2, l)
                    w = slot_w(s, KD, 512)
                    for c in range(2):
                        col = (m % 2) * 256 + c * P
                        for k in range(KD):
                            last = nc.tensor.matmul(b[:, c * SEQ:(c + 1) * SEQ], w[:, k, col:col + P], xT[:, k, :],
                                                    start=(k == 0), stop=(k == KD - 1))
                else:
                    t = m - 11
                    for part in range(2):
                        s = wait_piece2(pe, J_MIX + 5 + part, l)
                        w = slot_w(s, KD, 512)[:, :, 256:512] if part == 0 else slot_w(s, KD, 256)
                        for k in range(KD):
                            last = nc.tensor.matmul(b[:, part * 256:(part + 1) * 256], xT[:, k, t * P:(t + 1) * P],
                                                    w[:, k, :], start=(k == 0), stop=(k == KD - 1))
                last.then_inc(mp_full, 1)

            def rwkv_operands(l):
                pe.wait_ge(lo_ready, l * 2 + 2)
                pe.wait_ge(mp_act, (l + 1) * MP)
                for g in range(6):
                    kind, pair = g // 2, g % 2
                    for c in range(2):
                        m = 2 * pair + c
                        o = bank[g][:, c * SEQ:(c + 1) * SEQ]
                        ms_ = slice(m * P, (m + 1) * P)
                        if kind == 0:
                            last = nc.tensor.matmul(o, lora[0:64, ms_], pT[0:64, 12, :], start=True, stop=True)
                        elif kind == 1:
                            last = nc.tensor.matmul(o, lora[64:P, ms_], pT[64:P, 12, :], start=True, stop=True)
                        else:
                            last = nc.tensor.matmul(o, gup[:, ms_], pT[:, 13, :], start=True, stop=True)
                    last.then_inc(lora_psum, 1)
                pe.wait_ge(kk_sq, l + 1)
                for n in range(2):
                    nc.tensor.matmul(bank[6 + n][:, :], K[:, HEADS, :], flat(cw[:, 2 * n:2 * n + 2, :]),
                                     start=True, stop=True).then_inc(kk_psum, 1)
                pe.wait_ge(lora_act, (l + 1) * 6)
                for t in range(NT):
                    for m in range(4):
                        last = nc.tensor.transpose(bank[2 + t][:, m * P:(m + 1) * P],
                                                   pT[:, 8 + m, t * P:(t + 1) * P], eye)
                    last.then_inc(vt_psum, 1)

            def bonus(l):
                pe.wait_ge(rk_ready, l + 1)
                for n in range(2):
                    nc.tensor.matmul(bank[n][:, :], K[:, HEADS, :], flat(cw[:, 2 * n:2 * n + 2, :]),
                                     start=True, stop=True).then_inc(rk_psum, 1)

            def moba_attention(l):
                def scores(h):
                    r = slice((h % 2) * 64, (h % 2) * 64 + 64)
                    if h >= 2:
                        pe.wait_ge(mb_sb, l * NH + (h - 1))
                    b = bank[4 + h % 2]
                    nc.tensor.matmul(b[:, 0:P], qm[r, h // 2, 0:P], km[r, h // 2, 0:P], start=True, stop=True)
                    nc.tensor.matmul(b[:, P:384], qm[r, h // 2, P:SEQ], km[r, h // 2, :],
                                     start=True, stop=True).then_inc(mb_s, 1)

                def turned(h):
                    pe.wait_ge(mb_p, l * NH + (h + 1))
                    if h >= 2:
                        pe.wait_ge(mb_tc, l * NH + (h - 1))
                    b = bank[6 + h % 2]
                    for c, (dst, src) in enumerate(((0, 0), (P, P), (2 * P, 2 * P))):
                        last = nc.tensor.transpose(b[:, dst:dst + P], sm[:, h % 2, src:src + P], eye)
                    last.then_inc(mb_t, 1)

                def values(h):
                    pe.wait_ge(mb_tc, l * NH + (h + 1))
                    r = slice((h % 2) * 64, (h % 2) * 64 + 64)
                    o = bank[2 + h // 4][r, ((h // 2) % 2) * SEQ:((h // 2) % 2 + 1) * SEQ]
                    hs = slice(h * 64, (h + 1) * 64)
                    nc.tensor.matmul(o, vm[:, 0, hs], pmT[:, h % 2, 0:SEQ], start=True, stop=False)
                    nc.tensor.matmul(o[:, P:SEQ], vm[:, 1, hs], pmT[:, h % 2, SEQ:384],
                                     start=False, stop=True).then_inc(mb_o, 1)

                pe.wait_ge(kk_ss, (l + 1) * 2)
                pe.wait_ge(vt_ready, (l + 1) * 2)
                scores(0)
                scores(1)
                for h in range(NH):
                    turned(h)
                    if h + 2 < NH:
                        scores(h + 2)
                    values(h)

            def rwkv_heads(l, hb):
                r = l * 2 + hb
                rows_ = slice(hb * 64, hb * 64 + 64)
                c0, c1 = slice(0, P), slice(P, SEQ)

                def f(name, m, c):
                    if name == "R2":
                        return R2[rows_, m, :]
                    if name == "KK2":
                        return KK2[rows_, m, :]
                    t = {"B": aT, "KK": kk}.get(name)
                    if t is not None:
                        return t[rows_, m, c]
                    return pT[rows_, m + (4 if name == "K" else 0), c]

                if hb == 0:
                    pe.wait_ge(fac_ready, l + 1)
                    pe.wait_ge(mb_oc, (l + 1) * 2)
                    pe.wait_ge(bonus_ready, l + 1)
                else:
                    pe.wait_ge(yy_taken, l * 2 + 1)
                for idx, (lhs, lc_, rhs, rc_, by, nth) in enumerate(MATS):
                    if idx >= 8:
                        _, _, _, _, pby, pn = MATS[idx - 8]
                        pe.wait_ge(mat_dve if pby == "dve" else mat_act, r * (10 if pby == "dve" else 4) + (pn + 1))
                    for n in range(4):
                        last = nc.tensor.matmul(bank[idx % 8][:, n * P:(n + 1) * P], f(lhs, n, (c0, c1)[lc_]),
                                                f(rhs, n, (c0, c1)[rc_]), start=True, stop=True)
                    last.then_inc(mat_full, 1)
                pe.wait_ge(mat_dve, (r + 1) * 10)
                pe.wait_ge(mat_act, (r + 1) * 4)
                pe.wait_ge(inv_init, r + 1)
                for n in range(1, 7):
                    q = r * 12 + 2 * (n - 1)
                    for ch in range(2):
                        if n > 1:
                            pe.wait_ge(inv_xs, r * 12 + (2 * (n - 2) + ch + 1))
                        for h in range(4):
                            hs = slice(h * P, (h + 1) * P)
                            last = nc.tensor.matmul(bank[ch][:, hs], Lt[:, ch, hs], X[:, ch, hs],
                                                    start=True, stop=True)
                        last.then_inc(inv_p, 1)
                    for ch in range(2):
                        pe.wait_ge(inv_pm, q + (ch + 1))
                        if n > 1:
                            pe.wait_ge(inv_ys, r * 10 + (2 * (n - 2) + ch + 1))
                        for h in range(4):
                            hs = slice(h * P, (h + 1) * P)
                            last = nc.tensor.matmul(bank[2 + ch][:, hs], Y[:, ch, hs], Pm[:, ch, hs],
                                                    start=True, stop=True)
                        last.then_inc(inv_x, 1)
                        if n < 6:
                            for h in range(4):
                                hs = slice(h * P, (h + 1) * P)
                                last = nc.tensor.matmul(bank[4 + ch][:, hs], Pm[:, ch, hs], Y[:, ch, hs],
                                                        start=True, stop=True)
                            last.then_inc(inv_y, 1)
                pe.wait_ge(inv_xs, (r + 1) * 12)
                vs = [slice((2 * n + hb) * 64, (2 * n + hb + 1) * 64) for n in range(4)]
                us = [slice((4 * hb + n) * 64, (4 * hb + n + 1) * 64) for n in range(4)]
                for ch in range(2):
                    for n in range(4):
                        hs, o = slice(n * P, (n + 1) * P), bank[6][:, n * 64:(n + 1) * 64]
                        if ch == 0:
                            last = nc.tensor.matmul(o, Luk[:, 0, hs], vt[:, 0, vs[n]], start=True, stop=True)
                        else:
                            nc.tensor.matmul(o, Luk[:, 2, hs], vt[:, 0, vs[n]], start=True, stop=False)
                            nc.tensor.matmul(o, Luk[:, 1, hs], vt[:, 1, vs[n]], start=False, stop=False)
                            last = nc.tensor.matmul(o, Noff[:, hs], U[:, 0, us[n]], start=False, stop=True)
                    last.then_inc(u_psum, 1)
                    pe.wait_ge(u_taken, r * 4 + (2 * ch + 1))
                    for n in range(4):
                        hs = slice(n * P, (n + 1) * P)
                        last = nc.tensor.matmul(bank[7][:, n * 64:(n + 1) * 64], X[:, ch, hs],
                                                Pm[:, ch, n * 64:(n + 1) * 64], start=True, stop=True)
                    last.then_inc(u_psum, 1)
                    pe.wait_ge(u_taken, r * 4 + (2 * ch + 2))
                for n in range(4):
                    hs = slice(n * P, (n + 1) * P)
                    o = bank[n // 2][rows_, (n % 2) * SEQ:(n % 2 + 1) * SEQ]
                    v0, v1, u0, u1 = vt[:, 0, vs[n]], vt[:, 1, vs[n]], U[:, 0, us[n]], U[:, 1, us[n]]
                    nc.tensor.matmul(o[:, c0], u0, Mrb[:, 0, hs], start=True, stop=False)
                    nc.tensor.matmul(o[:, c0], v0, Mrk[:, 0, hs], start=False, stop=True)
                    nc.tensor.matmul(o[:, c1], u0, Mrb[:, 2, hs], start=True, stop=False)
                    nc.tensor.matmul(o[:, c1], v0, Mrk[:, 2, hs], start=False, stop=False)
                    nc.tensor.matmul(o[:, c1], u1, Mrb[:, 1, hs], start=False, stop=False)
                    last = nc.tensor.matmul(o[:, c1], v1, Mrk[:, 1, hs], start=False, stop=True)
                last.then_inc(yy_psum, 1)

            def to_tokens(l, src, j0, done, b0):
                for half in range(2):
                    s = wait_piece2(pe, j0 + half, l)
                    w = slot_w(s, KD, 512)
                    for t in range(NT):
                        for k in range(KD):
                            last = nc.tensor.matmul(bank[b0 + 2 * half + t][:, :], src[:, k, t * P:(t + 1) * P],
                                                    w[:, k, :], start=(k == 0), stop=(k == KD - 1))
                        last.then_inc(done, 1)

            def group_norm(l):
                pe.wait_ge(yy_taken, (l + 1) * 2)
                for n in range(2):
                    nc.tensor.matmul(bank[1 + n][:, :], K[:, HEADS, :], flat(xT[:, 2 * n:2 * n + 2, :]),
                                     start=True, stop=True).then_inc(gn_psum, 1)
                for n in range(2):
                    pe.wait_ge(gn_sq, l * 2 + (n + 1))
                    nc.tensor.matmul(bank[3 + n][:, :], K[:, HEADS, :], xs[:, 0, n * 512:(n + 1) * 512],
                                     start=True, stop=True).then_inc(gn_psum, 1)

            def cross_kv(l):
                pe.wait_ge(gm_ready, l * 2 + 2)
                for g in range(4):
                    s = wait_piece2(pe, J_KV + g // 2, l)
                    w = slot_w(s, KD, 512)
                    for c in range(2):
                        m = 2 * (g % 2) + c
                        for k in range(KD):
                            last = nc.tensor.matmul(bank[g][:, c * SEQ:(c + 1) * SEQ], w[:, k, m * P:(m + 1) * P],
                                                    gm[:, k, :], start=(k == 0), stop=(k == KD - 1))
                    last.then_inc(kv_psum, 1)
                pe.wait_ge(x_ready, l * 4 + 5)
                for half in range(2):
                    s = wait_piece2(pe, J_KV + 2 + half, l)
                    w = slot_w(s, KD, 512)
                    for t in range(NT):
                        for k in range(KD):
                            last = nc.tensor.matmul(bank[4 + 2 * half + t][:, :], gm[:, k, t * P:(t + 1) * P],
                                                    w[:, k, :], start=(k == 0), stop=(k == KD - 1))
                        last.then_inc(kv_psum, 1)

            def cross_attention(l):
                pe.wait_ge(kv_act, l * 8 + 4)
                norm_transposes(pe, l * 4 + 6, l * 4 + 6)
                pe.wait_ge(xT_act, l * 4 + 6)
                pe.wait_ge(xT_dve, l * 4 + 6)
                for g in range(4):
                    s = wait_piece2(pe, J_XQ + g // 2, l)
                    w = slot_w(s, KD, 512)
                    for c in range(2):
                        m = 2 * (g % 2) + c
                        for k in range(KD):
                            last = nc.tensor.matmul(bank[g][:, c * SEQ:(c + 1) * SEQ], w[:, k, m * P:(m + 1) * P],
                                                    xT[:, k, :], start=(k == 0), stop=(k == KD - 1))
                    last.then_inc(xq_psum, 1)
                pe.wait_ge(kv_act, (l + 1) * 8)
                pe.wait_ge(xq_act, (l + 1) * 4)

                def scores(h):
                    if h >= 2:
                        pe.wait_ge(xa_e, l * XH + (h - 1))
                    for t in range(NT):
                        for c in range(2):
                            last = nc.tensor.matmul(bank[4 + h % 2][:, t * SEQ:(t + 1) * SEQ],
                                                    qx[:, 2 * h + c, t * P:(t + 1) * P], kx[:, 2 * h + c, :],
                                                    start=(c == 0), stop=(c == 1))
                    last.then_inc(xa_s, 1)

                def turned(h):
                    pe.wait_ge(xa_p, l * XH + (h + 1))
                    if h >= 2:
                        pe.wait_ge(xa_tc, l * XH + (h - 1))
                    for t in range(NT):
                        for m in range(2):
                            last = nc.tensor.transpose(bank[6 + h % 2][:, m * SEQ + t * P:m * SEQ + (t + 1) * P],
                                                       sx[:, h % 2, t * SEQ + m * P:t * SEQ + (m + 1) * P], eye)
                    last.then_inc(xa_t, 1)

                def values(h):
                    pe.wait_ge(xa_tc, l * XH + (h + 1))
                    for c in range(2):
                        for m in range(2):
                            last = nc.tensor.matmul(bank[h][:, c * SEQ:(c + 1) * SEQ],
                                                    vx[:, m, h * XHD + c * P:h * XHD + (c + 1) * P],
                                                    pxT[:, h % 2, m * SEQ:(m + 1) * SEQ],
                                                    start=(m == 0), stop=(m == 1))
                    last.then_inc(xa_o, 1)

                scores(0)
                scores(1)
                for h in range(XH):
                    turned(h)
                    if h + 2 < XH:
                        scores(h + 2)
                    values(h)
                pe.wait_ge(xa_oc, (l + 1) * XH)
                to_tokens(l, xT, J_XO, xo_psum, 0)

            with pe.Fori(0, DEPTH_2) as l:
                norm_transposes(pe, l * 4 + 4, l * 4 + 4)
                ffn(l, 0)
                norm_transposes(pe, l * 4 + 5, l * 4 + 5)
                pe.wait_ge(xT_act, l * 4 + 5)
                pe.wait_ge(xT_dve, l * 4 + 5)
                for m in range(MP):
                    project(l, m)
                rwkv_operands(l)
                moba_attention(l)
                bonus(l)
                for hb in range(2):
                    rwkv_heads(l, hb)
                group_norm(l)
                pe.wait_ge(ycat, l + 1)
                to_tokens(l, xT, J_MIXOUT, mo_psum, 4)
                cross_kv(l)
                cross_attention(l)
                norm_transposes(pe, l * 4 + 7, l * 4 + 7)
                ffn(l, 1)
        def scalar2(act, st):
            act.wait_ge(mem_loaded, 16)
            act.wait_ge(x_ready, 3)
            norm_sums(act, 3, mem)
            for k in (0, 1, 4, 5):
                act.wait_ge(tr_full, 12 + k // 2 + 1)
                last = nc.scalar.activation(memT[:, k, :], tr_bank(k), ACT.Copy)
            last.then_inc(xT_act, 1)
            act.wait_ge(tr_full, 16)

            def ffn(l, n):
                f = l * 2 + n
                gain = column(lc, C2, ("ffn1_g", "ffn2_g")[n])
                act.wait_ge(x_ready, l * 4 + 3 + 3 * n)
                if n == 0:
                    act.wait_ge(lc_loaded, (l + 1) * 64)
                norm_sums(act, l * 4 + 4 + 3 * n)
                xT_by_act(act, l * 4 + 4 + 3 * n, gain)

                def silu(par, count):
                    act.wait_ge(hid_up, count)
                    nc.scalar.activation(fs[:, par, :], bank[2 * par][:, :], ACT.Silu).then_inc(hid_silu, 1)

                silu(0, f * FB + FF0 + 1)
                with act.Fori(0, FB // 2) as i:
                    silu(1, f * FB + i * 2 + (FF0 + 2))
                    silu(0, f * FB + i * 2 + (FF0 + 3))

            def mixer(l):
                act.wait_ge(x_ready, l * 4 + 4)
                norm_sums(act, l * 4 + 5)
                xT_by_act(act, l * 4 + 5, column(lc, C2, "mix_g"))

                def take(m):
                    act.wait_ge(mp_full, l * MP + (m + 1))
                    b = bank[m % 8][:, :]
                    if m < 7:
                        nc.scalar.activation(flat(pT[:, 2 * m:2 * m + 2, :]), b, ACT.Copy).then_inc(mp_act, 1)
                    elif m < 11:
                        t, n = (qm, m - 7) if m < 9 else (km, m - 9)
                        nc.scalar.activation(flat(t[:, 2 * n:2 * n + 2, :]), b, ACT.Copy,
                                             scale=HD ** -0.5 if m < 9 else 1.0).then_inc(mp_act, 1)
                    else:
                        nc.scalar.activation(vm[:, m - 11, :], b, ACT.Copy).then_inc(mp_act, 1)

                for m in range(7):
                    take(m)
                act.wait_ge(shifted, l * 7 + 4)
                for k in range(4):
                    st(nc.scalar.activation(kk[:, k, :], pT[:, 4 + k, :], ACT.Copy,
                                            scale=column(lc, C2, "k_k")[:, k:k + 1]))
                st.sync()
                nc.scalar.activation(flat(cw[:, :, :]), flat(kk[:, :, :]), ACT.Square).then_inc(kk_sq, 1)
                take(7)
                take(8)
                act.wait_ge(shifted, l * 7 + 7)
                nc.scalar.activation(pT[0:64, 12, :], pT[0:64, 12, :], ACT.Tanh).then_inc(lo_ready, 1)
                nc.scalar.activation(pT[:, 13, :], pT[:, 13, :], ACT.Sigmoid).then_inc(lo_ready, 1)
                for m in range(9, 13):
                    take(m)
                for n in range(2):
                    act.wait_ge(kk_ss, l * 2 + (n + 1))
                    t = flat(bon[:, 2 * n:2 * n + 2, :])
                    nc.scalar.activation(t, t, ACT.Sqrt).then_inc(kk_rs, 1)
                for g in range(6):
                    act.wait_ge(lora_psum, l * 6 + (g + 1))
                    kind, pair = g // 2, g % 2
                    if kind < 2:
                        for c in range(2):
                            m = 2 * pair + c
                            last = nc.scalar.activation((lw, aT)[kind][:, m, :], bank[g][:, c * SEQ:(c + 1) * SEQ],
                                                        ACT.Sigmoid,
                                                        bias=column(lc, C2, ("w0", "a0")[kind])[:, m:m + 1])
                    else:
                        last = nc.scalar.activation(flat(gT[:, 2 * pair:2 * pair + 2, :]), bank[g][:, :], ACT.Copy)
                    last.then_inc(lora_act, 1)
                for t in range(NT):
                    act.wait_ge(vt_psum, l * 2 + (t + 1))
                    nc.scalar.activation(vt[:, t, :], bank[2 + t][:, :], ACT.Copy).then_inc(vt_ready, 1)
                act.wait_ge(dec2_ready, l + 1)
                nc.scalar.activation(E3, E1, ACT.Exp, scale=KAPPA).then_inc(e_ready, 1)
                act.wait_ge(e_ready, l * 4 + 1)
                nc.scalar.activation(E1, E1, ACT.Exp, scale=-KAPPA).then_inc(e_ready, 1)
                nc.scalar.activation(flat(lw[:, :, :]), flat(lw[:, :, :]), ACT.Exp, scale=-KAPPA).then_inc(e_ready, 1)
                nc.scalar.activation(small[:, 0:4], small[:, 0:4], ACT.Exp, scale=-KAPPA).then_inc(e_ready, 1)

                def expo(h):
                    act.wait_ge(mb_max, l * NH + (h + 1))
                    o = 4 * (h % 2)
                    nc.scalar.activation(sm[:, h % 2, 0:P], sm[:, h % 2, 0:P], ACT.Exp,
                                         bias=small[:, 8 + o:9 + o], accum_out=small[:, 16 + o:17 + o])
                    nc.scalar.activation(sm[:, h % 2, P:384], sm[:, h % 2, P:384], ACT.Exp,
                                         bias=small[:, 9 + o:10 + o],
                                         accum_out=small[:, 17 + o:18 + o]).then_inc(mb_e, 1)

                expo(0)
                for h in range(NH):
                    if h + 1 < NH:
                        expo(h + 1)
                    act.wait_ge(mb_t, l * NH + (h + 1))
                    if h >= 2:
                        act.wait_ge(mb_o, l * NH + (h - 1))
                    nc.scalar.activation(pmT[:, h % 2, :], bank[6 + h % 2][:, 0:384], ACT.Copy).then_inc(mb_tc, 1)
                    if h % 4 == 3:
                        act.wait_ge(mb_o, l * NH + (h + 1))
                        m = 4 + 2 * (h // 4)
                        nc.scalar.activation(flat(xT[:, m:m + 2, :]), bank[2 + h // 4][:, :],
                                             ACT.Copy).then_inc(mb_oc, 1)
                for hb in range(2):
                    r = l * 2 + hb
                    for idx, (_, _, _, _, by, n) in enumerate(MATS):
                        if by == "act":
                            act.wait_ge(mat_full, r * len(MATS) + (idx + 1))
                            dst = (Noff[:, :], Luk[:, 2, :], Mrb[:, 2, :], Mrk[:, 2, :])[n]
                            nc.scalar.activation(dst, bank[idx % 8][:, :], ACT.Copy).then_inc(mat_act, 1)
                    for n in range(4):
                        act.wait_ge(u_psum, r * 4 + (n + 1))
                        if n % 2 == 0:
                            nc.scalar.activation(Pm[:, n // 2, 0:256], bank[6][:, 0:256], ACT.Copy,
                                                 scale=-1.0).then_inc(u_taken, 1)
                        else:
                            nc.scalar.activation(U[:, n // 2, hb * 256:(hb + 1) * 256], bank[7][:, 0:256],
                                                 ACT.Copy).then_inc(u_taken, 1)
                    act.wait_ge(yy_psum, r + 1)
                    rows_ = slice(hb * 64, hb * 64 + 64)
                    for n in range(2):
                        last = nc.scalar.activation(flat(xT[rows_, 2 * n:2 * n + 2, :]), bank[n][rows_, :], ACT.Copy)
                    last.then_inc(yy_taken, 1)
                for n in range(2):
                    act.wait_ge(gn_xc, l * 2 + (n + 1))
                    nc.scalar.activation(xs[:, 0, n * 512:(n + 1) * 512], flat(xT[:, 2 * n:2 * n + 2, :]),
                                         ACT.Square).then_inc(gn_sq, 1)
                for n in range(2):
                    act.wait_ge(gn_var, l * 2 + (n + 1))
                    t = xs[:, 1, n * 512:(n + 1) * 512]
                    nc.scalar.activation(t, t, ACT.Sqrt).then_inc(gn_rs, 1)
                for k in range(4):
                    act.wait_ge(gn_norm, l * 2 + (k // 2 + 1))
                    last = nc.scalar.activation(xT[:, k, :], xT[:, k, :], ACT.Identity,
                                                scale=column(lc, C2, "ln_g")[:, k:k + 1],
                                                bias=column(lc, C2, "ln_b")[:, k:k + 1])
                    if k % 2:
                        last.then_inc(gn_aff, 1)
                act.wait_ge(ycat, l + 1)
                for k in range(KD // 2):
                    last = nc.scalar.activation(gm[:, k, :], memT[:, k, :], ACT.Copy,
                                                scale=column(lc, C2, "mem_g")[:, k:k + 1])
                last.then_inc(gm_ready, 1)

            def cross(l):
                for g in range(4):
                    act.wait_ge(kv_psum, l * 8 + (g + 1))
                    nc.scalar.activation(flat(kx[:, 2 * g:2 * g + 2, :]), bank[g][:, :], ACT.Copy).then_inc(kv_act, 1)
                act.wait_ge(x_ready, l * 4 + 5)
                norm_sums(act, l * 4 + 6)
                for g in range(4):
                    act.wait_ge(kv_psum, l * 8 + (g + 5))
                    nc.scalar.activation(vx[:, g % 2, (g // 2) * 512:(g // 2 + 1) * 512], bank[4 + g][:, :],
                                         ACT.Copy).then_inc(kv_act, 1)
                xT_by_act(act, l * 4 + 6, column(lc, C2, "xattn_g"))
                for g in range(4):
                    act.wait_ge(xq_psum, l * 4 + (g + 1))
                    nc.scalar.activation(flat(qx[:, 2 * g:2 * g + 2, :]), bank[g][:, :], ACT.Copy).then_inc(xq_act, 1)

                def expo(h):
                    act.wait_ge(xa_max, l * XH + (h + 1))
                    if h >= 2:
                        act.wait_ge(xa_t, l * XH + (h - 1))
                    for t in range(NT):
                        ts = slice(t * SEQ, (t + 1) * SEQ)
                        o = 4 * (h % 2) + t
                        last = nc.scalar.activation(sx[:, h % 2, ts], bank[4 + h % 2][:, ts], ACT.Exp,
                                                    bias=xsm[:, o:o + 1], scale=XHD ** -0.5,
                                                    accum_out=xsm[:, o + 2:o + 3])
                    last.then_inc(xa_e, 1)

                def out(h):
                    act.wait_ge(xa_o, l * XH + (h + 1))
                    nc.scalar.activation(flat(xT[:, 2 * h:2 * h + 2, :]), bank[h][:, :], ACT.Copy).then_inc(xa_oc, 1)

                expo(0)
                for h in range(XH):
                    if h + 1 < XH:
                        expo(h + 1)
                    act.wait_ge(xa_t, l * XH + (h + 1))
                    if h >= 2:
                        act.wait_ge(xa_o, l * XH + (h - 1))
                    nc.scalar.activation(pxT[:, h % 2, :], bank[6 + h % 2][:, :], ACT.Copy).then_inc(xa_tc, 1)
                    if h:
                        out(h - 1)
                out(XH - 1)

            for l in st.loop(DEPTH_2, 4):
                ffn(l, 0)
                mixer(l)
                cross(l)
                ffn(l, 1)
            act.wait_ge(x_ready, 11)
            norm_sums(act, 12)

        def vector2(dve, st):
            dve.wait_ge(mem_loaded, 16)
            norm_scale(dve, 3, mem)
            for k in (2, 3, 6, 7):
                dve.wait_ge(tr_full, 12 + k // 2 + 1)
                last = nc.vector.tensor_copy(memT[:, k, :], tr_bank(k))
            last.then_inc(xT_dve, 1)
            dve.wait_ge(bd_psum, 1)
            st(nc.vector.tensor_copy(bydist[0:NH, 0:SEQ], bank[4][0:NH, 0:SEQ]))
            nc.vector.memset(bydist[0:NH, SEQ:NDIST], -BIG).then_inc(bd_ready, 1)

            def ffn(l, n):
                f = l * 2 + n
                e = l * 4 + 4 + 3 * n
                if n == 0:
                    dve.wait_ge(lc_loaded, (l + 1) * 64)
                norm_scale(dve, e)
                xT_by_dve(dve, e, column(lc, C2, ("ffn1_g", "ffn2_g")[n]))

                def hidden(par, count):
                    dve.wait_ge(hid_silu, count)
                    nc.vector.tensor_tensor(fh[:, par, :], fs[:, par, :], bank[2 * par + 1][:, :],
                                            ALU.mult).then_inc(hid_h, 1)

                hidden(0, f * FB + FF0 + 1)
                with dve.Fori(0, FB // 2) as i:
                    hidden(1, f * FB + i * 2 + (FF0 + 2))
                    hidden(0, f * FB + i * 2 + (FF0 + 3))
                dve.wait_ge(hid_down, f * FB + (FF0 + FB))
                for t in range(NT):
                    for half in range(2):
                        cs = slice(half * 512, (half + 1) * 512)
                        last = nc.vector.scalar_tensor_tensor(out=x[:, t, cs], in0=bank[4 + 2 * t + half][:, :],
                                                              scalar=0.5, in1=x[:, t, cs], op0=ALU.mult, op1=ALU.add)
                last.then_inc(x_ready, 1)
                dve.wait_ge(x_ready, e)

            def add_tokens(b0, done, count, e):
                for g in range(4):
                    half, t = g // 2, g % 2
                    cs = slice(half * 512, (half + 1) * 512)
                    dve.wait_ge(done, count + (g + 1))
                    last = nc.vector.tensor_tensor(x[:, t, cs], x[:, t, cs], bank[b0 + g][:, :], ALU.add)
                last.then_inc(x_ready, 1)
                dve.wait_ge(x_ready, e)

            def mixer(l):
                norm_scale(dve, l * 4 + 5)
                xT_by_dve(dve, l * 4 + 5, column(lc, C2, "mix_g"))
                for m in range(7):
                    dve.wait_ge(mp_act, l * MP + (m + 1))
                    p = pT[:, 2 * m:2 * m + 2, :]
                    d = bon[:, 2 * (m % 2):2 * (m % 2) + 2, :]
                    st(nc.vector.tensor_tensor(d[:, :, 1:SEQ], p[:, :, 0:SEQ - 1], p[:, :, 1:SEQ], ALU.subtract))
                    st(nc.vector.tensor_scalar(d[:, :, 0:1], p[:, :, 0:1], -1.0, None, ALU.mult))
                    st.sync()
                    for c in range(2):
                        last = nc.vector.scalar_tensor_tensor(
                            out=p[:, c, :], in0=d[:, c, :], scalar=column(lc, C2, "mu")[:, 2 * m + c:2 * m + c + 1],
                            in1=p[:, c, :], op0=ALU.mult, op1=ALU.add)
                    last.then_inc(shifted, 1)
                dve.wait_ge(shifted, (l + 1) * 7)
                for n in range(2):
                    dve.wait_ge(kk_psum, l * 2 + (n + 1))
                    nc.vector.tensor_scalar(flat(bon[:, 2 * n:2 * n + 2, :]), bank[6 + n][:, :], 1e-24, None,
                                            ALU.max).then_inc(kk_ss, 1)
                dve.wait_ge(lora_act, l * 6 + 4)
                for m in range(4):
                    for ch in range(2):
                        cs = slice(ch * P, (ch + 1) * P)
                        st(nc.vector.tensor_tensor_scan(cw[:, m, cs], ones256[:, 0:P], lw[:, m, cs], 0.0,
                                                        ALU.mult, ALU.add))
                st(nc.vector.tensor_scalar(small[:, 4:8], column(lc, C2, "k_a"), -1.0, 1.0, ALU.mult, ALU.add))
                st.sync()
                mid = P // 2 - 1
                c8 = cw[:, :, :].rearrange("p m (c t) -> p (m c) t", t=P)
                st(nc.vector.tensor_tensor(E1.rearrange("p (a t) -> p a t", t=P), c8,
                                           c8[:, :, mid:mid + 1].to_broadcast([P, 8, P]), ALU.subtract))
                sm4 = small[:, 0:4].unsqueeze(2)
                st(nc.vector.tensor_tensor(sm4, cw[:, :, P - 1:P], cw[:, :, mid:mid + 1], ALU.subtract))
                st.sync()
                st(nc.vector.tensor_tensor(sm4, sm4, cw[:, :, P + mid:P + mid + 1], ALU.add))
                nc.vector.tensor_tensor(flat(lw[:, :, :]), E1, flat(lw[:, :, :]), ALU.subtract).then_inc(dec2_ready, 1)
                st.sync()
                for m in range(4):
                    st(nc.vector.tensor_scalar(cw[:, m, :], aT[:, m, :], column(lc, C2, "k_a")[:, m:m + 1],
                                               small[:, 4 + m:5 + m], ALU.mult, ALU.add))
                st.sync()
                st(nc.vector.tensor_tensor(pT[:, 4:8, :], pT[:, 4:8, :], cw[:, :, :], ALU.mult))
                st.sync()
                for m in range(4):
                    last = nc.vector.scalar_tensor_tensor(out=cw[:, m, :], in0=pT[:, m, :],
                                                          scalar=column(lc, C2, "r_k")[:, m:m + 1],
                                                          in1=pT[:, 4 + m, :], op0=ALU.mult, op1=ALU.mult)
                last.then_inc(rk_ready, 1)
                dve.wait_ge(kk_rs, l * 2 + 2)
                st(nc.vector.reciprocal(flat(bon[:, :, :]), flat(bon[:, :, :])))
                st.sync()
                st(nc.vector.tensor_tensor(kk[:, :, :], kk[:, :, :], bon[:, :, :], ALU.mult))
                st.sync()
                st(nc.vector.tensor_tensor(aT[:, :, :], kk[:, :, :], aT[:, :, :], ALU.mult))
                st.sync()
                dve.wait_ge(e_ready, l * 4 + 4)
                e1, e3 = (e.rearrange("p (m t) -> p m t", t=SEQ) for e in (E1, E3))
                st(nc.vector.tensor_tensor(pT[:, 0:4, :], pT[:, 0:4, :], e1, ALU.mult))
                st(nc.vector.tensor_tensor(kk[:, :, :], kk[:, :, :], lw[:, :, :], ALU.mult))
                st(nc.vector.tensor_tensor(aT[:, :, :], aT[:, :, :], e3, ALU.mult))
                st(nc.vector.tensor_tensor(pT[:, 4:8, :], pT[:, 4:8, :], e3, ALU.mult))
                st.sync()
                for m in range(4):
                    st(nc.vector.tensor_scalar(R2[:, m, :], pT[:, m, P:SEQ], small[:, m:m + 1], None, ALU.mult))
                    ins = nc.vector.tensor_scalar(KK2[:, m, :], kk[:, m, P:SEQ], small[:, m:m + 1], None, ALU.mult)
                    st(ins) if m < 3 else ins.then_inc(fac_ready, 1)

                def logits(h):
                    dve.wait_ge(mb_s, l * NH + (h + 1))
                    b = bank[4 + h % 2]
                    o = 8 + 4 * (h % 2)
                    st(nc.vector.tensor_tensor(sm[:, h % 2, 0:P], b[:, 0:P], biasT[:, h, P:SEQ], ALU.add))
                    nc.vector.tensor_tensor(sm[:, h % 2, P:384], b[:, P:384], biasT[:, h, :],
                                            ALU.add).then_inc(mb_sb, 1)
                    dve.wait_ge(mb_sb, l * NH + (h + 1))
                    nc.vector.tensor_reduce(small[:, o:o + 1], sm[:, h % 2, 0:P], AX.X, ALU.max, negate=True)
                    nc.vector.tensor_reduce(small[:, o + 1:o + 2], sm[:, h % 2, P:384], AX.X, ALU.max,
                                            negate=True).then_inc(mb_max, 1)

                def probs(h):
                    dve.wait_ge(mb_e, l * NH + (h + 1))
                    o = 16 + 4 * (h % 2)
                    st(nc.vector.reciprocal(small[:, o + 2:o + 4], small[:, o:o + 2]))
                    st.sync()
                    st(nc.vector.tensor_scalar(sm[:, h % 2, 0:P], sm[:, h % 2, 0:P], small[:, o + 2:o + 3], None,
                                               ALU.mult))
                    nc.vector.tensor_scalar(sm[:, h % 2, P:384], sm[:, h % 2, P:384], small[:, o + 3:o + 4], None,
                                            ALU.mult).then_inc(mb_p, 1)

                dve.wait_ge(bias_loaded, 16)
                logits(0)
                for h in range(NH):
                    if h + 1 < NH:
                        if h >= 1:
                            dve.wait_ge(mb_t, l * NH + h)
                        logits(h + 1)
                    probs(h)
                for n in range(2):
                    dve.wait_ge(rk_psum, l * 2 + (n + 1))
                    last = nc.vector.tensor_tensor(flat(bon[:, 2 * n:2 * n + 2, :]), bank[n][:, :],
                                                   flat(pT[:, 8 + 2 * n:10 + 2 * n, :]), ALU.mult)
                last.then_inc(bonus_ready, 1)
                for hb in range(2):
                    r = l * 2 + hb
                    for idx, (_, _, _, _, by, n) in enumerate(MATS):
                        if by == "dve":
                            dve.wait_ge(mat_full, r * len(MATS) + (idx + 1))
                            dst, mask = ((Nd[:, 0, :], UPPER), (Nd[:, 1, :], UPPER), (Lt[:, 0, :], LOWER),
                                         (Lt[:, 1, :], LOWER), (Luk[:, 0, :], UPPER), (Luk[:, 1, :], UPPER),
                                         (Mrb[:, 0, :], UPPER_EQ), (Mrb[:, 1, :], UPPER_EQ),
                                         (Mrk[:, 0, :], UPPER_EQ), (Mrk[:, 1, :], UPPER_EQ))[n]
                            nc.vector.tensor_tensor(heads4(dst), heads4(bank[idx % 8][:, :]),
                                                    K[:, mask, :].unsqueeze(1).to_broadcast([P, 4, P]),
                                                    ALU.mult).then_inc(mat_dve, 1)
                    dve.wait_ge(mat_dve, (r + 1) * 10)

                    def bc(n, k=8):
                        return K[:, n, :].unsqueeze(1).to_broadcast([P, k, P])

                    def eight(t):
                        return t[:, :, :].rearrange("p c (h t) -> p (c h) t", t=P)

                    st(nc.vector.tensor_tensor(eight(X), eight(Nd), bc(LEV), ALU.mult))
                    st(nc.vector.tensor_tensor(eight(Y), eight(Lt), bc(LEVT), ALU.mult))
                    st.sync()
                    st(nc.vector.tensor_tensor(eight(X), bc(EYE), eight(X), ALU.subtract))
                    nc.vector.tensor_tensor(eight(Y), bc(EYE), eight(Y), ALU.subtract).then_inc(inv_init, 1)
                    dve.wait_ge(inv_init, r + 1)
                    st.sync()
                    for n in range(1, 7):
                        q = r * 12 + 2 * (n - 1)
                        for ch in range(2):
                            dve.wait_ge(inv_p, q + (ch + 1))
                            nc.vector.tensor_tensor(heads4(Pm[:, ch, :]), heads4(bank[ch][:, :]), bc(LEV + n, 4),
                                                    ALU.mult).then_inc(inv_pm, 1)
                        for ch in range(2):
                            dve.wait_ge(inv_x, q + (ch + 1))
                            nc.vector.tensor_tensor(X[:, ch, :], X[:, ch, :], bank[2 + ch][:, :],
                                                    ALU.subtract).then_inc(inv_xs, 1)
                            if n < 6:
                                dve.wait_ge(inv_y, r * 10 + (2 * (n - 1) + ch + 1))
                                nc.vector.tensor_tensor(Y[:, ch, :], Y[:, ch, :], bank[4 + ch][:, :],
                                                        ALU.subtract).then_inc(inv_ys, 1)
                        dve.wait_ge(inv_xs, q + 2)
                for n in range(2):
                    dve.wait_ge(gn_psum, l * 4 + (n + 1))
                    t = flat(xT[:, 2 * n:2 * n + 2, :])
                    nc.vector.scalar_tensor_tensor(out=t, in0=bank[1 + n][:, :], scalar=-1.0 / HD, in1=t,
                                                   op0=ALU.mult, op1=ALU.add).then_inc(gn_xc, 1)
                for n in range(2):
                    dve.wait_ge(gn_psum, l * 4 + (n + 3))
                    nc.vector.tensor_scalar(xs[:, 1, n * 512:(n + 1) * 512], bank[3 + n][:, :], 1.0 / HD, LNX_EPS,
                                            ALU.mult, ALU.add).then_inc(gn_var, 1)
                for n in range(2):
                    dve.wait_ge(gn_rs, l * 2 + (n + 1))
                    t = flat(xT[:, 2 * n:2 * n + 2, :])
                    st(nc.vector.reciprocal(xs[:, 1, n * 512:(n + 1) * 512], xs[:, 1, n * 512:(n + 1) * 512]))
                    st.sync()
                    nc.vector.tensor_tensor(t, t, xs[:, 1, n * 512:(n + 1) * 512], ALU.mult).then_inc(gn_norm, 1)
                for n in range(2):
                    dve.wait_ge(gn_aff, l * 2 + (n + 1))
                    st(nc.vector.tensor_tensor(xT[:, 2 * n:2 * n + 2, :], xT[:, 2 * n:2 * n + 2, :],
                                               bon[:, 2 * n:2 * n + 2, :], ALU.add))
                st.sync()
                nc.vector.tensor_tensor(xT[:, 0:4, :], xT[:, 0:4, :], gT[:, :, :], ALU.mult).then_inc(ycat, 1)
                dve.wait_ge(ycat, l + 1)
                for k in range(KD // 2, KD):
                    last = nc.vector.tensor_scalar(gm[:, k, :], memT[:, k, :], column(lc, C2, "mem_g")[:, k:k + 1],
                                                   None, ALU.mult)
                last.then_inc(gm_ready, 1)
                add_tokens(4, mo_psum, l * 4, l * 4 + 5)

            def cross(l):
                norm_scale(dve, l * 4 + 6)
                xT_by_dve(dve, l * 4 + 6, column(lc, C2, "xattn_g"))

                def maxima(h):
                    dve.wait_ge(xa_s, l * XH + (h + 1))
                    o = 4 * (h % 2)
                    st(nc.vector.tensor_reduce(xsm[:, o:o + 2],
                                               bank[4 + h % 2][:, :].rearrange("p (t m) -> p t m", t=NT),
                                               AX.X, ALU.max))
                    st.sync()
                    nc.vector.tensor_scalar(xsm[:, o:o + 2], xsm[:, o:o + 2], -XHD ** -0.5, None,
                                            ALU.mult).then_inc(xa_max, 1)

                def probs(h):
                    dve.wait_ge(xa_e, l * XH + (h + 1))
                    o = 4 * (h % 2)
                    st(nc.vector.reciprocal(xsm[:, 8 + o:10 + o], xsm[:, o + 2:o + 4]))
                    st.sync()
                    for t in range(NT):
                        s_ = sx[:, h % 2, t * SEQ:(t + 1) * SEQ]
                        last = nc.vector.tensor_scalar(s_, s_, xsm[:, 8 + o + t:9 + o + t], None, ALU.mult)
                    last.then_inc(xa_p, 1)

                maxima(0)
                for h in range(XH):
                    if h + 1 < XH:
                        maxima(h + 1)
                    probs(h)
                add_tokens(0, xo_psum, l * 4, l * 4 + 6)

            for l in st.loop(DEPTH_2, VECTOR_STEPS):
                ffn(l, 0)
                mixer(l)
                cross(l)
                ffn(l, 1)
            norm_scale(dve, 12)
            dve.wait_ge(xs_act, 13)
            dve.wait_ge(xs_dve, 13)
            dve.wait_ge(gf2_loaded, 16)
            for t in range(NT):
                last = nc.vector.tensor_tensor(x[:, t, :], xs[:, t, :], gf2_row[:, :], ALU.mult)
            last.then_inc(x_ready, 1)

        block = ctx.enter_context(nc.Block())

        @block.sync
        def _(sp):
            sync1(sp)
            sync2(sp)
            sp.wait_ge(x_ready, 12)
            sp.dma_start(out[0].rearrange("(t p) d -> p t d", p=P), x[:, :, :]).then_inc(out_stored, 16)
            sp.wait_ge(out_stored, 16)

        @block.gpsimd
        def _(pool):
            pool1(pool)
            pool2(pool)

        @block.tensor
        def _(pe):
            tensor1(pe)
            tensor_moe(pe)
            tensor2(pe)

        @block.scalar
        def _(act):
            st = scalar1(act)
            scalar_moe(act)
            scalar2(act, st)

        @block.vector
        def _(dve):
            st = vector1(dve)
            vector_moe(dve, st)
            vector2(dve, st)


def kernel(**inputs):
    import concourse.bacc as bacc
    from concourse.bass_utils import run_bass_kernel_spmd

    def tiles(v):
        v = v.reshape(v.shape[:-1] + (v.shape[-1] // P, P))
        return np.swapaxes(v, -1, -2)

    i = {k: np.asarray(v) for k, v in inputs.items()}
    b_ada = i["b_ada"][0].reshape(6, D)
    first = {"c": i["c"][0], "g_norm1": i["g_norm1"][0], "sh1": b_ada[0], "sc1": b_ada[1], "sh2": b_ada[3],
             "sc2": b_ada[4], **{n: i[n][0] for n in ("b_dw", "g_conv_ln", "b_conv_ln", "b_conv_pw", "b_a2",
                                                     "g_gla_norm", "g_norm2")}}
    parts = [tiles(first[n]) for n in C1 if n != "w_dw"]
    parts.append(np.transpose(i["w_dw"][0, :, 0, :].reshape(CONV_WIDTH, 4, P), (2, 1, 0)).reshape(P, 4 * CONV_WIDTH))
    second = {"ffn1_g": "ffn1_norm_g_2", "mix_g": "mix_norm_g_2", "mu": "rwkv_mu_2", "w0": "rwkv_w0_2",
              "a0": "rwkv_a0_2", "k_k": "rwkv_k_k_2", "k_a": "rwkv_k_a_2", "r_k": "rwkv_r_k_2",
              "ln_g": "rwkv_ln_g_2", "ln_b": "rwkv_ln_b_2", "xattn_g": "xattn_norm_g_2",
              "mem_g": "mem_norm_g_2", "ffn2_g": "ffn2_norm_g_2"}
    arrays = {n: i[n] for n in ("x", "w_ada", "b_ada", "w_in", "w_conv_pw", "w_a2", "w_gla_o", "w_out", "w_router_g",
                                "b_router_g", "w_router_e", "b_router_e", "w1", "w3", "w2", "w_ada_f", "b_ada_f",
                                "g_final", "mem_2", "final_norm_g_2", "ffn1_w_in_2", "ffn1_w_out_2", "w_mix_in_2",
                                "w_mix_out_2", "rwkv_w_up_2", "rwkv_a_up_2", "rwkv_g_up_2", "xattn_w_q_2",
                                "xattn_w_kv_2", "xattn_w_o_2", "ffn2_w_in_2", "ffn2_w_out_2")}
    arrays["cols1"] = np.concatenate(parts, axis=1)
    arrays["cols2"] = np.concatenate([tiles(i[second[n]].reshape(DEPTH_2, -1)) for n in C2], axis=2)
    arrays["rel_bias"] = i["rel_bias_2"].T
    arrays["const_tiles"] = const_tiles()
    arrays["bucket_onehot"] = bucket_onehot()
    nc = bacc.Bacc("TRN2", target_bir_lowering=False, num_devices=1)
    arrays = {n: np.ascontiguousarray(v) for n, v in arrays.items()}
    aps = {n: nc.dram_tensor("in_" + n, v.shape, F32, kind="ExternalInput").ap() for n, v in arrays.items()}
    out = nc.dram_tensor("out", (1, SEQ, D), F32, kind="ExternalOutput").ap()
    build(nc, aps, out)
    r = run_bass_kernel_spmd(nc, [{"in_" + n: v for n, v in arrays.items()}], core_ids=[0])
    return r.results[0]["out"]
```

```python
import concourse.bass as bass
from concourse import mybir
from contextlib import ExitStack
import numpy as np

F32 = mybir.dt.float32
ALU = mybir.AluOpType
ACT = mybir.ActivationFunctionType
AX = mybir.AxisListType

P = 128
SEQ = 256
D = 1024
KD = D // P
NT = SEQ // P
SLOTS = 4
SLOT = 4096
EPS = 1e-6
CAP = 64

CONV_DIM, CONV_WIDTH = 512, 31
GH, GDK, GDV, LOWRANK, TAU = 4, 128, 256, 16, 16.0
NG, EPG, NE, DE = 4, 8, 32, 512
DEPTH_2 = 2
W = 512
HD = 64
NH = 8
RB = 32
XH, XHD = 4, 256
D_FF = 2816
LNX_EPS = 64e-5
NGRP = D_FF // 256
BIG = 1.0e30
VECTOR_STEPS = 87

EYE = 0
LEV = 1
LEVT = 8
UPPER = 15
UPPER_EQ = 16
HEADS = 17
ONES = 18
DESC = 19
LOWER = 20
NCONST = 21


def const_tiles():
    i, j = np.arange(P)[:, None], np.arange(P)[None, :]
    c = np.zeros((P, NCONST, P), np.float32)
    c[:, EYE] = i == j
    for n in range(7):
        s = 1 << n
        lev = (i // (2 * s) == j // (2 * s)) & (i % (2 * s) < s) & (j % (2 * s) >= s)
        c[:, LEV + n] = lev
        c[:, LEVT + n] = lev.T
    c[:, UPPER] = i < j
    c[:, UPPER_EQ] = i <= j
    c[:, HEADS] = i // HD == j // HD
    c[:, ONES] = 1.0
    c[:, DESC] = P - j
    c[:, LOWER] = i > j
    return c


BUCKET_START = list(range(17)) + [21, 27, 35, 46, 59, 77, 99, 128, 166, 216]
NDIST = 3 * P


def bucket_onehot():
    out = np.zeros((RB, NDIST), np.float32)
    for dist in range(SEQ):
        b = max(n for n, start in enumerate(BUCKET_START) if start <= dist)
        out[b, SEQ - 1 - dist] = 1.0
    return out


C1 = {}
_at = 0
for _name, _n in (("c", 8), ("g_norm1", 8), ("sh1", 8), ("sc1", 8), ("sh2", 8), ("sc2", 8), ("b_dw", 4),
                  ("g_conv_ln", 4), ("b_conv_ln", 4), ("b_conv_pw", 8), ("b_a2", 4), ("g_gla_norm", 8),
                  ("g_norm2", 8), ("w_dw", 4 * CONV_WIDTH)):
    C1[_name] = (_at, _at + _n)
    _at += _n
NC1 = _at
C2 = {}
_at = 0
for _name, _n in (("ffn1_g", 8), ("mix_g", 8), ("mu", 14), ("w0", 4), ("a0", 4), ("k_k", 4), ("k_a", 4),
                  ("r_k", 4), ("ln_g", 4), ("ln_b", 4), ("xattn_g", 8), ("mem_g", 8), ("ffn2_g", 8)):
    C2[_name] = (_at, _at + _n)
    _at += _n
NC2 = _at
def column(t, spec, name):
    a, b = spec[name]
    return t[:, a:b]


def piece(j, base=(0,) * SLOTS, turn=0):
    return j % SLOTS, base[j % SLOTS] + j // SLOTS + turn


PIECES1 = ([("ada", n) for n in range(4)] + [("in", 0), ("ada", 4), ("in", 1), ("ada", 5)]
           + [("in", n) for n in range(2, 8)]
           + [("ada", 6), ("in", 8), ("ada", 7), ("in", 9), ("ada", 8), ("ada", 9), ("in", 10), ("ada", 10),
              ("ada", 11), ("in", 11), ("ada", 12), ("ada", 13), ("pw", 0), ("ada", 14), ("ada", 15),
              ("glao", 0), ("glao", 1), ("out", 0), ("out", 1)])
J1 = {key: j for j, key in enumerate(PIECES1)}
J_MOE = len(PIECES1)
N36 = NG + NE
COL_A1 = 2 * CONV_DIM + 2 * GH * GDK + 2 * GH * GDV
COL_GATES = COL_A1 + LOWRANK
PROJ_COLS = [512 * n for n in range(8)] + [COL_GATES + 512 * n for n in range(4)]
U_BLOCK2 = [sum(1 for j in range(J_MOE + 3 * NE) if j % SLOTS == s) for s in range(SLOTS)]


def expert_index(e, m):
    return 6 * (e // 2) + (4 + e % 2 if m == 2 else 2 * (e % 2) + m)


def expert_matrix(p):
    e2, q = divmod(p, 6)
    return (2 * e2 + q - 4, 2) if q >= 4 else (2 * e2 + q // 2, q % 2)


def build(nc, a, out):
    ctx = ExitStack()
    with ctx:
        def sem(name):
            return ctx.enter_context(nc.semaphore(name))

        def sb(name, shape, where=None):
            return (where or ctx).enter_context(nc.sbuf_tensor(name, [P] + shape, F32))

        bank = [ctx.enter_context(nc.psum_tensor(f"bank{n}", [P, 512], F32)) for n in range(8)]

        x = sb("x", [NT, D])
        xT = sb("xT", [KD, SEQ])
        xs = sb("xs", [NT, D])
        ring = sb("ring", [SLOTS, SLOT])
        K = sb("K", [NCONST, P])
        neghalf = sb("neghalf", [8])
        ss = sb("ss", [8])
        ms = sb("ms", [8])
        rstd = sb("rstd", [8])
        eye = K[:, EYE, :]
        ones = K[:, ONES, :]

        w_full = [sem(f"w_full{n}") for n in range(SLOTS)]
        consts_loaded = sem("consts_loaded")
        x_loaded = sem("x_loaded")
        rows_loaded = sem("rows_loaded")
        filled = sem("filled")
        x_ready = sem("x_ready")
        ss_ready = sem("ss_ready")
        ms_ready = sem("ms_ready")
        rstd_ready = sem("rstd_ready")
        xs_act = sem("xs_act")
        xs_dve = sem("xs_dve")
        tr_full = sem("tr_full")
        xT_act = sem("xT_act")
        xT_dve = sem("xT_dve")
        dve_steps = sem("dve_steps")
        act_steps = sem("act_steps")
        out_stored = sem("out_stored")
        sp_passed = sem("sp_passed")
        pool_passed = sem("pool_passed")

        def flat(t):
            return t.rearrange("p a b -> p (a b)")

        def slot_w(s, k, n):
            return ring[:, s, 0:k * n].rearrange("p (k n) -> p k n", k=k)

        class Steps:

            def __init__(self, eng, s):
                self.eng, self.s, self.base, self.n = eng, s, 0, 0

            def __call__(self, ins):
                ins.then_inc(self.s, 1)
                self.n += 1

            def sync(self, back=0):
                self.eng.wait_ge(self.s, self.base + self.n - back)

            def loop(self, count, per, start=0):
                outer = self.base + self.n
                with self.eng.Fori(0, count) as i:
                    self.base, self.n = outer + i * per, 0
                    yield i
                    assert self.n == per, (self.n, per)
                self.base, self.n = outer + count * per, 0

        def norm_sums(act, n, src=None, ready=None):
            src = x if src is None else src
            for t in range(NT):
                if t == 1 and ready is not None:
                    act.wait_ge(x_ready, ready)
                last = nc.scalar.activation(xs[:, t, :], src[:, t, :], ACT.Square, accum_out=ss[:, t:t + 1])
            last.then_inc(ss_ready, 1)
            act.wait_ge(rstd_ready, n + 1)
            nc.scalar.activation(xs[:, 0, :], src[:, 0, :], ACT.Copy, scale=rstd[:, 0:1]).then_inc(xs_act, 1)

        def norm_rstd(pool, n):
            pool.wait_ge(ss_ready, n + 1)
            pool.sem_inc(pool_passed, 1)
            nc.gpsimd.tensor_scalar(ms[:, 0:NT], ss[:, 0:NT], 1.0 / D, EPS, ALU.mult, ALU.add).then_inc(ms_ready, 1)
            pool.wait_ge(ms_ready, n + 1)
            nc.gpsimd.tensor_tensor(rstd[:, 0:NT], ms[:, 0:NT], neghalf[:, 0:NT], ALU.pow).then_inc(rstd_ready, 1)

        def norm_scale(dve, n, src=None):
            src = x if src is None else src
            dve.wait_ge(rstd_ready, n + 1)
            nc.vector.tensor_scalar(xs[:, 1, :], src[:, 1, :], rstd[:, 1:2], None, ALU.mult).then_inc(xs_dve, 1)

        def transposes(pe, q, src):
            for b in range(KD // 2):
                for k in (2 * b, 2 * b + 1):
                    for t in range(NT):
                        last = nc.tensor.transpose(bank[b][:, (k % 2) * SEQ + t * P:(k % 2) * SEQ + (t + 1) * P],
                                                   src[:, t, k * P:(k + 1) * P], eye)
                last.then_inc(tr_full, 1)

        def norm_transposes(pe, n, q):
            pe.wait_ge(xs_act, n + 1)
            pe.wait_ge(xs_dve, n + 1)
            transposes(pe, q, xs)

        def tr_bank(k):
            return bank[k // 2][:, (k % 2) * SEQ:(k % 2 + 1) * SEQ]

        def xT_by_act(act, q, scale, bias=None, dst=None):
            dst = xT if dst is None else dst
            for k in (0, 1, 4, 5):
                act.wait_ge(tr_full, 4 * q + k // 2 + 1)
                if bias is None:
                    last = nc.scalar.activation(dst[:, k, :], tr_bank(k), ACT.Copy, scale=scale[:, k:k + 1])
                else:
                    last = nc.scalar.activation(dst[:, k, :], tr_bank(k), ACT.Identity, scale=scale[:, k:k + 1],
                                                bias=bias[:, k:k + 1])
            last.then_inc(xT_act, 1)

        def xT_by_dve(dve, q, scale, bias=None, dst=None):
            dst = xT if dst is None else dst
            for k in (2, 3, 6, 7):
                dve.wait_ge(tr_full, 4 * q + k // 2 + 1)
                if bias is None:
                    last = nc.vector.tensor_scalar(dst[:, k, :], tr_bank(k), scale[:, k:k + 1], None, ALU.mult)
                else:
                    last = nc.vector.tensor_scalar(dst[:, k, :], tr_bank(k), scale[:, k:k + 1], bias[:, k:k + 1],
                                                   ALU.mult, ALU.add)
            last.then_inc(xT_dve, 1)

        ph1 = ExitStack()
        ones256 = sb("ones256", [SEQ], ph1)
        cols = sb("cols", [NC1], ph1)
        c_act = sb("c_act", [KD], ph1)
        mcol = sb("mcol", [4, KD], ph1)
        acc = sb("acc", [2, 512], ph1)
        rows = sb("rows", [4, D], ph1)
        ga1_row, ga2_row, shf_row, scf_row = (rows[:, n, :] for n in range(4))
        brow = sb("brow", [N36], ph1)
        wr = sb("wr", [KD, N36], ph1)

        mix = ExitStack()
        wa1 = sb("wa1", [KD, LOWRANK], mix)
        wa2 = sb("wa2", [512], mix)
        zpad = sb("zpad", [4, CONV_WIDTH - 1 + SEQ], mix)
        cz = sb("cz", [4, SEQ], mix)
        qT = sb("qT", [GH, SEQ], mix)
        kT = sb("kT", [GH, SEQ], mix)
        cum = sb("cum", [GH, SEQ], mix)
        v = sb("v", [NT, D], mix)
        srT = sb("srT", [KD, SEQ], mix)
        sgT = sb("sgT", [2 * KD, SEQ], mix)
        dec = sb("dec", [GH, SEQ], mix)
        QS = sb("QS", [2, GH, SEQ], mix)
        KS = sb("KS", [2, GH, SEQ], mix)
        AT = sb("AT", [3, GH * P], mix)
        tmp = sb("tmp", [2, 512], mix)
        a1T = tmp[:, 1, 0:SEQ]
        mix.close()

        moe = ExitStack()
        lg = sb("lg", [NT, N36], moe)
        rt = sb("rt", [NT, 128], moe)
        comb = sb("comb", [NT, NE + 2], moe)
        y = sb("y", [NT, D], moe)
        gf_row = sb("gf_row", [D], moe)
        hT = sb("hT", [2, 512], moe)
        sg = sb("sg", [2, 512], moe)
        sel = sb("sel", [NT, NE], moe)
        place = sb("place", [NT, NE + 2], moe)
        most = sb("most", [1], moe)
        fits = moe.enter_context(nc.sbuf_tensor("fits", [P, 1], mybir.dt.int32))
        hot = sb("hot", [NT, P], moe)
        whot = sb("whot", [NT, P], moe)
        whotT = sb("whotT", [2, NT * P], moe)
        xg = sb("xg", [KD, P], moe)
        ye = sb("ye", [2, 512], moe)
        moe.close()
        ph1.close()

        c_ready = sem("c_ready")
        ada_acc = sem("ada_acc")
        ada_psum = sem("ada_psum")
        ada_taken = sem("ada_taken")
        mod_ready = sem("mod_ready")
        proj_full = sem("proj_full")
        proj_act = sem("proj_act")
        proj_dve = sem("proj_dve")
        conv_ready = sem("conv_ready")
        ln_psum = sem("ln_psum")
        ln_sq = sem("ln_sq")
        ln_var = sem("ln_var")
        ln_rstd = sem("ln_rstd")
        ln_norm = sem("ln_norm")
        zc_ready = sem("zc_ready")
        y_psum = sem("y_psum")
        y_taken = sem("y_taken")
        soft_ready = sem("soft_ready")
        dist_ready = sem("dist_ready")
        dec_ready = sem("dec_ready")
        qk_ready = sem("qk_ready")
        att_psum = sem("att_psum")
        att_taken = sem("att_taken")
        o_psum = sem("o_psum")
        o_sq = sem("o_sq")
        o_ms = sem("o_ms")
        o_rstd = sem("o_rstd")
        o_normed = sem("o_normed")
        ogT_ready = sem("ogT_ready")
        merged = sem("merged")
        out_psum = sem("out_psum")
        gf_loaded = sem("gf_loaded")
        router_psum = sem("router_psum")
        gap_ready = sem("gap_ready")
        gap_exp = sem("gap_exp")
        hid_up = sem("hid_up")
        hid_silu = sem("hid_silu")
        hid_h = sem("hid_h")
        hid_down = sem("hid_down")
        moe_taken = sem("moe_taken")
        sel_ready = sem("sel_ready")
        place_psum = sem("place_psum")
        fits_ready = sem("fits_ready")
        hot_ready = sem("hot_ready")
        whotT_psum = sem("whotT_psum")
        whotT_ready = sem("whotT_ready")
        xg_psum = sem("xg_psum")
        xg_act = sem("xg_act")
        xg_dve = sem("xg_dve")
        ye_act = sem("ye_act")
        ye_dve = sem("ye_dve")
        scattered = sem("scattered")
        branch_steps = sem("branch_steps")

        LEVELS = 8

        G_A, G_GT, G_Q, G_K, G_A1, G_DEC, G_V, G_R, G_GATES, G_N = 0, 2, 4, 6, 8, 9, 11, 15, 19, 27
        NB = 5
        BY_DVE = [0, 1, 6, 7, 9, 10]
        BY_ACT = [g for g in range(G_N) if g not in BY_DVE]

        def taken(pe, g):
            if g in BY_DVE:
                pe.wait_ge(proj_dve, BY_DVE.index(g) + 1)
            else:
                pe.wait_ge(proj_act, BY_ACT.index(g) + 1)
        ph2 = ExitStack()
        lc = sb("lc", [NC2], ph2)
        memT = sb("memT", [KD, SEQ], ph2)
        biasT = sb("biasT", [NH, SEQ], ph2)
        lora = sb("lora", [W], ph2)
        gup = sb("gup", [W], ph2)

        pre = ExitStack()
        below = sb("below", [9728], pre)
        mem = sb("mem", [NT, D], pre)
        relT = sb("relT", [NH], pre)
        onehot = sb("onehot", [NDIST], pre)
        bydist = sb("bydist", [NDIST], pre)
        gf2_row = sb("gf2_row", [D], pre)
        pre.close()

        ffn = ExitStack()
        fh = sb("fh", [2, 512], ffn)
        fs = sb("fs", [2, 512], ffn)
        ffn.close()

        mix2 = ExitStack()
        pT = sb("pT", [14, SEQ], mix2)
        lw = sb("lw", [4, SEQ], mix2)
        cw = sb("cw", [4, SEQ], mix2)
        aT = sb("aT", [4, SEQ], mix2)
        kk = sb("kk", [4, SEQ], mix2)
        R2 = sb("R2", [4, P], mix2)
        KK2 = sb("KK2", [4, P], mix2)
        bon = sb("bon", [4, SEQ], mix2)
        gT = sb("gT", [4, SEQ], mix2)
        vt = sb("vt", [NT, W], mix2)
        small = sb("small", [48], mix2)
        moba = ExitStack()
        qm = sb("qm", [4, SEQ], moba)
        km = sb("km", [4, SEQ], moba)
        vm = sb("vm", [NT, W], moba)
        sm = sb("sm", [2, 384], moba)
        pmT = sb("pmT", [2, 384], moba)
        gm = sb("gm", [KD, SEQ], moba)
        k_out = sb("k_out", [KD, SEQ], moba)
        v_out = sb("v_out", [NT, D], moba)
        moba.close()
        mats = ExitStack()
        Mrb = sb("Mrb", [3, 512], mats)
        Mrk = sb("Mrk", [3, 512], mats)
        Luk = sb("Luk", [3, 512], mats)
        Noff = sb("Noff", [512], mats)
        Nd = sb("Nd", [2, 512], mats)
        Lt = sb("Lt", [2, 512], mats)
        X = sb("X", [2, 512], mats)
        Y = sb("Y", [2, 512], mats)
        Pm = sb("Pm", [2, 512], mats)
        mats.close()
        mix2.close()
        U = lw[:, :, :].rearrange("p a b -> p (a b)").rearrange("p (c n) -> p c n", c=2)
        E1, E3 = xs[:, 0, :], xs[:, 1, :]

        xat = ExitStack()
        qx = sb("qx", [KD, SEQ], xat)
        kx = sb("kx", [KD, SEQ], xat)
        vx = sb("vx", [NT, D], xat)
        sx = sb("sx", [2, 512], xat)
        pxT = sb("pxT", [2, 512], xat)
        xsm = sb("xsm", [16], xat)
        xat.close()
        ph2.close()
        k_dram = nc.dram_tensor("cross_keys", (P, KD * SEQ), F32)
        v_dram = nc.dram_tensor("cross_values", (P, NT * D), F32)
        bias_dram = nc.dram_tensor("bias_by_distance", (NH, P, NDIST), F32)

        up_full = [sem(f"up_full{n}") for n in range(SLOTS)]
        mem_loaded = sem("mem_loaded")
        x_first = sem("x_first")
        ffn_out = sem("ffn_out")
        rel_loaded = sem("rel_loaded")
        lc_loaded = sem("lc_loaded")
        bd_psum = sem("bd_psum")
        bd_ready = sem("bd_ready")
        bd_stored = sem("bd_stored")
        bias_loaded = sem("bias_loaded")
        mp_full = sem("mp_full")
        mp_act = sem("mp_act")
        shifted = sem("shifted")
        lo_ready = sem("lo_ready")
        lora_psum = sem("lora_psum")
        lora_act = sem("lora_act")
        kk_sq = sem("kk_sq")
        kk_psum = sem("kk_psum")
        kk_ss = sem("kk_ss")
        kk_rs = sem("kk_rs")
        rk_ready = sem("rk_ready")
        rk_psum = sem("rk_psum")
        dec2_ready = sem("dec2_ready")
        e_ready = sem("e_ready")
        vt_psum = sem("vt_psum")
        vt_ready = sem("vt_ready")
        fac_ready = sem("fac_ready")
        mb_s = sem("mb_s")
        mb_sb = sem("mb_sb")
        mb_max = sem("mb_max")
        mb_e = sem("mb_e")
        mb_p = sem("mb_p")
        mb_t = sem("mb_t")
        mb_tc = sem("mb_tc")
        mb_o = sem("mb_o")
        mb_oc = sem("mb_oc")
        mat_full = sem("mat_full")
        mat_dve = sem("mat_dve")
        mat_act = sem("mat_act")
        inv_init = sem("inv_init")
        inv_p = sem("inv_p")
        inv_pm = sem("inv_pm")
        inv_x = sem("inv_x")
        inv_y = sem("inv_y")
        inv_xs = sem("inv_xs")
        inv_ys = sem("inv_ys")
        u_psum = sem("u_psum")
        u_taken = sem("u_taken")
        yy_psum = sem("yy_psum")
        yy_taken = sem("yy_taken")
        gn_psum = sem("gn_psum")
        gn_xc = sem("gn_xc")
        gn_sq = sem("gn_sq")
        gn_var = sem("gn_var")
        gn_rs = sem("gn_rs")
        gn_norm = sem("gn_norm")
        gn_aff = sem("gn_aff")
        bonus_ready = sem("bonus_ready")
        ycat = sem("ycat")
        mo_psum = sem("mo_psum")
        gm_ready = sem("gm_ready")
        kv_psum = sem("kv_psum")
        kv_act = sem("kv_act")
        k_stored = sem("k_stored")
        v_stored = sem("v_stored")
        kv_loaded = sem("kv_loaded")
        xq_psum = sem("xq_psum")
        xq_act = sem("xq_act")
        xa_s = sem("xa_s")
        xa_max = sem("xa_max")
        xa_e = sem("xa_e")
        xa_p = sem("xa_p")
        xa_t = sem("xa_t")
        xa_tc = sem("xa_tc")
        xa_o = sem("xa_o")
        xa_oc = sem("xa_oc")
        xo_psum = sem("xo_psum")
        gf2_loaded = sem("gf2_loaded")

        def wait_piece(eng, j, base=(0,) * SLOTS, turn=0):
            s, u = piece(j, base, turn)
            eng.wait_ge(w_full[s], (u + 1) * 16)
            return s

        def grouped(g):
            n = {**{g: (g // 2, g % 2) for g in range(8)}, **{11: (4, 0), 12: (4, 1), 13: (5, 0), 14: (5, 1)},
                 **{15 + i: (6 + i // 2, i % 2) for i in range(12)}}[g]
            return n

        def level_views(t, s):
            return t.rearrange("p h (b s) -> p (h b) s", s=2 * s)

        def sync1(sp):
            def load(j, src, k, n, base=(0,) * SLOTS, turn=0):
                s, u = piece(j, base, turn)
                sp.dma_start(slot_w(s, k, n), src).then_inc(w_full[s], 16)

            def read(key):
                kind, n = key
                if kind == "ada":
                    sp.wait_ge(ada_acc, n + 1)
                elif kind == "in":
                    sp.wait_ge(proj_full, {4: 13, 5: 15}.get(n, 2 * n + 2 if n < 4 else G_R + 2 * (n - 6) + 2))
                elif kind == "pw":
                    sp.wait_ge(y_psum, 4)
                elif kind == "glao":
                    sp.wait_ge(y_psum, 4 + 2 * (n + 1))
                else:
                    sp.wait_ge(out_psum, 2 * (n + 1))

            sp.dma_start(x[:, :, :], a["x"][0].rearrange("(t p) d -> p t d", p=P)).then_inc(x_loaded, 16)
            sp.dma_start(cols[:, :], a["cols1"]).then_inc(consts_loaded, 16)
            sp.dma_start(K[:, :, :], a["const_tiles"]).then_inc(consts_loaded, 16)
            srcs = {}
            for n in range(12):
                srcs["ada", n] = a["w_ada"][0][:, n * 512:(n + 1) * 512]
                srcs["in", n] = a["w_in"][0][:, PROJ_COLS[n]:PROJ_COLS[n] + 512]
            for n in range(4):
                srcs["ada", 12 + n] = a["w_ada_f"][:, n * 512:(n + 1) * 512]
            for n in range(2):
                srcs["glao", n] = a["w_gla_o"][0][:, n * 512:(n + 1) * 512]
                srcs["out", n] = a["w_out"][0][:, n * 512:(n + 1) * 512]
            for j, key in enumerate(PIECES1):
                if j >= SLOTS:
                    read(PIECES1[j - SLOTS])
                if key[0] == "pw":
                    load(j, a["w_conv_pw"][0].rearrange("(k p) n -> p k n", p=P), CONV_DIM // P, D)
                else:
                    load(j, srcs[key].rearrange("(k p) n -> p k n", p=P), KD, 512)
                if j == 3:
                    sp.dma_start(wa1[:, :, :], a["w_in"][0][:, COL_A1:COL_A1 + LOWRANK].rearrange(
                        "(k p) n -> p k n", p=P)).then_inc(rows_loaded, 16)
                    sp.dma_start(wa2[0:LOWRANK, :], a["w_a2"][0]).then_inc(rows_loaded, 16)
                    sp.dma_start(wr[:, :, 0:NG], a["w_router_g"][0].rearrange(
                        "(k p) n -> p k n", p=P)).then_inc(rows_loaded, 16)
                    sp.dma_start(wr[:, :, NG:N36], a["w_router_e"][0].rearrange(
                        "(k p) n -> p k n", p=P)).then_inc(rows_loaded, 16)
                    sp.dma_start(brow[:, 0:NG], a["b_router_g"][0].partition_broadcast(P)).then_inc(rows_loaded, 16)
                    sp.dma_start(brow[:, NG:N36], a["b_router_e"][0].partition_broadcast(P)).then_inc(rows_loaded, 16)
                    sp.dma_start(ga1_row, a["b_ada"][0][2 * D:3 * D].partition_broadcast(P)).then_inc(rows_loaded, 16)
                    sp.dma_start(ga2_row, a["b_ada"][0][5 * D:6 * D].partition_broadcast(P)).then_inc(rows_loaded, 16)
                    sp.dma_start(rows[:, 2:4, :], a["b_ada_f"].rearrange("(r d) -> r d", r=2).partition_broadcast(P)
                                 ).then_inc(rows_loaded, 16)
            for key in PIECES1[-SLOTS:]:
                read(key)
            def expert_piece(i, p):
                e, m = expert_matrix(p)
                src, k, n = (("w1", KD, DE), ("w3", KD, DE), ("w2", DE // P, D))[m]
                load(J_MOE + p, a[src][0, i * 4 + e].rearrange("(k p) n -> p k n", p=P), k, n, turn=i * 3)

            def expert_read(i, p):
                e, m = expert_matrix(p)
                sp.wait_ge(hid_down if m == 2 else hid_up, i * 8 + 2 * e + 2)

            for p in range(SLOTS):
                expert_piece(0, p)
            with sp.Fori(0, NE // 4 - 1) as i:
                for p in range(SLOTS, 12 + SLOTS):
                    expert_read(i, p - SLOTS)
                    expert_piece(i + p // 12, p % 12)
            for p in range(SLOTS, 12):
                expert_read(NE // 4 - 1, p - SLOTS)
                expert_piece(NE // 4 - 1, p)
        ROWS = 16 * 9

        def pool1(pool):
            nc.gpsimd.memset(ones256[:, :], 1.0).then_inc(filled, 1)
            nc.gpsimd.memset(neghalf[:, :], -0.5).then_inc(filled, 1)
            nc.gpsimd.memset(zpad[:, :, 0:CONV_WIDTH - 1], 0.0).then_inc(filled, 1)
            for t in (QS, KS):
                nc.gpsimd.memset(t[:, :, :, :], 0.0).then_inc(filled, 1)
            pool.wait_ge(filled, 5)
            norm_rstd(pool, 0)
            pool.wait_ge(o_sq, 1)
            nc.gpsimd.tensor_scalar(ms[:, :], ss[:, :], 1.0 / GDV, EPS, ALU.mult, ALU.add).then_inc(o_ms, 1)
            pool.wait_ge(o_ms, 1)
            nc.gpsimd.tensor_tensor(rstd[:, :], ms[:, :], neghalf[:, 0:8], ALU.pow).then_inc(o_rstd, 1)
            norm_rstd(pool, 1)

        def tensor1(pe):
            pe.wait_ge(consts_loaded, 32)

            def ada_mm(i):
                pe.wait_ge(ada_acc, i + 1)
                if i:
                    pe.wait_ge(ada_taken, i)
                if i < 4 or 6 <= i < 10:
                    for c in range(4):
                        last = nc.tensor.matmul(bank[5][:, c:c + 1], acc[:, i % 2, c * P:(c + 1) * P], ones[:, 0:1],
                                                start=True, stop=True)
                else:
                    last = nc.tensor.matmul(bank[5][:, :], ones, acc[:, i % 2, :], start=True, stop=True)
                last.then_inc(ada_psum, 1)

            norm_transposes(pe, 0, 0)
            for i in range(4):
                ada_mm(i)
            pe.wait_ge(xT_act, 1)
            pe.wait_ge(xT_dve, 1)

            def project(g):
                if g >= NB:
                    taken(pe, g - NB)
                b = bank[g % NB]
                if g == G_A1:
                    pe.wait_ge(rows_loaded, ROWS)
                    for k in range(KD):
                        last = nc.tensor.matmul(b[0:LOWRANK, 0:SEQ], wa1[:, k, :], xT[:, k, :],
                                                start=(k == 0), stop=(k == KD - 1))
                elif g in (G_DEC, G_DEC + 1):
                    pe.wait_ge(proj_act, BY_ACT.index(G_A1) + 1)
                    for c in range(2):
                        h = 2 * (g - G_DEC) + c
                        last = nc.tensor.matmul(b[:, c * SEQ:(c + 1) * SEQ], wa2[0:LOWRANK, h * P:(h + 1) * P],
                                                a1T[0:LOWRANK, :], start=True, stop=True)
                else:
                    n, half = grouped(g)
                    j = J1["in", n]
                    s = wait_piece(pe, j)
                    w = slot_w(s, KD, 512)
                    if G_V <= g < G_R:
                        for k in range(KD):
                            last = nc.tensor.matmul(b[:, :], xT[:, k, half * P:(half + 1) * P], w[:, k, :],
                                                    start=(k == 0), stop=(k == KD - 1))
                    else:
                        for c in range(2):
                            m = 2 * half + c
                            for k in range(KD):
                                last = nc.tensor.matmul(b[:, c * SEQ:(c + 1) * SEQ], w[:, k, m * P:(m + 1) * P],
                                                        xT[:, k, :], start=(k == 0), stop=(k == KD - 1))
                last.then_inc(proj_full, 1)

            def level(l):
                if l:
                    pe.wait_ge(qk_ready, l)
                    pe.wait_ge(att_taken, l)
                else:
                    pe.wait_ge(proj_dve, 4)
                    pe.wait_ge(ln_var, 1)
                q, k = (qT, kT) if l == 0 else (QS[:, l % 2], KS[:, l % 2])
                if l < LEVELS:
                    for ch in range(2):
                        for h in range(GH):
                            last = nc.tensor.matmul(bank[6 + ch][:, h * P:(h + 1) * P], k[:, h, ch * P:(ch + 1) * P],
                                                    q[:, h, ch * P:(ch + 1) * P], start=True, stop=True)
                else:
                    for h in range(GH):
                        last = nc.tensor.matmul(bank[6][:, h * P:(h + 1) * P], k[:, h, 0:P], q[:, h, P:SEQ],
                                                start=True, stop=True)
                last.then_inc(att_psum, 1)

            after = {1: [("ada", 4)], 3: [("ada", 5)], 15: [("ln", 0)], 16: [("ln", 1)], 18: [("ada", 6)],
                     19: [("level", 0)], **{19 + l: [("ada", 6 + l), ("level", l)] for l in range(1, 8)}}
            after[26] += [("level", 8)]
            for g in range(G_N):
                project(g)
                for kind, n in after.get(g, ()):
                    if kind == "ada":
                        ada_mm(n)
                    elif kind == "level":
                        level(n)
                    else:
                        if n == 0:
                            pe.wait_ge(conv_ready, 1)
                        else:
                            pe.wait_ge(ln_sq, 1)
                        src = cz if n == 0 else dec
                        for k in range(4):
                            last = nc.tensor.matmul(bank[6 + n][:, 0:SEQ], ones, src[:, k, :],
                                                    start=(k == 0), stop=(k == 3))
                        last.then_inc(ln_psum, 1)

            s = wait_piece(pe, J1["pw", 0])
            w = slot_w(s, 4, D)
            pe.wait_ge(zc_ready, 1)
            pe.wait_ge(proj_act, len(BY_ACT))
            for g in range(4):
                for c in range(2):
                    m = 2 * g + c
                    for k in range(4):
                        last = nc.tensor.matmul(bank[g][:, c * SEQ:(c + 1) * SEQ], w[:, k, m * P:(m + 1) * P],
                                                cz[:, k, :], start=(k == 0), stop=(k == 3))
                last.then_inc(y_psum, 1)
            pe.wait_ge(att_taken, LEVELS + 1)
            pe.wait_ge(ada_taken, 14)
            for g in range(4):
                t, hp = g // 2, g % 2
                for c in range(2):
                    h = 2 * hp + c
                    o = bank[4 + g][:, c * GDV:(c + 1) * GDV]
                    vs = slice(h * GDV, (h + 1) * GDV)
                    hs = slice(h * P, (h + 1) * P)
                    if t == 0:
                        last = nc.tensor.matmul(o, AT[:, 0, hs], v[:, 0, vs], start=True, stop=True)
                    else:
                        nc.tensor.matmul(o, AT[:, 2, hs], v[:, 0, vs], start=True, stop=False)
                        last = nc.tensor.matmul(o, AT[:, 1, hs], v[:, 1, vs], start=False, stop=True)
                last.then_inc(o_psum, 1)
            pe.wait_ge(o_normed, 2)
            pe.wait_ge(y_taken, 4)
            transposes(pe, 1, xs)
            pe.wait_ge(ogT_ready, 1)
            for g in range(4):
                s = wait_piece(pe, J1["glao", g // 2])
                w = slot_w(s, KD, 512)
                for c in range(2):
                    m = 2 * (g % 2) + c
                    for k in range(KD):
                        last = nc.tensor.matmul(bank[4 + g][:, c * SEQ:(c + 1) * SEQ], w[:, k, m * P:(m + 1) * P],
                                                xT[:, k, :], start=(k == 0), stop=(k == KD - 1))
                last.then_inc(y_psum, 1)
            pe.wait_ge(merged, 1)
            for half in range(2):
                s = wait_piece(pe, J1["out", half])
                w = slot_w(s, KD, 512)
                for t in range(NT):
                    for k in range(KD):
                        last = nc.tensor.matmul(bank[2 * half + t][:, :], sgT[:, k, t * P:(t + 1) * P], w[:, k, :],
                                                start=(k == 0), stop=(k == KD - 1))
                    last.then_inc(out_psum, 1)
            for i in (14, 15):
                ada_mm(i)

        def scalar1(act):
            st = Steps(act, act_steps)
            act.wait_ge(x_loaded, 16)
            norm_sums(act, 0)
            act.wait_ge(consts_loaded, 32)
            nc.scalar.activation(c_act[:, :], column(cols, C1, "c"), ACT.Silu).then_inc(c_ready, 1)
            act.wait_ge(mod_ready, 1)
            xT_by_act(act, 0, mcol[:, 1, :], mcol[:, 0, :])

            def full(g):
                act.wait_ge(proj_full, g + 1)
                return bank[g % NB]

            for p in range(2):
                b = full(G_GT + p)
                nc.scalar.activation(flat(cz[:, 2 * p:2 * p + 2, :]), b[:, :], ACT.Sigmoid).then_inc(proj_act, 1)
            for p in range(2):
                b = full(G_Q + p)
                nc.scalar.activation(flat(qT[:, 2 * p:2 * p + 2, :]), b[:, :], ACT.Copy,
                                     scale=GDK ** -0.5).then_inc(proj_act, 1)
            b = full(G_A1)
            nc.scalar.activation(a1T[0:LOWRANK, :], b[0:LOWRANK, 0:SEQ], ACT.Copy).then_inc(proj_act, 1)
            act.wait_ge(proj_dve, 6)
            act.wait_ge(filled, 5)
            z, t = flat(dec[:, :, :]), flat(QS[:, 0, :, :])
            st(nc.scalar.activation(t, z, ACT.Abs))
            st.sync()
            st(nc.scalar.activation(t, t, ACT.Exp, scale=-1.0))
            st.sync()
            nc.scalar.activation(t, t, ACT.Ln, bias=1.0).then_inc(soft_ready, 1)
            for g in range(G_V, G_R):
                b = full(g)
                half = (g - G_V) // 2
                nc.scalar.activation(v[:, (g - G_V) % 2, half * 512:(half + 1) * 512], b[:, :],
                                     ACT.Copy).then_inc(proj_act, 1)
            for g in range(G_R, G_GATES):
                b = full(g)
                m = 2 * (g - G_R)
                nc.scalar.activation(flat(srT[:, m:m + 2, :]), b[:, :], ACT.Silu).then_inc(proj_act, 1)
                if g == G_R + 1:
                    act.wait_ge(ln_var, 1)
                    nc.scalar.activation(tmp[:, 1, 0:SEQ], tmp[:, 0, 0:SEQ], ACT.Sqrt).then_inc(ln_rstd, 1)
                if g == G_R + 2:
                    act.wait_ge(ln_norm, 1)
                    for k in range(4):
                        last = nc.scalar.activation(cz[:, k, :], cz[:, k, :], ACT.Silu,
                                                    scale=column(cols, C1, "g_conv_ln")[:, k:k + 1],
                                                    bias=column(cols, C1, "b_conv_ln")[:, k:k + 1])
                    last.then_inc(zc_ready, 1)
            for g in range(G_GATES, G_N):
                b = full(g)
                m = 2 * (g - G_GATES)
                nc.scalar.activation(flat(sgT[:, m:m + 2, :]), b[:, :], ACT.Sigmoid).then_inc(proj_act, 1)
                l = g - G_GATES + 1
                act.wait_ge(dist_ready, l)
                nc.scalar.activation(flat(dec[:, :, :]), flat(dec[:, :, :]), ACT.Exp,
                                     scale=1.0 / TAU).then_inc(dec_ready, 1)
            for g in range(4):
                act.wait_ge(o_psum, g + 1)
                for c in range(2):
                    last = nc.scalar.activation(xs[:, g // 2, (2 * (g % 2) + c) * GDV:(2 * (g % 2) + c + 1) * GDV],
                                                bank[4 + g][:, c * GDV:(c + 1) * GDV], ACT.Square,
                                                accum_out=ss[:, 2 * g + c:2 * g + c + 1])
            last.then_inc(o_sq, 1)
            act.wait_ge(o_rstd, 1)
            for h in range(GH):
                last = nc.scalar.activation(xs[:, 0, h * GDV:(h + 1) * GDV],
                                            bank[4 + h // 2][:, (h % 2) * GDV:(h % 2 + 1) * GDV], ACT.Copy,
                                            scale=rstd[:, h:h + 1])
            last.then_inc(o_normed, 1)
            act.wait_ge(x_ready, 1)
            norm_sums(act, 1)
            act.wait_ge(mod_ready, 2)
            xT_by_act(act, 2, mcol[:, 3, :], mcol[:, 2, :])
            return st

        def vector1(dve):
            st = Steps(dve, dve_steps)

            def ada_sum(i):
                s = wait_piece(dve, J1["ada", i])
                w = slot_w(s, KD, 512)
                if i >= 2:
                    dve.wait_ge(ada_psum, i - 1)
                st(nc.vector.tensor_scalar(acc[:, i % 2, :], w[:, 0, :], c_act[:, 0:1], None, ALU.mult))
                for k in range(1, KD):
                    st.sync()
                    ins = nc.vector.scalar_tensor_tensor(out=acc[:, i % 2, :], in0=w[:, k, :],
                                                         scalar=c_act[:, k:k + 1], in1=acc[:, i % 2, :],
                                                         op0=ALU.mult, op1=ALU.add)
                    if k < KD - 1:
                        st(ins)
                    else:
                        ins.then_inc(ada_acc, 1)
                dve.wait_ge(ada_acc, i + 1)

            def ada_take(i):
                dve.wait_ge(ada_psum, i + 1)
                if i < 4 or 6 <= i < 10:
                    n = i if i < 4 else i - 2
                    nc.vector.tensor_copy(mcol[:, n // 2, (n % 2) * 4:(n % 2) * 4 + 4],
                                          bank[5][:, 0:4]).then_inc(ada_taken, 1)
                else:
                    n = {4: 0, 5: 1, 10: 2, 11: 3}.get(i, i - 8)
                    r = rows[:, n // 2, (n % 2) * 512:(n % 2 + 1) * 512]
                    dve.wait_ge(rows_loaded, ROWS)
                    nc.vector.tensor_tensor(r, bank[5][:, :], r, ALU.add).then_inc(ada_taken, 1)

            def modulation(n, shift, scale, gain):
                i = 2 * n
                st(nc.vector.tensor_tensor(mcol[:, i, :], mcol[:, i, :], column(cols, C1, shift), ALU.add))
                st(nc.vector.scalar_tensor_tensor(out=mcol[:, i + 1, :], in0=mcol[:, i + 1, :], scalar=1.0,
                                                  in1=column(cols, C1, scale), op0=ALU.add, op1=ALU.add))
                st.sync()
                nc.vector.tensor_tensor(mcol[:, i + 1, :], mcol[:, i + 1, :], column(cols, C1, gain),
                                        ALU.mult).then_inc(mod_ready, 1)
                dve.wait_ge(mod_ready, n + 1)

            dve.wait_ge(x_loaded, 16)
            norm_scale(dve, 0)
            dve.wait_ge(consts_loaded, 32)
            dve.wait_ge(c_ready, 1)
            for i in range(4):
                ada_sum(i)
                if i:
                    ada_take(i - 1)
            ada_take(3)
            dve.wait_ge(ada_taken, 4)
            modulation(0, "sh1", "sc1", "g_norm1")
            xT_by_dve(dve, 0, mcol[:, 1, :], mcol[:, 0, :])
            ada_sum(4)
            ada_sum(5)
            dve.wait_ge(filled, 5)
            for p in range(2):
                dve.wait_ge(proj_full, G_A + p + 1)
                dve.wait_ge(proj_act, p + 1)
                nc.vector.tensor_tensor(zpad[:, 2 * p:2 * p + 2, CONV_WIDTH - 1:],
                                        bank[(G_A + p) % NB][:, :].rearrange("p (c t) -> p c t", c=2),
                                        cz[:, 2 * p:2 * p + 2, :], ALU.mult).then_inc(proj_dve, 1)
            wd = column(cols, C1, "w_dw").rearrange("p (k n) -> p k n", k=4)

            def convolve(taps):
                for tap in taps:
                    for k in range(4):
                        src = zpad[:, k, tap:tap + SEQ]
                        if tap == 0:
                            st(nc.vector.tensor_scalar(cz[:, k, :], src, wd[:, k, 0:1],
                                                       column(cols, C1, "b_dw")[:, k:k + 1], ALU.mult, ALU.add))
                        else:
                            st.sync(back=3)
                            ins = nc.vector.scalar_tensor_tensor(out=cz[:, k, :], in0=src,
                                                                 scalar=wd[:, k, tap:tap + 1], in1=cz[:, k, :],
                                                                 op0=ALU.mult, op1=ALU.add)
                            if tap == CONV_WIDTH - 1 and k == 3:
                                ins.then_inc(conv_ready, 1)
                            else:
                                st(ins)

            ada_take(4)
            ada_take(5)
            dve.wait_ge(proj_dve, 2)
            convolve(range(0, 17))
            for p in range(2):
                dve.wait_ge(proj_full, G_K + p + 1)
                nc.vector.tensor_copy(flat(kT[:, 2 * p:2 * p + 2, :]), bank[(G_K + p) % NB][:, :]).then_inc(proj_dve, 1)
            convolve(range(17, 20))
            for p in range(2):
                dve.wait_ge(proj_full, G_DEC + p + 1)
                for c in range(2):
                    h = 2 * p + c
                    last = nc.vector.tensor_scalar(dec[:, h, :], bank[(G_DEC + p) % NB][:, c * SEQ:(c + 1) * SEQ],
                                                   column(cols, C1, "b_a2")[:, h:h + 1], None, ALU.add)
                last.then_inc(proj_dve, 1)
            convolve(range(20, CONV_WIDTH))
            dve.wait_ge(proj_dve, 6)
            dve.wait_ge(soft_ready, 1)
            st(nc.vector.scalar_tensor_tensor(out=flat(dec[:, :, :]), in0=flat(dec[:, :, :]), scalar=0.0,
                                              in1=flat(QS[:, 0, :, :]), op0=ALU.min, op1=ALU.subtract))
            st.sync()
            for h in range(GH):
                st(nc.vector.tensor_tensor_scan(cum[:, h, :], ones256[:, :], dec[:, h, :], 0.0, ALU.mult, ALU.add))
            dve.wait_ge(ln_psum, 1)
            for k in range(4):
                st(nc.vector.scalar_tensor_tensor(out=cz[:, k, :], in0=bank[6][:, 0:SEQ], scalar=-1.0 / CONV_DIM,
                                                  in1=cz[:, k, :], op0=ALU.mult, op1=ALU.add))
            st.sync()
            nc.vector.tensor_tensor(dec[:, :, :], cz[:, :, :], cz[:, :, :], ALU.mult).then_inc(ln_sq, 1)
            dve.wait_ge(ln_psum, 2)
            nc.vector.tensor_scalar(tmp[:, 0, 0:SEQ], bank[7][:, 0:SEQ], 1.0 / CONV_DIM, EPS,
                                    ALU.mult, ALU.add).then_inc(ln_var, 1)
            dve.wait_ge(ln_rstd, 1)
            st(nc.vector.reciprocal(tmp[:, 1, 0:SEQ], tmp[:, 1, 0:SEQ]))
            st.sync()
            for k in range(4):
                last = nc.vector.tensor_tensor(cz[:, k, :], cz[:, k, :], tmp[:, 1, 0:SEQ], ALU.mult)
            last.then_inc(ln_norm, 1)
            dve.wait_ge(ln_norm, 1)

            def distances(l):
                s = 1 << (l - 1)
                c, d = level_views(cum[:, :, :], s), level_views(dec[:, :, :], s)
                nb = GH * SEQ // (2 * s)
                ref = c[:, :, s - 1:s].to_broadcast([P, nb, s])
                st(nc.vector.tensor_tensor(d[:, :, s:2 * s], c[:, :, s:2 * s], ref, ALU.subtract))
                nc.vector.tensor_tensor(d[:, :, 0:s], ref, c[:, :, 0:s], ALU.subtract).then_inc(dist_ready, 1)

            def scaled(l):
                s = 1 << (l - 1)
                d = level_views(dec[:, :, :], s)
                dve.wait_ge(dec_ready, l)
                if l >= 3:
                    dve.wait_ge(att_psum, l - 1)
                q, k = level_views(QS[:, l % 2], s), level_views(KS[:, l % 2], s)
                st(nc.vector.tensor_tensor(q[:, :, s:2 * s], level_views(qT[:, :, :], s)[:, :, s:2 * s],
                                           d[:, :, s:2 * s], ALU.mult))
                st.sync()
                nc.vector.tensor_tensor(k[:, :, 0:s], level_views(kT[:, :, :], s)[:, :, 0:s],
                                        d[:, :, 0:s], ALU.mult).then_inc(qk_ready, 1)
                dve.wait_ge(qk_ready, l)

            def accumulate(l):
                dve.wait_ge(att_psum, l + 1)
                if l == LEVELS:
                    nc.vector.tensor_copy(AT[:, 2, :], bank[6][:, :]).then_inc(att_taken, 1)
                    return
                mask = K[:, EYE if l == 0 else LEV + l - 1, :].unsqueeze(1).to_broadcast([P, GH, P])
                if l:
                    dve.wait_ge(att_taken, l)
                for ch in range(2):
                    ps = bank[6 + ch][:, :].rearrange("p (h t) -> p h t", h=GH)
                    dst = AT[:, ch, :] if l == 0 else tmp[:, ch, :]
                    ins = nc.vector.tensor_tensor(dst.rearrange("p (h t) -> p h t", h=GH), ps, mask, ALU.mult)
                    st(ins) if l or ch == 0 else ins.then_inc(att_taken, 1)
                if l:
                    st.sync()
                    st(nc.vector.tensor_tensor(AT[:, 0, :], AT[:, 0, :], tmp[:, 0, :], ALU.add))
                    nc.vector.tensor_tensor(AT[:, 1, :], AT[:, 1, :], tmp[:, 1, :], ALU.add).then_inc(att_taken, 1)

            for l in range(1, LEVELS + 1):
                distances(l)
                ada_sum(5 + l)
                if l > 1:
                    ada_take(4 + l)
                scaled(l)
                accumulate(l - 1)
            accumulate(LEVELS)
            ada_take(13)

            def merge(g, bias):
                m = 2 * (g % 4)
                ps = bank[g][:, :]
                dve.wait_ge(y_psum, g + 1)
                if g < 4:
                    for c in range(2):
                        last = nc.vector.scalar_tensor_tensor(
                            out=sgT[:, m + c, :], in0=ps[:, c * SEQ:(c + 1) * SEQ], scalar=bias[:, m + c:m + c + 1],
                            in1=sgT[:, m + c, :], op0=ALU.add, op1=ALU.mult)
                    last.then_inc(y_taken, 1)
                else:
                    t = tmp[:, g % 2, :]
                    st(nc.vector.tensor_tensor(t, ps, flat(sgT[:, KD + m:KD + m + 2, :]), ALU.mult))
                    st.sync()
                    dst = flat(sgT[:, m:m + 2, :])
                    ins = nc.vector.tensor_tensor(dst, dst, t, ALU.add)
                    st(ins) if g < 7 else ins.then_inc(merged, 1)

            for g in range(4):
                merge(g, column(cols, C1, "b_conv_pw"))
            dve.wait_ge(y_taken, 4)
            dve.wait_ge(o_rstd, 1)
            for h in range(GH):
                last = nc.vector.tensor_scalar(xs[:, 1, h * GDV:(h + 1) * GDV],
                                               bank[6 + h // 2][:, (h % 2) * GDV:(h % 2 + 1) * GDV],
                                               rstd[:, 4 + h:5 + h], None, ALU.mult)
            last.then_inc(o_normed, 1)
            for k in range(KD):
                dve.wait_ge(tr_full, 4 + k // 2 + 1)
                last = nc.vector.scalar_tensor_tensor(out=xT[:, k, :], in0=tr_bank(k),
                                                      scalar=column(cols, C1, "g_gla_norm")[:, k:k + 1],
                                                      in1=srT[:, k, :], op0=ALU.mult, op1=ALU.mult)
            last.then_inc(ogT_ready, 1)
            for i in (14, 15):
                ada_sum(i)
            for g in range(4, 8):
                merge(g, None)
            for g in range(4):
                half, t = g // 2, g % 2
                cs = slice(half * 512, (half + 1) * 512)
                dve.wait_ge(out_psum, g + 1)
                st(nc.vector.tensor_tensor(tmp[:, g % 2, :], bank[g][:, :], ga1_row[:, cs], ALU.mult))
                st.sync()
                ins = nc.vector.tensor_tensor(x[:, t, cs], x[:, t, cs], tmp[:, g % 2, :], ALU.add)
                st(ins) if g < 3 else ins.then_inc(x_ready, 1)
            for i in (14, 15):
                ada_take(i)
            norm_scale(dve, 1)
            dve.wait_ge(ada_taken, 16)
            modulation(1, "sh2", "sc2", "g_norm2")
            xT_by_dve(dve, 2, mcol[:, 3, :], mcol[:, 2, :])
            return st

        def tensor_moe(pe):
            norm_transposes(pe, 1, 2)
            pe.wait_ge(xT_act, 2)
            pe.wait_ge(xT_dve, 2)
            for t in range(NT):
                for k in range(KD):
                    last = nc.tensor.matmul(bank[4][:, t * 64:t * 64 + N36], xT[:, k, t * P:(t + 1) * P], wr[:, k, :],
                                            start=(k == 0), stop=(k == KD - 1))
            last.then_inc(router_psum, 1)
            pe.wait_ge(sel_ready, 1)
            nc.tensor.matmul(bank[5][:, 0:NE], K[:, UPPER, :], sel[:, 0, :], start=True, stop=True)
            nc.tensor.matmul(bank[5][:, NE:2 * NE], K[:, UPPER, :], sel[:, 1, :], start=True, stop=False)
            nc.tensor.matmul(bank[5][:, NE:2 * NE], ones, sel[:, 0, :], start=False, stop=True)
            nc.tensor.matmul(bank[5][:, 2 * NE:3 * NE], ones, sel[:, 0, :], start=True, stop=False)
            nc.tensor.matmul(bank[5][:, 2 * NE:3 * NE], ones, sel[:, 1, :], start=False,
                             stop=True).then_inc(place_psum, 1)
            pe.wait_ge(fits_ready, 1)
            few = pe.value_load(fits[0:1, 0:1], min_val=0, max_val=1)
            with pe.If(few > 0):
                tensor_gathered(pe)
            with pe.Else():
                tensor_dense(pe)

        def tensor_gathered(pe):
            def gather(n):
                pe.wait_ge(hot_ready, n + 1)
                for t in range(NT):
                    last = nc.tensor.transpose(bank[3][:, t * P:(t + 1) * P], whot[:, t, :], eye)
                last.then_inc(whotT_psum, 1)

            def rows_of(n, first):
                if not first:
                    pe.wait_ge(ye_act, n)
                    pe.wait_ge(ye_dve, n)
                for half in range(2):
                    for k in range(4):
                        for t in range(NT):
                            f = (half * 4 + k) * P
                            last = nc.tensor.matmul(bank[half][:, k * P:(k + 1) * P], xs[:, t, f:f + P], hot[:, t, :],
                                                    start=(t == 0), stop=(t == NT - 1))
                    last.then_inc(xg_psum, 1)

            gather(0)
            rows_of(0, True)
            for b in range(4, 8):
                nc.tensor.matmul(bank[b][:, :], y[:, 0, 0:P], y[:, 1, 0:512], start=True, stop=False)
            with pe.Fori(0, NE // 4) as i:
                for q in range(2):
                    n = i * 2 + q
                    pe.wait_ge(xg_act, n + 1)
                    pe.wait_ge(xg_dve, n + 1)
                    for e in range(2):
                        if e == 1:
                            pe.wait_ge(whotT_ready, n + 1)
                        for m in range(2):
                            s = wait_piece(pe, J_MOE + expert_index(2 * q + e, m), turn=i * 3)
                            w = slot_w(s, KD, DE)
                            for c in range(DE // P):
                                for k in range(KD):
                                    last = nc.tensor.matmul(
                                        bank[2 + e][:, m * 256 + c * CAP:m * 256 + (c + 1) * CAP],
                                        w[:, k, c * P:(c + 1) * P], xg[:, k, e * CAP:(e + 1) * CAP],
                                        start=(k == 0), stop=(k == KD - 1))
                            last.then_inc(hid_up, 1)
                    for e in range(2):
                        pe.wait_ge(hid_h, i * 8 + (4 * q + 2 * e + 2))
                        s = wait_piece(pe, J_MOE + expert_index(2 * q + e, 2), turn=i * 3)
                        w = slot_w(s, DE // P, D)
                        for half in range(2):
                            for c in range(DE // P):
                                last = nc.tensor.matmul(bank[half][e * CAP:(e + 1) * CAP, :],
                                                        hT[:, e, c * CAP:(c + 1) * CAP],
                                                        w[:, c, half * 512:(half + 1) * 512],
                                                        start=(c == 0), stop=(c == DE // P - 1))
                            last.then_inc(hid_down, 1)
                    gather(n + 1)
                    rows_of(n + 1, False)
                    for t in range(NT):
                        for half in range(2):
                            last = nc.tensor.matmul(bank[4 + 2 * t + half][:, :], whotT[:, q, t * P:(t + 1) * P],
                                                    ye[:, half, :], start=False, stop=False)
                    last.then_inc(scattered, 1)
            for b in range(4, 8):
                last = nc.tensor.matmul(bank[b][:, :], y[:, 0, 0:P], y[:, 1, 0:512], start=False, stop=True)
            last.then_inc(scattered, 1)

        def tensor_dense(pe):
            with pe.Fori(0, NE // 4) as i:
                def up(g):
                    e, hh = g // 2, g % 2
                    for m in range(2):
                        s = wait_piece(pe, J_MOE + expert_index(e, m), turn=i * 3)
                        w = slot_w(s, KD, DE)
                        for c in range(2):
                            f = (2 * hh + c) * P
                            for k in range(KD):
                                last = nc.tensor.matmul(bank[2 * (g % 2) + m][:, c * SEQ:(c + 1) * SEQ],
                                                        w[:, k, f:f + P], xT[:, k, :],
                                                        start=(k == 0), stop=(k == KD - 1))
                    last.then_inc(hid_up, 1)

                def down(g):
                    e, hh = g // 2, g % 2
                    pe.wait_ge(hid_h, i * 8 + g + 1)
                    s = wait_piece(pe, J_MOE + expert_index(e, 2), turn=i * 3)
                    w = slot_w(s, DE // P, D)
                    if hh == 0:
                        pe.wait_ge(moe_taken, i * 4 + e + 1)
                    for t in range(NT):
                        for half in range(2):
                            for c in range(2):
                                last = nc.tensor.matmul(bank[4 + 2 * t + half][:, :],
                                                        hT[:, g % 2, c * SEQ + t * P:c * SEQ + (t + 1) * P],
                                                        w[:, 2 * hh + c, half * 512:(half + 1) * 512],
                                                        start=(hh == 0 and c == 0), stop=(hh == 1 and c == 1))
                    last.then_inc(hid_down, 1)

                up(0)
                for g in range(1, 8):
                    up(g)
                    down(g - 1)
                down(7)

        def scalar_moe(act):
            act.wait_ge(x_ready, 1)
            act.dma_start(gf_row[:, :], a["g_final"].partition_broadcast(P)).then_inc(gf_loaded, 16)
            for n in range(2):
                act.wait_ge(gap_ready, n + 1)
                t = rt[:, :, 4:8] if n == 0 else rt[:, :, 64:65]
                nc.scalar.activation(t, t, ACT.Exp).then_inc(gap_exp, 1)
            act.wait_ge(fits_ready, 1)
            few = act.value_load(fits[0:1, 0:1], min_val=0, max_val=1)
            with act.If(few > 0):
                scalar_gathered(act)
            with act.Else():
                with act.Fori(0, NE // 4) as i:
                    for g in range(8):
                        act.wait_ge(hid_up, i * 8 + g + 1)
                        nc.scalar.activation(sg[:, g % 2, :], bank[2 * (g % 2)][:, :], ACT.Silu).then_inc(hid_silu, 1)
            act.wait_ge(x_ready, 2)
            norm_sums(act, 2)

        def scalar_gathered(act):
            def gathered(n, par):
                act.wait_ge(whotT_psum, n + 1)
                nc.scalar.activation(whotT[:, par, :], bank[3][:, 0:NT * P], ACT.Copy).then_inc(whotT_ready, 1)
                act.wait_ge(xg_psum, n * 2 + 1)
                for k in range(4):
                    last = nc.scalar.activation(xg[:, k, :], bank[0][:, k * P:(k + 1) * P], ACT.Identity,
                                                scale=mcol[:, 3, k:k + 1], bias=mcol[:, 2, k:k + 1])
                last.then_inc(xg_act, 1)

            gathered(0, 0)
            with act.Fori(0, NE // 4) as i:
                for q in range(2):
                    for e in range(2):
                        act.wait_ge(hid_up, i * 8 + (4 * q + 2 * e + 2))
                        for c in range(2):
                            cs = slice(c * 2 * CAP, (c + 1) * 2 * CAP)
                            nc.scalar.activation(sg[:, e, cs], bank[2 + e][:, cs], ACT.Silu).then_inc(hid_silu, 1)
                    act.wait_ge(hid_down, i * 8 + (4 * q + 3))
                    nc.scalar.activation(ye[:, 0, :], bank[0][:, :], ACT.Copy).then_inc(ye_act, 1)
                    gathered(i * 2 + (q + 1), (q + 1) % 2)

        def vector_moe(dve, st):
            dve.wait_ge(x_ready, 1)
            dve.wait_ge(router_psum, 1)
            for t in range(NT):
                st(nc.vector.tensor_tensor(lg[:, t, :], bank[4][:, t * 64:t * 64 + N36], brow[:, :], ALU.add))
            nc.vector.memset(y[:, :, :], 0.0).then_inc(moe_taken, 1)
            st(nc.vector.memset(comb[:, :, NE:], 0.0))
            st(nc.vector.memset(place[:, :, NE:], 0.0))
            st.sync()

            def first_max(values, width, top, hot, weight):
                st(nc.vector.tensor_reduce(top, values, AX.X, ALU.max))
                st.sync()
                st(nc.vector.tensor_tensor(hot, values, top.to_broadcast([P, NT, width]), ALU.is_equal))
                st.sync()
                st(nc.vector.tensor_tensor(hot, hot, K[:, DESC, 0:width].unsqueeze(1).to_broadcast([P, NT, width]),
                                           ALU.mult))
                st.sync()
                st(nc.vector.tensor_reduce(weight, hot, AX.X, ALU.max))
                st.sync()
                st(nc.vector.tensor_tensor(hot, hot, weight.to_broadcast([P, NT, width]), ALU.is_equal))
                st.sync()

            gtop, gsum, wt = rt[:, :, 0:1], rt[:, :, 1:2], rt[:, :, 2:3]
            gexp, ghot = rt[:, :, 4:8], rt[:, :, 8:12]
            own, hot1, hot2, rest = rt[:, :, 16:24], rt[:, :, 24:32], rt[:, :, 32:40], rt[:, :, 40:48]
            top1, top2, gap, tot = rt[:, :, 48:49], rt[:, :, 49:50], rt[:, :, 64:65], rt[:, :, 65:66]
            prod = rt[:, :, 96:128]
            lgr = lg[:, :, 0:NG]
            first_max(lgr, NG, gtop, ghot, wt)
            nc.vector.tensor_tensor(gexp, lgr, gtop.to_broadcast([P, NT, NG]), ALU.subtract).then_inc(gap_ready, 1)
            for t in range(NT):
                st(nc.vector.tensor_tensor(prod[:, t, :].rearrange("p (g e) -> p g e", g=NG),
                                           lg[:, t, NG:N36].rearrange("p (g e) -> p g e", g=NG),
                                           ghot[:, t, :].unsqueeze(2).to_broadcast([P, NG, EPG]), ALU.mult))
            st.sync()
            for t in range(NT):
                st(nc.vector.tensor_reduce(own[:, t, :], prod[:, t, :].rearrange("p (g e) -> p e g", g=NG),
                                           AX.X, ALU.add))
            st.sync()
            first_max(own, EPG, top1, hot1, wt)
            st(nc.vector.scalar_tensor_tensor(out=rest, in0=hot1, scalar=-BIG, in1=own, op0=ALU.mult, op1=ALU.add))
            st.sync()
            first_max(rest, EPG, top2, hot2, wt)
            nc.vector.tensor_tensor(gap, top2, top1, ALU.subtract).then_inc(gap_ready, 1)
            dve.wait_ge(gap_exp, 2)
            st(nc.vector.tensor_reduce(gsum, gexp, AX.X, ALU.add))
            st(nc.vector.tensor_scalar(tot, gap, 1.0, None, ALU.add))
            st.sync()
            st(nc.vector.tensor_tensor(tot, tot, gsum, ALU.mult))
            st.sync()
            st(nc.vector.reciprocal(tot, tot))
            st.sync()
            st(nc.vector.tensor_tensor(gap, gap, tot, ALU.mult))
            st(nc.vector.tensor_tensor(hot1, hot1, tot.to_broadcast([P, NT, EPG]), ALU.mult))
            st.sync()
            st(nc.vector.tensor_tensor(hot2, hot2, gap.to_broadcast([P, NT, EPG]), ALU.mult))
            st.sync()
            st(nc.vector.tensor_tensor(hot1, hot1, hot2, ALU.add))
            st.sync()
            for t in range(NT):
                st(nc.vector.tensor_tensor(comb[:, t, 0:NE].rearrange("p (g e) -> p g e", g=NG),
                                           ghot[:, t, :].unsqueeze(2).to_broadcast([P, NG, EPG]),
                                           hot1[:, t, :].unsqueeze(1).to_broadcast([P, NG, EPG]), ALU.mult))
            st.sync()

            nc.vector.tensor_scalar(sel[:, :, :], comb[:, :, 0:NE], 0.0, None, ALU.is_gt).then_inc(sel_ready, 1)
            dve.wait_ge(place_psum, 1)
            st(nc.vector.tensor_reduce(most[:, :], bank[5][:, 2 * NE:3 * NE], AX.X, ALU.max))
            for t in range(NT):
                st(nc.vector.tensor_scalar(place[:, t, 0:NE], bank[5][:, t * NE:(t + 1) * NE], -1.0, float(P),
                                           ALU.mult, ALU.add))
            st.sync()
            st(nc.vector.tensor_tensor(place[:, :, 0:NE], place[:, :, 0:NE], sel[:, :, :], ALU.mult))
            nc.vector.tensor_scalar(fits[:, :], most[:, :], CAP + 0.5, None, ALU.is_lt).then_inc(fits_ready, 1)
            st.sync()
            dve.wait_ge(fits_ready, 1)
            few = dve.value_load(fits[0:1, 0:1], min_val=0, max_val=1)
            with dve.If(few > 0):
                vector_gathered(dve)
            with dve.Else():
                vector_dense(dve, Steps(dve, branch_steps))
            dve.wait_ge(gf_loaded, 16)
            st(nc.vector.scalar_tensor_tensor(out=scf_row, in0=scf_row, scalar=1.0, in1=gf_row[:, :],
                                              op0=ALU.add, op1=ALU.mult))
            st.sync()
            nc.vector.tensor_tensor(x[:, :, :], x[:, :, :], y[:, :, :], ALU.add).then_inc(x_ready, 1)
            dve.wait_ge(x_ready, 2)
            norm_scale(dve, 2)
            dve.wait_ge(xs_act, 3)
            dve.wait_ge(xs_dve, 3)
            for t in range(NT):
                st(nc.vector.tensor_tensor(y[:, t, :], xs[:, t, :], scf_row, ALU.mult))
            st.sync()
            for t in range(NT):
                last = nc.vector.tensor_tensor(x[:, t, :], y[:, t, :], shf_row, ALU.add)
                if t == 0:
                    last.then_inc(x_first, 1)
            last.then_inc(x_ready, 1)
            dve.wait_ge(x_ready, 3)

        def vector_gathered(dve):
            st = Steps(dve, branch_steps)

            def one_hot(n):
                for t in range(NT):
                    st(nc.vector.tensor_tensor(
                        hot[:, t, :].rearrange("p (e c) -> p e c", e=2),
                        K[:, DESC, 0:CAP].unsqueeze(1).to_broadcast([P, 2, CAP]),
                        place[:, t, bass.ds(n * 2, 2)].unsqueeze(2).to_broadcast([P, 2, CAP]), ALU.is_equal))
                st.sync()
                for t in range(NT):
                    last = nc.vector.tensor_tensor(
                        whot[:, t, :].rearrange("p (e c) -> p e c", e=2),
                        hot[:, t, :].rearrange("p (e c) -> p e c", e=2),
                        comb[:, t, bass.ds(n * 2, 2)].unsqueeze(2).to_broadcast([P, 2, CAP]), ALU.mult)
                    if t < NT - 1:
                        st(last)
                last.then_inc(hot_ready, 1)

            def gathered(n):
                dve.wait_ge(xg_psum, n * 2 + 2)
                for k in range(4, 8):
                    last = nc.vector.tensor_scalar(xg[:, k, :], bank[1][:, (k - 4) * P:(k - 3) * P],
                                                   mcol[:, 3, k:k + 1], mcol[:, 2, k:k + 1], ALU.mult, ALU.add)
                last.then_inc(xg_dve, 1)

            one_hot(0)
            gathered(0)
            for i in st.loop(NE // 4, 6):
                for q in range(2):
                    one_hot(i * 2 + (q + 1))
                    for e in range(2):
                        dve.wait_ge(hid_silu, i * 8 + (4 * q + 2 * e + 2))
                        for c in range(2):
                            cs = slice(c * 2 * CAP, (c + 1) * 2 * CAP)
                            up = bank[2 + e][:, 256 + c * 2 * CAP:256 + (c + 1) * 2 * CAP]
                            nc.vector.tensor_tensor(hT[:, e, cs], sg[:, e, cs], up, ALU.mult).then_inc(hid_h, 1)
                    dve.wait_ge(hid_down, i * 8 + (4 * q + 4))
                    nc.vector.tensor_copy(ye[:, 1, :], bank[1][:, :]).then_inc(ye_dve, 1)
                    gathered(i * 2 + (q + 1))
            dve.wait_ge(scattered, NE // 2 + 1)
            for t in range(NT):
                for half in range(2):
                    cs = slice(half * 512, (half + 1) * 512)
                    st(nc.vector.tensor_tensor(y[:, t, cs], bank[4 + 2 * t + half][:, :], ga2_row[:, cs], ALU.mult))
            st.sync()

        def vector_dense(dve, st):
            for i in st.loop(NE // 4, 12):
                def hidden(g):
                    dve.wait_ge(hid_silu, i * 8 + g + 1)
                    nc.vector.tensor_tensor(hT[:, g % 2, :], sg[:, g % 2, :], bank[2 * (g % 2) + 1][:, :],
                                            ALU.mult).then_inc(hid_h, 1)

                def take(e):
                    dve.wait_ge(hid_down, i * 8 + 2 * e + 2)
                    dve.wait_ge(moe_taken, i * 4 + e + 1)
                    for t in range(NT):
                        for half in range(2):
                            cs = slice(half * 512, (half + 1) * 512)
                            ins = nc.vector.scalar_tensor_tensor(
                                out=y[:, t, cs], in0=bank[4 + 2 * t + half][:, :],
                                scalar=comb[:, t, bass.ds(i * 4 + e, 1)], in1=y[:, t, cs],
                                op0=ALU.mult, op1=ALU.add)
                            if (t, half) == (1, 1):
                                ins.then_inc(moe_taken, 1)
                            else:
                                st(ins)

                hidden(0)
                hidden(1)
                for e in range(3):
                    hidden(2 * e + 2)
                    take(e)
                    hidden(2 * e + 3)
                take(3)
            dve.wait_ge(moe_taken, NE + 1)
            for t in range(NT):
                st(nc.vector.tensor_tensor(y[:, t, :], y[:, t, :], ga2_row, ALU.mult))
            st.sync()

        J_FFN1, J_MIX, J_KV, J_MIXOUT, J_XQ, J_XO, J_FFN2 = 0, 22, 30, 35, 37, 39, 42
        PER_LAYER = 64
        J_SKIPPED = (29, 34, 41)
        assert PER_LAYER % SLOTS == 0

        def slot_of(j):
            return (J_MOE + 3 * NE + j) % SLOTS

        def uses_before(j):
            return sum(1 for i in range(j) if i not in J_SKIPPED and slot_of(i) == slot_of(j))

        LAYER_USES = [sum(1 for j in range(PER_LAYER) if j not in J_SKIPPED and slot_of(j) == s)
                      for s in range(SLOTS)]
        MP = 13
        KAPPA = float(np.exp(-0.5))
        FB = NGRP
        FF0 = 2 * NE
        MATS = [("B", 0, "KK", 0, "dve", 0), ("B", 1, "KK", 1, "dve", 1), ("KK", 0, "B", 0, "dve", 2),
                ("KK", 1, "B", 1, "dve", 3), ("B", 0, "KK2", 0, "act", 0), ("K", 0, "KK", 0, "dve", 4),
                ("K", 1, "KK", 1, "dve", 5), ("K", 0, "KK2", 0, "act", 1), ("B", 0, "R", 0, "dve", 6),
                ("B", 1, "R", 1, "dve", 7), ("B", 0, "R2", 0, "act", 2), ("K", 0, "R", 0, "dve", 8),
                ("K", 1, "R", 1, "dve", 9), ("K", 0, "R2", 0, "act", 3)]

        def wait_piece2(eng, j, l, turn=0):
            s = slot_of(j)
            eng.wait_ge(w_full[s], (l * LAYER_USES[s] + (U_BLOCK2[s] + uses_before(j) + 1) + turn) * 16)
            return s

        def heads4(t):
            return t.rearrange("p (h t) -> p h t", t=P)

        def sync2(sp):
            def load(s, src, k, n):
                sp.dma_start(slot_w(s, k, n), src).then_inc(w_full[s], 16)

            def ffn_piece(l, name, g, p, s):
                if p == 0:
                    w = a[name + "_w_in_2"][l].rearrange("(k p) n -> p k n", p=P)
                    dst = slot_w(s, KD, 512)
                    sp.dma_start(dst[:, :, 0:256], w[:, :, bass.ds(g * 256, 256)]).then_inc(w_full[s], 16)
                    sp.dma_start(dst[:, :, 256:512], w[:, :, bass.ds(g * 256 + D_FF, 256)]).then_inc(up_full[s], 16)
                else:
                    w = a[name + "_w_out_2"][l][bass.ds(g * 256, 256), :]
                    load(s, w.rearrange("(k p) n -> p k n", p=P), 2, D)

            def ffn(l, n):
                f = l * 2 + n
                name = ("ffn1", "ffn2")[n]
                j0 = (J_FFN1, J_FFN2)[n]
                for p in range(SLOTS):
                    if n == 0:
                        before_layer(l, p)
                    else:
                        read(l, j0 + p - SLOTS)
                    ffn_piece(l, name, p // 2, p % 2, slot_of(j0 + p))
                with sp.Fori(0, 4) as i:
                    for p in range(SLOTS):
                        sp.wait_ge(hid_up if p % 2 == 0 else hid_down, f * FB + i * 2 + (FF0 + p // 2 + 1))
                        sp.sem_inc(sp_passed, 1)
                        ffn_piece(l, name, i * 2 + (2 + p // 2), p % 2, slot_of(j0 + p))
                for p in range(2):
                    sp.wait_ge(hid_up if p % 2 == 0 else hid_down, f * FB + (FF0 + 9))
                    sp.sem_inc(sp_passed, 1)
                    ffn_piece(l, name, 10, p, slot_of(j0 + p))

            def before_layer(l, p):
                if p == 0:
                    sp.wait_ge(hid_up, l * (2 * FB) + FF0)
                    sp.sem_inc(sp_passed, 1)
                elif p == 1:
                    sp.wait_ge(hid_down, l * (2 * FB) + (FF0 - 1))
                    sp.sem_inc(sp_passed, 1)
                elif p == 3:
                    sp.wait_ge(hid_down, l * (2 * FB) + FF0)
                    sp.sem_inc(sp_passed, 1)

            def read(l, j):
                if j in J_SKIPPED:
                    j -= SLOTS
                if j < J_MIX:
                    sp.wait_ge(hid_up if j % 2 == 0 else hid_down, l * (2 * FB) + (FF0 + j // 2 + 1))
                    sp.sem_inc(sp_passed, 1)
                elif j < J_KV:
                    n = j - J_MIX
                    sp.wait_ge(mp_full, l * MP + (2 * n + 2 if n < 5 else MP))
                    sp.sem_inc(sp_passed, 1)
                elif j < J_MIXOUT:
                    sp.wait_ge(kv_psum, l * 8 + 2 * (j - J_KV + 1))
                    sp.sem_inc(sp_passed, 1)
                elif j < J_XQ:
                    sp.wait_ge(mo_psum, l * 4 + 2 * (j - J_MIXOUT + 1))
                    sp.sem_inc(sp_passed, 1)
                elif j < J_XO:
                    sp.wait_ge(xq_psum, l * 4 + 2 * (j - J_XQ + 1))
                    sp.sem_inc(sp_passed, 1)
                else:
                    sp.wait_ge(xo_psum, l * 4 + 2 * (j - J_XO + 1))
                    sp.sem_inc(sp_passed, 1)

            with sp.Fori(0, DEPTH_2) as l:
                ffn(l, 0)
                mid = [(a["w_mix_in_2"], 512 * n, 512 if n < 6 else 256) for n in range(7)]
                mid += [(a["xattn_w_kv_2"], 512 * n, 512) for n in range(4)]
                mid += [(a["w_mix_out_2"], 512 * n, 512) for n in range(2)]
                mid += [(a["xattn_w_q_2"], 512 * n, 512) for n in range(2)]
                mid += [(a["xattn_w_o_2"], 512 * n, 512) for n in range(2)]
                js = [j for j in range(J_MIX, J_FFN2) if j not in J_SKIPPED]
                for j, (w, c, width) in zip(js, mid, strict=True):
                    read(l, j - SLOTS)
                    load(slot_of(j), w[l][:, c:c + width].rearrange("(k p) n -> p k n", p=P), KD, width)
                ffn(l, 1)

        def pool2(pool):
            pool.wait_ge(x_ready, 1)
            pool.dma_start(mem[:, :, :], a["mem_2"][0].rearrange("(t p) d -> p t d", p=P)).then_inc(mem_loaded, 16)
            pool.dma_start(relT[0:RB, :], a["rel_bias"]).then_inc(rel_loaded, 16)
            pool.dma_start(onehot[0:RB, :], a["bucket_onehot"]).then_inc(rel_loaded, 16)
            norm_rstd(pool, 2)
            pool.wait_ge(x_ready, 3)
            pool.dma_start(lc[:, :], a["cols2"][0]).then_inc(lc_loaded, 16)
            pool.dma_start(lora[0:64, :], a["rwkv_w_up_2"][0]).then_inc(lc_loaded, 16)
            pool.dma_start(lora[64:P, :], a["rwkv_a_up_2"][0]).then_inc(lc_loaded, 16)
            pool.dma_start(gup[:, :], a["rwkv_g_up_2"][0]).then_inc(lc_loaded, 16)
            norm_rstd(pool, 3)
            pool.wait_ge(bd_ready, 1)
            pool.dma_start(bias_dram.ap(), bydist[0:NH, :].unsqueeze(1).to_broadcast([NH, P, NDIST])
                           ).then_inc(bd_stored, 16)
            pool.wait_ge(bd_stored, 16)
            src = bass.AP(bias_dram, P - 1, [[NDIST - 1, P], [P * NDIST, NH], [1, SEQ]])
            pool.dma_start(biasT[:, :, :], src).then_inc(bias_loaded, 16)
            with pool.Fori(0, DEPTH_2) as l:
                norm_rstd(pool, l * 4 + 4)
                pool.wait_ge(lc_loaded, (l + 1) * 64)
                pool.wait_ge(xT_act, l * 4 + 4)
                pool.wait_ge(xT_dve, l * 4 + 4)
                pool.sem_inc(pool_passed, 1)
                nc.gpsimd.tensor_tensor(gm[:, :, :], memT[:, :, :],
                                        column(lc, C2, "mem_g").unsqueeze(2).to_broadcast([P, KD, SEQ]),
                                        ALU.mult).then_inc(gm_ready, 1)
                norm_rstd(pool, l * 4 + 5)
                pool.wait_ge(kv_act, l * 8 + 4)
                pool.sem_inc(pool_passed, 1)
                pool.dma_start(k_dram.ap(), flat(k_out[:, :, :])).then_inc(k_stored, 16)
                pool.wait_ge(kv_act, l * 8 + 8)
                pool.sem_inc(pool_passed, 1)
                pool.dma_start(v_dram.ap(), flat(v_out[:, :, :])).then_inc(v_stored, 16)
                pool.wait_ge(k_stored, (l + 1) * 16)
                pool.wait_ge(v_stored, (l + 1) * 16)
                pool.wait_ge(ycat, l + 1)
                pool.sem_inc(pool_passed, 1)
                pool.dma_start(flat(kx[:, :, :]), k_dram.ap()).then_inc(kv_loaded, 16)
                pool.dma_start(flat(vx[:, :, :]), v_dram.ap()).then_inc(kv_loaded, 16)
                norm_rstd(pool, l * 4 + 6)
                norm_rstd(pool, l * 4 + 7)
                pool.wait_ge(kv_loaded, (l + 1) * 32)
                pool.wait_ge(x_ready, l * 4 + 7)
                pool.sem_inc(pool_passed, 1)
                nxt = 1
                pool.dma_start(lc[:, :], a["cols2"][nxt]).then_inc(lc_loaded, 16)
                pool.dma_start(lora[0:64, :], a["rwkv_w_up_2"][nxt]).then_inc(lc_loaded, 16)
                pool.dma_start(lora[64:P, :], a["rwkv_a_up_2"][nxt]).then_inc(lc_loaded, 16)
                pool.dma_start(gup[:, :], a["rwkv_g_up_2"][nxt]).then_inc(lc_loaded, 16)
            pool.dma_start(gf2_row[:, :], a["final_norm_g_2"].partition_broadcast(P)).then_inc(gf2_loaded, 16)
            norm_rstd(pool, 12)
            pool.wait_ge(lc_loaded, 3 * 64)

        def tensor2(pe):
            norm_transposes(pe, 3, 3)
            pe.wait_ge(rel_loaded, 32)
            nc.tensor.matmul(bank[4][0:NH, 0:NDIST], relT[0:RB, :], onehot[0:RB, :],
                             start=True, stop=True).then_inc(bd_psum, 1)
            pe.wait_ge(bd_ready, 1)

            def ffn(l, n):
                f = l * 2 + n
                j0 = (J_FFN1, J_FFN2)[n]
                pe.wait_ge(xT_act, l * 4 + (4 + 3 * n))
                pe.wait_ge(xT_dve, l * 4 + (4 + 3 * n))

                def up(g, par, i=None):
                    turn = 0 if i is None else i
                    s = wait_piece2(pe, j0 + 2 * g, l, turn)
                    w = slot_w(s, KD, 512)
                    first = 0 if n == 0 else (FB // 2 if par == 0 else (FB + 1) // 2)
                    pe.wait_ge(up_full[s], (l * FB + (first + g // 2 + 1) + turn) * 16)
                    for u in range(2):
                        for c in range(2):
                            for k in range(KD):
                                m = u * 256 + c * P
                                last = nc.tensor.matmul(bank[2 * par + u][:, c * SEQ:(c + 1) * SEQ],
                                                        w[:, k, m:m + P], xT[:, k, :],
                                                        start=(k == 0), stop=(k == KD - 1))
                    last.then_inc(hid_up, 1)

                def down(g, par, i=None, start=False, stop=False):
                    turn = 0 if i is None else i
                    count = f * FB + (FF0 + g + 1) if i is None else f * FB + i * 2 + (FF0 + g + 1)
                    pe.wait_ge(hid_h, count)
                    s = wait_piece2(pe, j0 + 2 * g + 1, l, turn)
                    w = slot_w(s, 2, D)
                    for t in range(NT):
                        for half in range(2):
                            for c in range(2):
                                last = nc.tensor.matmul(bank[4 + 2 * t + half][:, :],
                                                        fh[:, par, c * SEQ + t * P:c * SEQ + (t + 1) * P],
                                                        w[:, c, half * 512:(half + 1) * 512],
                                                        start=(start and c == 0), stop=(stop and c == 1))
                        if stop and t == 0:
                            last.then_inc(ffn_out, 1)
                    last.then_inc(hid_down, 1)

                up(0, 0)
                up(1, 1)
                down(0, 0, start=True)
                with pe.Fori(0, 4) as i:
                    up(2, 0, i)
                    down(1, 1, i)
                    up(3, 1, i)
                    down(2, 0, i)
                up(10, 0)
                down(9, 1)
                down(10, 0, stop=True)

            def project(l, m):
                if m >= 8:
                    pe.wait_ge(mp_act, l * MP + (m - 7))
                b = bank[m % 8]
                if m < 11:
                    s = wait_piece2(pe, J_MIX + m // 2, l)
                    w = slot_w(s, KD, 512)
                    for c in range(2):
                        col = (m % 2) * 256 + c * P
                        for k in range(KD):
                            last = nc.tensor.matmul(b[:, c * SEQ:(c + 1) * SEQ], w[:, k, col:col + P], xT[:, k, :],
                                                    start=(k == 0), stop=(k == KD - 1))
                else:
                    t = m - 11
                    for part in range(2):
                        s = wait_piece2(pe, J_MIX + 5 + part, l)
                        w = slot_w(s, KD, 512)[:, :, 256:512] if part == 0 else slot_w(s, KD, 256)
                        for k in range(KD):
                            last = nc.tensor.matmul(b[:, part * 256:(part + 1) * 256], xT[:, k, t * P:(t + 1) * P],
                                                    w[:, k, :], start=(k == 0), stop=(k == KD - 1))
                last.then_inc(mp_full, 1)

            def rwkv_operands(l):
                pe.wait_ge(lo_ready, l * 2 + 2)
                pe.wait_ge(mp_act, (l + 1) * MP)
                for g in range(6):
                    kind, pair = g // 2, g % 2
                    for c in range(2):
                        m = 2 * pair + c
                        o = bank[g][:, c * SEQ:(c + 1) * SEQ]
                        ms_ = slice(m * P, (m + 1) * P)
                        if kind == 0:
                            last = nc.tensor.matmul(o, lora[0:64, ms_], pT[0:64, 12, :], start=True, stop=True)
                        elif kind == 1:
                            last = nc.tensor.matmul(o, lora[64:P, ms_], pT[64:P, 12, :], start=True, stop=True)
                        else:
                            last = nc.tensor.matmul(o, gup[:, ms_], pT[:, 13, :], start=True, stop=True)
                    last.then_inc(lora_psum, 1)
                pe.wait_ge(kk_sq, l + 1)
                for n in range(2):
                    nc.tensor.matmul(bank[6 + n][:, :], K[:, HEADS, :], flat(cw[:, 2 * n:2 * n + 2, :]),
                                     start=True, stop=True).then_inc(kk_psum, 1)
                pe.wait_ge(lora_act, (l + 1) * 6)
                for t in range(NT):
                    for m in range(4):
                        last = nc.tensor.transpose(bank[2 + t][:, m * P:(m + 1) * P],
                                                   pT[:, 8 + m, t * P:(t + 1) * P], eye)
                    last.then_inc(vt_psum, 1)

            def cross_kv(l, g):
                if g >= 2:
                    pe.wait_ge(kv_act, l * 8 + (g - 1))
                s = wait_piece2(pe, J_KV + g // 2, l)
                w = slot_w(s, KD, 512)
                if g >= 4:
                    t = g % 2
                    for k in range(KD):
                        last = nc.tensor.matmul(bank[g % 2][:, :], gm[:, k, t * P:(t + 1) * P], w[:, k, :],
                                                start=(k == 0), stop=(k == KD - 1))
                else:
                    for c in range(2):
                        m = 2 * (g % 2) + c
                        for k in range(KD):
                            last = nc.tensor.matmul(bank[g % 2][:, c * SEQ:(c + 1) * SEQ], w[:, k, m * P:(m + 1) * P],
                                                    gm[:, k, :], start=(k == 0), stop=(k == KD - 1))
                last.then_inc(kv_psum, 1)

            def bonus(l):
                pe.wait_ge(kv_act, (l + 1) * 8)
                pe.wait_ge(rk_ready, l + 1)
                for n in range(2):
                    nc.tensor.matmul(bank[n][:, :], K[:, HEADS, :], flat(cw[:, 2 * n:2 * n + 2, :]),
                                     start=True, stop=True).then_inc(rk_psum, 1)

            def moba_attention(l):
                def scores(h):
                    r = slice((h % 2) * 64, (h % 2) * 64 + 64)
                    if h >= 2:
                        pe.wait_ge(mb_sb, l * NH + (h - 1))
                    b = bank[4 + h % 2]
                    nc.tensor.matmul(b[:, 0:P], qm[r, h // 2, 0:P], km[r, h // 2, 0:P], start=True, stop=True)
                    nc.tensor.matmul(b[:, P:384], qm[r, h // 2, P:SEQ], km[r, h // 2, :],
                                     start=True, stop=True).then_inc(mb_s, 1)

                def turned(h):
                    pe.wait_ge(mb_p, l * NH + (h + 1))
                    if h >= 2:
                        pe.wait_ge(mb_tc, l * NH + (h - 1))
                    b = bank[6 + h % 2]
                    for c, (dst, src) in enumerate(((0, 0), (P, P), (2 * P, 2 * P))):
                        last = nc.tensor.transpose(b[:, dst:dst + P], sm[:, h % 2, src:src + P], eye)
                    last.then_inc(mb_t, 1)

                def values(h):
                    pe.wait_ge(mb_tc, l * NH + (h + 1))
                    r = slice((h % 2) * 64, (h % 2) * 64 + 64)
                    o = bank[2 + h // 4][r, ((h // 2) % 2) * SEQ:((h // 2) % 2 + 1) * SEQ]
                    hs = slice(h * 64, (h + 1) * 64)
                    nc.tensor.matmul(o, vm[:, 0, hs], pmT[:, h % 2, 0:SEQ], start=True, stop=False)
                    nc.tensor.matmul(o[:, P:SEQ], vm[:, 1, hs], pmT[:, h % 2, SEQ:384],
                                     start=False, stop=True).then_inc(mb_o, 1)

                pe.wait_ge(kk_ss, (l + 1) * 2)
                pe.wait_ge(vt_ready, (l + 1) * 2)
                scores(0)
                scores(1)
                pe.wait_ge(gm_ready, l + 1)
                for g in range(4):
                    cross_kv(l, g)
                for h in range(NH):
                    turned(h)
                    if h + 2 < NH:
                        scores(h + 2)
                    values(h)
                    if h < 4:
                        cross_kv(l, 4 + h)

            def rwkv_heads(l, hb):
                r = l * 2 + hb
                rows_ = slice(hb * 64, hb * 64 + 64)
                c0, c1 = slice(0, P), slice(P, SEQ)

                def f(name, m, c):
                    if name == "R2":
                        return R2[rows_, m, :]
                    if name == "KK2":
                        return KK2[rows_, m, :]
                    t = {"B": aT, "KK": kk}.get(name)
                    if t is not None:
                        return t[rows_, m, c]
                    return pT[rows_, m + (4 if name == "K" else 0), c]

                if hb == 0:
                    pe.wait_ge(fac_ready, l + 1)
                    pe.wait_ge(k_stored, (l + 1) * 16)
                    pe.wait_ge(mb_oc, (l + 1) * 2)
                    pe.wait_ge(bonus_ready, l + 1)
                else:
                    pe.wait_ge(yy_taken, l * 2 + 1)
                for idx, (lhs, lc_, rhs, rc_, by, nth) in enumerate(MATS):
                    if idx >= 8:
                        _, _, _, _, pby, pn = MATS[idx - 8]
                        pe.wait_ge(mat_dve if pby == "dve" else mat_act, r * (10 if pby == "dve" else 4) + (pn + 1))
                    for n in range(4):
                        last = nc.tensor.matmul(bank[idx % 8][:, n * P:(n + 1) * P], f(lhs, n, (c0, c1)[lc_]),
                                                f(rhs, n, (c0, c1)[rc_]), start=True, stop=True)
                    last.then_inc(mat_full, 1)
                pe.wait_ge(mat_dve, (r + 1) * 10)
                pe.wait_ge(mat_act, (r + 1) * 4)
                pe.wait_ge(inv_init, r + 1)
                for n in range(1, 7):
                    q = r * 12 + 2 * (n - 1)
                    for ch in range(2):
                        if n > 1:
                            pe.wait_ge(inv_xs, r * 12 + (2 * (n - 2) + ch + 1))
                        for h in range(4):
                            hs = slice(h * P, (h + 1) * P)
                            last = nc.tensor.matmul(bank[ch][:, hs], Lt[:, ch, hs], X[:, ch, hs],
                                                    start=True, stop=True)
                        last.then_inc(inv_p, 1)
                    for ch in range(2):
                        pe.wait_ge(inv_pm, q + (ch + 1))
                        if n > 1:
                            pe.wait_ge(inv_ys, r * 10 + (2 * (n - 2) + ch + 1))
                        for h in range(4):
                            hs = slice(h * P, (h + 1) * P)
                            last = nc.tensor.matmul(bank[2 + ch][:, hs], Y[:, ch, hs], Pm[:, ch, hs],
                                                    start=True, stop=True)
                        last.then_inc(inv_x, 1)
                        if n < 6:
                            for h in range(4):
                                hs = slice(h * P, (h + 1) * P)
                                last = nc.tensor.matmul(bank[4 + ch][:, hs], Pm[:, ch, hs], Y[:, ch, hs],
                                                        start=True, stop=True)
                            last.then_inc(inv_y, 1)
                pe.wait_ge(inv_xs, (r + 1) * 12)
                vs = [slice((2 * n + hb) * 64, (2 * n + hb + 1) * 64) for n in range(4)]
                us = [slice((4 * hb + n) * 64, (4 * hb + n + 1) * 64) for n in range(4)]
                for ch in range(2):
                    for n in range(4):
                        hs, o = slice(n * P, (n + 1) * P), bank[6][:, n * 64:(n + 1) * 64]
                        if ch == 0:
                            last = nc.tensor.matmul(o, Luk[:, 0, hs], vt[:, 0, vs[n]], start=True, stop=True)
                        else:
                            nc.tensor.matmul(o, Luk[:, 2, hs], vt[:, 0, vs[n]], start=True, stop=False)
                            nc.tensor.matmul(o, Luk[:, 1, hs], vt[:, 1, vs[n]], start=False, stop=False)
                            last = nc.tensor.matmul(o, Noff[:, hs], U[:, 0, us[n]], start=False, stop=True)
                    last.then_inc(u_psum, 1)
                    pe.wait_ge(u_taken, r * 4 + (2 * ch + 1))
                    for n in range(4):
                        hs = slice(n * P, (n + 1) * P)
                        last = nc.tensor.matmul(bank[7][:, n * 64:(n + 1) * 64], X[:, ch, hs],
                                                Pm[:, ch, n * 64:(n + 1) * 64], start=True, stop=True)
                    last.then_inc(u_psum, 1)
                    pe.wait_ge(u_taken, r * 4 + (2 * ch + 2))
                for n in range(4):
                    hs = slice(n * P, (n + 1) * P)
                    o = bank[n // 2][rows_, (n % 2) * SEQ:(n % 2 + 1) * SEQ]
                    v0, v1, u0, u1 = vt[:, 0, vs[n]], vt[:, 1, vs[n]], U[:, 0, us[n]], U[:, 1, us[n]]
                    nc.tensor.matmul(o[:, c0], u0, Mrb[:, 0, hs], start=True, stop=False)
                    nc.tensor.matmul(o[:, c0], v0, Mrk[:, 0, hs], start=False, stop=True)
                    nc.tensor.matmul(o[:, c1], u0, Mrb[:, 2, hs], start=True, stop=False)
                    nc.tensor.matmul(o[:, c1], v0, Mrk[:, 2, hs], start=False, stop=False)
                    nc.tensor.matmul(o[:, c1], u1, Mrb[:, 1, hs], start=False, stop=False)
                    last = nc.tensor.matmul(o[:, c1], v1, Mrk[:, 1, hs], start=False, stop=True)
                last.then_inc(yy_psum, 1)

            def to_tokens(l, src, j0, done, b0):
                for half in range(2):
                    s = wait_piece2(pe, j0 + half, l)
                    w = slot_w(s, KD, 512)
                    for t in range(NT):
                        for k in range(KD):
                            last = nc.tensor.matmul(bank[b0 + 2 * half + t][:, :], src[:, k, t * P:(t + 1) * P],
                                                    w[:, k, :], start=(k == 0), stop=(k == KD - 1))
                        last.then_inc(done, 1)

            def mixer_out(l, half, ks):
                s = wait_piece2(pe, J_MIXOUT + half, l)
                w = slot_w(s, KD, 512)
                for t in range(NT):
                    for k in ks:
                        last = nc.tensor.matmul(bank[4 + 2 * half + t][:, :], xT[:, k, t * P:(t + 1) * P],
                                                w[:, k, :], start=(k == 4), stop=(k == 3))
                    if ks[-1] == 3:
                        last.then_inc(mo_psum, 1)

            def group_norm(l):
                pe.wait_ge(yy_taken, (l + 1) * 2)
                for n in range(2):
                    nc.tensor.matmul(bank[n][:, :], K[:, HEADS, :], flat(xT[:, 2 * n:2 * n + 2, :]),
                                     start=True, stop=True).then_inc(gn_psum, 1)
                mixer_out(l, 0, (4, 5, 6, 7))
                for n in range(2):
                    pe.wait_ge(gn_sq, l * 2 + (n + 1))
                    nc.tensor.matmul(bank[2 + n][:, :], K[:, HEADS, :], xs[:, 0, n * 512:(n + 1) * 512],
                                     start=True, stop=True).then_inc(gn_psum, 1)
                mixer_out(l, 1, (4, 5, 6, 7))
                pe.wait_ge(ycat, l + 1)
                mixer_out(l, 0, (0, 1, 2, 3))
                mixer_out(l, 1, (0, 1, 2, 3))

            def cross_attention(l):
                norm_transposes(pe, l * 4 + 6, l * 4 + 6)
                pe.wait_ge(xT_act, l * 4 + 6)
                pe.wait_ge(xT_dve, l * 4 + 6)
                for g in range(4):
                    s = wait_piece2(pe, J_XQ + g // 2, l)
                    w = slot_w(s, KD, 512)
                    for c in range(2):
                        m = 2 * (g % 2) + c
                        for k in range(KD):
                            last = nc.tensor.matmul(bank[g][:, c * SEQ:(c + 1) * SEQ], w[:, k, m * P:(m + 1) * P],
                                                    xT[:, k, :], start=(k == 0), stop=(k == KD - 1))
                    last.then_inc(xq_psum, 1)
                pe.wait_ge(kv_loaded, (l + 1) * 32)
                pe.wait_ge(xq_act, (l + 1) * 4)

                def scores(h):
                    if h >= 2:
                        pe.wait_ge(xa_e, l * XH + (h - 1))
                    for t in range(NT):
                        for c in range(2):
                            last = nc.tensor.matmul(bank[4 + h % 2][:, t * SEQ:(t + 1) * SEQ],
                                                    qx[:, 2 * h + c, t * P:(t + 1) * P], kx[:, 2 * h + c, :],
                                                    start=(c == 0), stop=(c == 1))
                    last.then_inc(xa_s, 1)

                def turned(h):
                    pe.wait_ge(xa_p, l * XH + (h + 1))
                    if h >= 2:
                        pe.wait_ge(xa_tc, l * XH + (h - 1))
                    for t in range(NT):
                        for m in range(2):
                            last = nc.tensor.transpose(bank[6 + h % 2][:, m * SEQ + t * P:m * SEQ + (t + 1) * P],
                                                       sx[:, h % 2, t * SEQ + m * P:t * SEQ + (m + 1) * P], eye)
                    last.then_inc(xa_t, 1)

                def values(h):
                    pe.wait_ge(xa_tc, l * XH + (h + 1))
                    for c in range(2):
                        for m in range(2):
                            last = nc.tensor.matmul(bank[h][:, c * SEQ:(c + 1) * SEQ],
                                                    vx[:, m, h * XHD + c * P:h * XHD + (c + 1) * P],
                                                    pxT[:, h % 2, m * SEQ:(m + 1) * SEQ],
                                                    start=(m == 0), stop=(m == 1))
                    last.then_inc(xa_o, 1)

                scores(0)
                scores(1)
                for h in range(XH):
                    turned(h)
                    if h + 2 < XH:
                        scores(h + 2)
                    values(h)
                pe.wait_ge(xa_oc, (l + 1) * XH)
                to_tokens(l, xT, J_XO, xo_psum, 0)

            with pe.Fori(0, DEPTH_2) as l:
                norm_transposes(pe, l * 4 + 4, l * 4 + 4)
                ffn(l, 0)
                norm_transposes(pe, l * 4 + 5, l * 4 + 5)
                pe.wait_ge(xT_act, l * 4 + 5)
                pe.wait_ge(xT_dve, l * 4 + 5)
                for m in range(MP):
                    project(l, m)
                rwkv_operands(l)
                moba_attention(l)
                bonus(l)
                for hb in range(2):
                    rwkv_heads(l, hb)
                group_norm(l)
                cross_attention(l)
                norm_transposes(pe, l * 4 + 7, l * 4 + 7)
                ffn(l, 1)
        def scalar2(act, st):
            act.wait_ge(mem_loaded, 16)
            act.wait_ge(x_ready, 3)
            norm_sums(act, 3, mem)
            for k in (0, 1, 4, 5):
                act.wait_ge(tr_full, 12 + k // 2 + 1)
                last = nc.scalar.activation(memT[:, k, :], tr_bank(k), ACT.Copy)
            last.then_inc(xT_act, 1)
            act.wait_ge(tr_full, 16)

            def ffn(l, n):
                f = l * 2 + n
                gain = column(lc, C2, ("ffn1_g", "ffn2_g")[n])
                act.wait_ge(x_first, l * 4 + 1 + 3 * n)
                if n == 0:
                    act.wait_ge(lc_loaded, (l + 1) * 64)
                norm_sums(act, l * 4 + 4 + 3 * n, ready=l * 4 + 3 + 3 * n)
                xT_by_act(act, l * 4 + 4 + 3 * n, gain)

                def silu(par, count):
                    act.wait_ge(hid_up, count)
                    nc.scalar.activation(fs[:, par, :], bank[2 * par][:, :], ACT.Silu).then_inc(hid_silu, 1)

                silu(0, f * FB + FF0 + 1)
                with act.Fori(0, FB // 2) as i:
                    silu(1, f * FB + i * 2 + (FF0 + 2))
                    silu(0, f * FB + i * 2 + (FF0 + 3))

            def mixer(l):
                act.wait_ge(x_first, l * 4 + 2)
                norm_sums(act, l * 4 + 5, ready=l * 4 + 4)
                xT_by_act(act, l * 4 + 5, column(lc, C2, "mix_g"))

                def take(m):
                    act.wait_ge(mp_full, l * MP + (m + 1))
                    b = bank[m % 8][:, :]
                    if m < 7:
                        nc.scalar.activation(flat(pT[:, 2 * m:2 * m + 2, :]), b, ACT.Copy).then_inc(mp_act, 1)
                    elif m < 11:
                        t, n = (qm, m - 7) if m < 9 else (km, m - 9)
                        nc.scalar.activation(flat(t[:, 2 * n:2 * n + 2, :]), b, ACT.Copy,
                                             scale=HD ** -0.5 if m < 9 else 1.0).then_inc(mp_act, 1)
                    else:
                        nc.scalar.activation(vm[:, m - 11, :], b, ACT.Copy).then_inc(mp_act, 1)

                for m in range(7):
                    take(m)
                act.wait_ge(shifted, l * 7 + 4)
                for k in range(4):
                    st(nc.scalar.activation(kk[:, k, :], pT[:, 4 + k, :], ACT.Copy,
                                            scale=column(lc, C2, "k_k")[:, k:k + 1]))
                st.sync()
                nc.scalar.activation(flat(cw[:, :, :]), flat(kk[:, :, :]), ACT.Square).then_inc(kk_sq, 1)
                take(7)
                take(8)
                act.wait_ge(shifted, l * 7 + 7)
                nc.scalar.activation(pT[0:64, 12, :], pT[0:64, 12, :], ACT.Tanh).then_inc(lo_ready, 1)
                nc.scalar.activation(pT[:, 13, :], pT[:, 13, :], ACT.Sigmoid).then_inc(lo_ready, 1)
                for m in range(9, 13):
                    take(m)
                for n in range(2):
                    act.wait_ge(kk_ss, l * 2 + (n + 1))
                    t = flat(bon[:, 2 * n:2 * n + 2, :])
                    nc.scalar.activation(t, t, ACT.Sqrt).then_inc(kk_rs, 1)
                for g in range(6):
                    act.wait_ge(lora_psum, l * 6 + (g + 1))
                    kind, pair = g // 2, g % 2
                    if kind < 2:
                        for c in range(2):
                            m = 2 * pair + c
                            last = nc.scalar.activation((lw, aT)[kind][:, m, :], bank[g][:, c * SEQ:(c + 1) * SEQ],
                                                        ACT.Sigmoid,
                                                        bias=column(lc, C2, ("w0", "a0")[kind])[:, m:m + 1])
                    else:
                        last = nc.scalar.activation(flat(gT[:, 2 * pair:2 * pair + 2, :]), bank[g][:, :], ACT.Copy)
                    last.then_inc(lora_act, 1)
                for t in range(NT):
                    act.wait_ge(vt_psum, l * 2 + (t + 1))
                    nc.scalar.activation(vt[:, t, :], bank[2 + t][:, :], ACT.Copy).then_inc(vt_ready, 1)
                act.wait_ge(dec2_ready, l + 1)
                nc.scalar.activation(E3, E1, ACT.Exp, scale=KAPPA).then_inc(e_ready, 1)
                act.wait_ge(e_ready, l * 4 + 1)
                nc.scalar.activation(E1, E1, ACT.Exp, scale=-KAPPA).then_inc(e_ready, 1)
                nc.scalar.activation(flat(lw[:, :, :]), flat(lw[:, :, :]), ACT.Exp, scale=-KAPPA).then_inc(e_ready, 1)
                nc.scalar.activation(small[:, 0:4], small[:, 0:4], ACT.Exp, scale=-KAPPA).then_inc(e_ready, 1)

                def expo(h):
                    act.wait_ge(mb_max, l * NH + (h + 1))
                    o = 4 * (h % 2)
                    nc.scalar.activation(sm[:, h % 2, 0:P], sm[:, h % 2, 0:P], ACT.Exp,
                                         bias=small[:, 8 + o:9 + o], accum_out=small[:, 16 + o:17 + o])
                    nc.scalar.activation(sm[:, h % 2, P:384], sm[:, h % 2, P:384], ACT.Exp,
                                         bias=small[:, 9 + o:10 + o],
                                         accum_out=small[:, 17 + o:18 + o]).then_inc(mb_e, 1)

                def take_kv(g):
                    act.wait_ge(kv_psum, l * 8 + (g + 1))
                    dst = flat(k_out[:, 2 * g:2 * g + 2, :]) if g < 4 else v_out[:, g % 2, (g // 2 - 2) * 512:
                                                                                 (g // 2 - 1) * 512]
                    nc.scalar.activation(dst, bank[g % 2][:, :], ACT.Copy).then_inc(kv_act, 1)

                for g in range(3):
                    take_kv(g)
                expo(0)
                take_kv(3)
                for h in range(NH):
                    if h + 1 < NH:
                        expo(h + 1)
                    act.wait_ge(mb_t, l * NH + (h + 1))
                    if h >= 2:
                        act.wait_ge(mb_o, l * NH + (h - 1))
                    nc.scalar.activation(pmT[:, h % 2, :], bank[6 + h % 2][:, 0:384], ACT.Copy).then_inc(mb_tc, 1)
                    if 1 <= h <= 4:
                        take_kv(3 + h)
                    if h % 4 == 3:
                        act.wait_ge(mb_o, l * NH + (h + 1))
                        m = 4 + 2 * (h // 4)
                        nc.scalar.activation(flat(xT[:, m:m + 2, :]), bank[2 + h // 4][:, :],
                                             ACT.Copy).then_inc(mb_oc, 1)
                for hb in range(2):
                    r = l * 2 + hb
                    for idx, (_, _, _, _, by, n) in enumerate(MATS):
                        if by == "act":
                            act.wait_ge(mat_full, r * len(MATS) + (idx + 1))
                            dst = (Noff[:, :], Luk[:, 2, :], Mrb[:, 2, :], Mrk[:, 2, :])[n]
                            nc.scalar.activation(dst, bank[idx % 8][:, :], ACT.Copy).then_inc(mat_act, 1)
                    for n in range(4):
                        act.wait_ge(u_psum, r * 4 + (n + 1))
                        if n % 2 == 0:
                            nc.scalar.activation(Pm[:, n // 2, 0:256], bank[6][:, 0:256], ACT.Copy,
                                                 scale=-1.0).then_inc(u_taken, 1)
                        else:
                            nc.scalar.activation(U[:, n // 2, hb * 256:(hb + 1) * 256], bank[7][:, 0:256],
                                                 ACT.Copy).then_inc(u_taken, 1)
                    act.wait_ge(yy_psum, r + 1)
                    rows_ = slice(hb * 64, hb * 64 + 64)
                    for n in range(2):
                        last = nc.scalar.activation(flat(xT[rows_, 2 * n:2 * n + 2, :]), bank[n][rows_, :], ACT.Copy)
                    last.then_inc(yy_taken, 1)
                for n in range(2):
                    act.wait_ge(gn_xc, l * 2 + (n + 1))
                    nc.scalar.activation(xs[:, 0, n * 512:(n + 1) * 512], flat(xT[:, 2 * n:2 * n + 2, :]),
                                         ACT.Square).then_inc(gn_sq, 1)
                for n in range(2):
                    act.wait_ge(gn_var, l * 2 + (n + 1))
                    t = xs[:, 1, n * 512:(n + 1) * 512]
                    nc.scalar.activation(t, t, ACT.Sqrt).then_inc(gn_rs, 1)
                for k in range(4):
                    act.wait_ge(gn_norm, l * 2 + (k // 2 + 1))
                    last = nc.scalar.activation(xT[:, k, :], xT[:, k, :], ACT.Identity,
                                                scale=column(lc, C2, "ln_g")[:, k:k + 1],
                                                bias=column(lc, C2, "ln_b")[:, k:k + 1])
                    if k % 2:
                        last.then_inc(gn_aff, 1)

            def cross(l):
                act.wait_ge(x_first, l * 4 + 3)
                norm_sums(act, l * 4 + 6, ready=l * 4 + 5)
                xT_by_act(act, l * 4 + 6, column(lc, C2, "xattn_g"))
                for g in range(4):
                    act.wait_ge(xq_psum, l * 4 + (g + 1))
                    nc.scalar.activation(flat(qx[:, 2 * g:2 * g + 2, :]), bank[g][:, :], ACT.Copy).then_inc(xq_act, 1)

                def expo(h):
                    act.wait_ge(xa_max, l * XH + (h + 1))
                    if h >= 2:
                        act.wait_ge(xa_t, l * XH + (h - 1))
                    for t in range(NT):
                        ts = slice(t * SEQ, (t + 1) * SEQ)
                        o = 4 * (h % 2) + t
                        last = nc.scalar.activation(sx[:, h % 2, ts], bank[4 + h % 2][:, ts], ACT.Exp,
                                                    bias=xsm[:, o:o + 1], scale=XHD ** -0.5,
                                                    accum_out=xsm[:, o + 2:o + 3])
                    last.then_inc(xa_e, 1)

                def out(h):
                    act.wait_ge(xa_o, l * XH + (h + 1))
                    nc.scalar.activation(flat(xT[:, 2 * h:2 * h + 2, :]), bank[h][:, :], ACT.Copy).then_inc(xa_oc, 1)

                expo(0)
                for h in range(XH):
                    if h + 1 < XH:
                        expo(h + 1)
                    act.wait_ge(xa_t, l * XH + (h + 1))
                    if h >= 2:
                        act.wait_ge(xa_o, l * XH + (h - 1))
                    nc.scalar.activation(pxT[:, h % 2, :], bank[6 + h % 2][:, :], ACT.Copy).then_inc(xa_tc, 1)
                    if h:
                        out(h - 1)
                out(XH - 1)

            for l in st.loop(DEPTH_2, 4):
                ffn(l, 0)
                mixer(l)
                cross(l)
                ffn(l, 1)
            act.wait_ge(x_first, 9)
            norm_sums(act, 12, ready=11)

        def vector2(dve, st):
            dve.wait_ge(mem_loaded, 16)
            norm_scale(dve, 3, mem)
            for k in (2, 3, 6, 7):
                dve.wait_ge(tr_full, 12 + k // 2 + 1)
                last = nc.vector.tensor_copy(memT[:, k, :], tr_bank(k))
            last.then_inc(xT_dve, 1)
            dve.wait_ge(bd_psum, 1)
            st(nc.vector.tensor_copy(bydist[0:NH, 0:SEQ], bank[4][0:NH, 0:SEQ]))
            nc.vector.memset(bydist[0:NH, SEQ:NDIST], -BIG).then_inc(bd_ready, 1)

            def ffn(l, n):
                f = l * 2 + n
                e = l * 4 + 4 + 3 * n
                if n == 0:
                    dve.wait_ge(lc_loaded, (l + 1) * 64)
                norm_scale(dve, e)
                xT_by_dve(dve, e, column(lc, C2, ("ffn1_g", "ffn2_g")[n]))

                def hidden(par, count):
                    dve.wait_ge(hid_silu, count)
                    nc.vector.tensor_tensor(fh[:, par, :], fs[:, par, :], bank[2 * par + 1][:, :],
                                            ALU.mult).then_inc(hid_h, 1)

                hidden(0, f * FB + FF0 + 1)
                with dve.Fori(0, FB // 2) as i:
                    hidden(1, f * FB + i * 2 + (FF0 + 2))
                    hidden(0, f * FB + i * 2 + (FF0 + 3))
                for t in range(NT):
                    if t == 0:
                        dve.wait_ge(ffn_out, f + 1)
                    else:
                        dve.wait_ge(hid_down, f * FB + (FF0 + FB))
                    for half in range(2):
                        cs = slice(half * 512, (half + 1) * 512)
                        last = nc.vector.scalar_tensor_tensor(out=x[:, t, cs], in0=bank[4 + 2 * t + half][:, :],
                                                              scalar=0.5, in1=x[:, t, cs], op0=ALU.mult, op1=ALU.add)
                    if t == 0:
                        last.then_inc(x_first, 1)
                last.then_inc(x_ready, 1)
                dve.wait_ge(x_ready, e)

            def add_tokens(b0, done, count, e):
                for g in range(4):
                    half, t = g // 2, g % 2
                    cs = slice(half * 512, (half + 1) * 512)
                    dve.wait_ge(done, count + (g + 1))
                    last = nc.vector.tensor_tensor(x[:, t, cs], x[:, t, cs], bank[b0 + g][:, :], ALU.add)
                    if g == 2:
                        last.then_inc(x_first, 1)
                last.then_inc(x_ready, 1)
                dve.wait_ge(x_ready, e)

            def mixer(l):
                norm_scale(dve, l * 4 + 5)
                xT_by_dve(dve, l * 4 + 5, column(lc, C2, "mix_g"))
                for m in range(7):
                    dve.wait_ge(mp_act, l * MP + (m + 1))
                    p = pT[:, 2 * m:2 * m + 2, :]
                    d = bon[:, 2 * (m % 2):2 * (m % 2) + 2, :]
                    st(nc.vector.tensor_tensor(d[:, :, 1:SEQ], p[:, :, 0:SEQ - 1], p[:, :, 1:SEQ], ALU.subtract))
                    st(nc.vector.tensor_scalar(d[:, :, 0:1], p[:, :, 0:1], -1.0, None, ALU.mult))
                    st.sync()
                    for c in range(2):
                        last = nc.vector.scalar_tensor_tensor(
                            out=p[:, c, :], in0=d[:, c, :], scalar=column(lc, C2, "mu")[:, 2 * m + c:2 * m + c + 1],
                            in1=p[:, c, :], op0=ALU.mult, op1=ALU.add)
                    last.then_inc(shifted, 1)
                dve.wait_ge(shifted, (l + 1) * 7)
                for n in range(2):
                    dve.wait_ge(kk_psum, l * 2 + (n + 1))
                    nc.vector.tensor_scalar(flat(bon[:, 2 * n:2 * n + 2, :]), bank[6 + n][:, :], 1e-24, None,
                                            ALU.max).then_inc(kk_ss, 1)
                dve.wait_ge(lora_act, l * 6 + 4)
                for m in range(4):
                    for ch in range(2):
                        cs = slice(ch * P, (ch + 1) * P)
                        st(nc.vector.tensor_tensor_scan(cw[:, m, cs], ones, lw[:, m, cs], 0.0,
                                                        ALU.mult, ALU.add))
                st(nc.vector.tensor_scalar(small[:, 4:8], column(lc, C2, "k_a"), -1.0, 1.0, ALU.mult, ALU.add))
                st.sync()
                mid = P // 2 - 1
                c8 = cw[:, :, :].rearrange("p m (c t) -> p (m c) t", t=P)
                st(nc.vector.tensor_tensor(E1.rearrange("p (a t) -> p a t", t=P), c8,
                                           c8[:, :, mid:mid + 1].to_broadcast([P, 8, P]), ALU.subtract))
                sm4 = small[:, 0:4].unsqueeze(2)
                st(nc.vector.tensor_tensor(sm4, cw[:, :, P - 1:P], cw[:, :, mid:mid + 1], ALU.subtract))
                st.sync()
                st(nc.vector.tensor_tensor(sm4, sm4, cw[:, :, P + mid:P + mid + 1], ALU.add))
                nc.vector.tensor_tensor(flat(lw[:, :, :]), E1, flat(lw[:, :, :]), ALU.subtract).then_inc(dec2_ready, 1)
                st.sync()
                for m in range(4):
                    st(nc.vector.tensor_scalar(cw[:, m, :], aT[:, m, :], column(lc, C2, "k_a")[:, m:m + 1],
                                               small[:, 4 + m:5 + m], ALU.mult, ALU.add))
                st.sync()
                st(nc.vector.tensor_tensor(pT[:, 4:8, :], pT[:, 4:8, :], cw[:, :, :], ALU.mult))
                st.sync()
                for m in range(4):
                    last = nc.vector.scalar_tensor_tensor(out=cw[:, m, :], in0=pT[:, m, :],
                                                          scalar=column(lc, C2, "r_k")[:, m:m + 1],
                                                          in1=pT[:, 4 + m, :], op0=ALU.mult, op1=ALU.mult)
                last.then_inc(rk_ready, 1)
                dve.wait_ge(kk_rs, l * 2 + 2)
                st(nc.vector.reciprocal(flat(bon[:, :, :]), flat(bon[:, :, :])))
                st.sync()
                st(nc.vector.tensor_tensor(kk[:, :, :], kk[:, :, :], bon[:, :, :], ALU.mult))
                st.sync()
                st(nc.vector.tensor_tensor(aT[:, :, :], kk[:, :, :], aT[:, :, :], ALU.mult))
                st.sync()
                dve.wait_ge(e_ready, l * 4 + 4)
                e1, e3 = (e.rearrange("p (m t) -> p m t", t=SEQ) for e in (E1, E3))
                st(nc.vector.tensor_tensor(pT[:, 0:4, :], pT[:, 0:4, :], e1, ALU.mult))
                st(nc.vector.tensor_tensor(kk[:, :, :], kk[:, :, :], lw[:, :, :], ALU.mult))
                st(nc.vector.tensor_tensor(aT[:, :, :], aT[:, :, :], e3, ALU.mult))
                st(nc.vector.tensor_tensor(pT[:, 4:8, :], pT[:, 4:8, :], e3, ALU.mult))
                st.sync()
                for m in range(4):
                    st(nc.vector.tensor_scalar(R2[:, m, :], pT[:, m, P:SEQ], small[:, m:m + 1], None, ALU.mult))
                    ins = nc.vector.tensor_scalar(KK2[:, m, :], kk[:, m, P:SEQ], small[:, m:m + 1], None, ALU.mult)
                    st(ins) if m < 3 else ins.then_inc(fac_ready, 1)

                def logits(h):
                    dve.wait_ge(mb_s, l * NH + (h + 1))
                    b = bank[4 + h % 2]
                    o = 8 + 4 * (h % 2)
                    st(nc.vector.tensor_tensor(sm[:, h % 2, 0:P], b[:, 0:P], biasT[:, h, P:SEQ], ALU.add))
                    nc.vector.tensor_tensor(sm[:, h % 2, P:384], b[:, P:384], biasT[:, h, :],
                                            ALU.add).then_inc(mb_sb, 1)
                    dve.wait_ge(mb_sb, l * NH + (h + 1))
                    nc.vector.tensor_reduce(small[:, o:o + 1], sm[:, h % 2, 0:P], AX.X, ALU.max, negate=True)
                    nc.vector.tensor_reduce(small[:, o + 1:o + 2], sm[:, h % 2, P:384], AX.X, ALU.max,
                                            negate=True).then_inc(mb_max, 1)

                def probs(h):
                    dve.wait_ge(mb_e, l * NH + (h + 1))
                    o = 16 + 4 * (h % 2)
                    st(nc.vector.reciprocal(small[:, o + 2:o + 4], small[:, o:o + 2]))
                    st.sync()
                    st(nc.vector.tensor_scalar(sm[:, h % 2, 0:P], sm[:, h % 2, 0:P], small[:, o + 2:o + 3], None,
                                               ALU.mult))
                    nc.vector.tensor_scalar(sm[:, h % 2, P:384], sm[:, h % 2, P:384], small[:, o + 3:o + 4], None,
                                            ALU.mult).then_inc(mb_p, 1)

                dve.wait_ge(bias_loaded, 16)
                logits(0)
                for h in range(NH):
                    if h + 1 < NH:
                        if h >= 1:
                            dve.wait_ge(mb_t, l * NH + h)
                        logits(h + 1)
                    probs(h)
                for n in range(2):
                    dve.wait_ge(rk_psum, l * 2 + (n + 1))
                    last = nc.vector.tensor_tensor(flat(bon[:, 2 * n:2 * n + 2, :]), bank[n][:, :],
                                                   flat(pT[:, 8 + 2 * n:10 + 2 * n, :]), ALU.mult)
                last.then_inc(bonus_ready, 1)

                def bc(n, k=8):
                    return K[:, n, :].unsqueeze(1).to_broadcast([P, k, P])

                def eight(t):
                    return t[:, :, :].rearrange("p c (h t) -> p (c h) t", t=P)

                def invert_pairs(r, hb):
                    dve.wait_ge(mat_dve, r * 10 + 4)
                    if hb == 0:
                        dve.wait_ge(v_stored, (l + 1) * 16)
                    st(nc.vector.tensor_tensor(eight(X), eight(Nd), bc(LEV), ALU.mult))
                    st(nc.vector.tensor_tensor(eight(Y), eight(Lt), bc(LEVT), ALU.mult))
                    st.sync()
                    st(nc.vector.tensor_tensor(eight(X), bc(EYE), eight(X), ALU.subtract))
                    nc.vector.tensor_tensor(eight(Y), bc(EYE), eight(Y), ALU.subtract).then_inc(inv_init, 1)

                for hb in range(2):
                    r = l * 2 + hb
                    for idx, (_, _, _, _, by, n) in enumerate(MATS):
                        if by == "dve":
                            dve.wait_ge(mat_full, r * len(MATS) + (idx + 1))
                            dst, mask = ((Nd[:, 0, :], UPPER), (Nd[:, 1, :], UPPER), (Lt[:, 0, :], LOWER),
                                         (Lt[:, 1, :], LOWER), (Luk[:, 0, :], UPPER), (Luk[:, 1, :], UPPER),
                                         (Mrb[:, 0, :], UPPER_EQ), (Mrb[:, 1, :], UPPER_EQ),
                                         (Mrk[:, 0, :], UPPER_EQ), (Mrk[:, 1, :], UPPER_EQ))[n]
                            nc.vector.tensor_tensor(heads4(dst), heads4(bank[idx % 8][:, :]),
                                                    K[:, mask, :].unsqueeze(1).to_broadcast([P, 4, P]),
                                                    ALU.mult).then_inc(mat_dve, 1)
                            if n == 3:
                                invert_pairs(r, hb)
                    dve.wait_ge(inv_init, r + 1)
                    for n in range(1, 7):
                        q = r * 12 + 2 * (n - 1)
                        for ch in range(2):
                            dve.wait_ge(inv_p, q + (ch + 1))
                            nc.vector.tensor_tensor(heads4(Pm[:, ch, :]), heads4(bank[ch][:, :]), bc(LEV + n, 4),
                                                    ALU.mult).then_inc(inv_pm, 1)
                        for ch in range(2):
                            dve.wait_ge(inv_x, q + (ch + 1))
                            nc.vector.tensor_tensor(X[:, ch, :], X[:, ch, :], bank[2 + ch][:, :],
                                                    ALU.subtract).then_inc(inv_xs, 1)
                            if n < 6:
                                dve.wait_ge(inv_y, r * 10 + (2 * (n - 1) + ch + 1))
                                nc.vector.tensor_tensor(Y[:, ch, :], Y[:, ch, :], bank[4 + ch][:, :],
                                                        ALU.subtract).then_inc(inv_ys, 1)
                        dve.wait_ge(inv_xs, q + 2)
                for n in range(2):
                    dve.wait_ge(gn_psum, l * 4 + (n + 1))
                    t = flat(xT[:, 2 * n:2 * n + 2, :])
                    nc.vector.scalar_tensor_tensor(out=t, in0=bank[n][:, :], scalar=-1.0 / HD, in1=t,
                                                   op0=ALU.mult, op1=ALU.add).then_inc(gn_xc, 1)
                for n in range(2):
                    dve.wait_ge(gn_psum, l * 4 + (n + 3))
                    nc.vector.tensor_scalar(xs[:, 1, n * 512:(n + 1) * 512], bank[2 + n][:, :], 1.0 / HD, LNX_EPS,
                                            ALU.mult, ALU.add).then_inc(gn_var, 1)
                for n in range(2):
                    dve.wait_ge(gn_rs, l * 2 + (n + 1))
                    t = flat(xT[:, 2 * n:2 * n + 2, :])
                    st(nc.vector.reciprocal(xs[:, 1, n * 512:(n + 1) * 512], xs[:, 1, n * 512:(n + 1) * 512]))
                    st.sync()
                    nc.vector.tensor_tensor(t, t, xs[:, 1, n * 512:(n + 1) * 512], ALU.mult).then_inc(gn_norm, 1)
                for n in range(2):
                    dve.wait_ge(gn_aff, l * 2 + (n + 1))
                    st(nc.vector.tensor_tensor(xT[:, 2 * n:2 * n + 2, :], xT[:, 2 * n:2 * n + 2, :],
                                               bon[:, 2 * n:2 * n + 2, :], ALU.add))
                st.sync()
                nc.vector.tensor_tensor(xT[:, 0:4, :], xT[:, 0:4, :], gT[:, :, :], ALU.mult).then_inc(ycat, 1)
                add_tokens(4, mo_psum, l * 4, l * 4 + 5)

            def cross(l):
                norm_scale(dve, l * 4 + 6)
                xT_by_dve(dve, l * 4 + 6, column(lc, C2, "xattn_g"))

                def maxima(h):
                    dve.wait_ge(xa_s, l * XH + (h + 1))
                    o = 4 * (h % 2)
                    st(nc.vector.tensor_reduce(xsm[:, o:o + 2],
                                               bank[4 + h % 2][:, :].rearrange("p (t m) -> p t m", t=NT),
                                               AX.X, ALU.max))
                    st.sync()
                    nc.vector.tensor_scalar(xsm[:, o:o + 2], xsm[:, o:o + 2], -XHD ** -0.5, None,
                                            ALU.mult).then_inc(xa_max, 1)

                def probs(h):
                    dve.wait_ge(xa_e, l * XH + (h + 1))
                    o = 4 * (h % 2)
                    st(nc.vector.reciprocal(xsm[:, 8 + o:10 + o], xsm[:, o + 2:o + 4]))
                    st.sync()
                    for t in range(NT):
                        s_ = sx[:, h % 2, t * SEQ:(t + 1) * SEQ]
                        last = nc.vector.tensor_scalar(s_, s_, xsm[:, 8 + o + t:9 + o + t], None, ALU.mult)
                    last.then_inc(xa_p, 1)

                maxima(0)
                for h in range(XH):
                    if h + 1 < XH:
                        maxima(h + 1)
                    probs(h)
                add_tokens(0, xo_psum, l * 4, l * 4 + 6)

            for l in st.loop(DEPTH_2, VECTOR_STEPS):
                ffn(l, 0)
                mixer(l)
                cross(l)
                ffn(l, 1)
            norm_scale(dve, 12)
            dve.wait_ge(xs_act, 13)
            dve.wait_ge(xs_dve, 13)
            dve.wait_ge(gf2_loaded, 16)
            for t in range(NT):
                last = nc.vector.tensor_tensor(x[:, t, :], xs[:, t, :], gf2_row[:, :], ALU.mult)
            last.then_inc(x_ready, 1)

        block = ctx.enter_context(nc.Block())

        @block.sync
        def _(sp):
            sync1(sp)
            sync2(sp)
            sp.wait_ge(x_ready, 12)
            sp.dma_start(out[0].rearrange("(t p) d -> p t d", p=P), x[:, :, :]).then_inc(out_stored, 16)
            sp.wait_ge(out_stored, 16)

        @block.gpsimd
        def _(pool):
            pool1(pool)
            pool2(pool)

        @block.tensor
        def _(pe):
            tensor1(pe)
            tensor_moe(pe)
            tensor2(pe)

        @block.scalar
        def _(act):
            st = scalar1(act)
            scalar_moe(act)
            scalar2(act, st)

        @block.vector
        def _(dve):
            st = vector1(dve)
            vector_moe(dve, st)
            vector2(dve, st)


def kernel(**inputs):
    import concourse.bacc as bacc
    from concourse.bass_utils import run_bass_kernel_spmd

    def tiles(v):
        v = v.reshape(v.shape[:-1] + (v.shape[-1] // P, P))
        return np.swapaxes(v, -1, -2)

    i = {k: np.asarray(v) for k, v in inputs.items()}
    b_ada = i["b_ada"][0].reshape(6, D)
    first = {"c": i["c"][0], "g_norm1": i["g_norm1"][0], "sh1": b_ada[0], "sc1": b_ada[1], "sh2": b_ada[3],
             "sc2": b_ada[4], **{n: i[n][0] for n in ("b_dw", "g_conv_ln", "b_conv_ln", "b_conv_pw", "b_a2",
                                                     "g_gla_norm", "g_norm2")}}
    parts = [tiles(first[n]) for n in C1 if n != "w_dw"]
    parts.append(np.transpose(i["w_dw"][0, :, 0, :].reshape(CONV_WIDTH, 4, P), (2, 1, 0)).reshape(P, 4 * CONV_WIDTH))
    second = {"ffn1_g": "ffn1_norm_g_2", "mix_g": "mix_norm_g_2", "mu": "rwkv_mu_2", "w0": "rwkv_w0_2",
              "a0": "rwkv_a0_2", "k_k": "rwkv_k_k_2", "k_a": "rwkv_k_a_2", "r_k": "rwkv_r_k_2",
              "ln_g": "rwkv_ln_g_2", "ln_b": "rwkv_ln_b_2", "xattn_g": "xattn_norm_g_2",
              "mem_g": "mem_norm_g_2", "ffn2_g": "ffn2_norm_g_2"}
    arrays = {n: i[n] for n in ("x", "w_ada", "b_ada", "w_in", "w_conv_pw", "w_a2", "w_gla_o", "w_out", "w_router_g",
                                "b_router_g", "w_router_e", "b_router_e", "w1", "w3", "w2", "w_ada_f", "b_ada_f",
                                "g_final", "mem_2", "final_norm_g_2", "ffn1_w_in_2", "ffn1_w_out_2", "w_mix_in_2",
                                "w_mix_out_2", "rwkv_w_up_2", "rwkv_a_up_2", "rwkv_g_up_2", "xattn_w_q_2",
                                "xattn_w_kv_2", "xattn_w_o_2", "ffn2_w_in_2", "ffn2_w_out_2")}
    arrays["cols1"] = np.concatenate(parts, axis=1)
    arrays["cols2"] = np.concatenate([tiles(i[second[n]].reshape(DEPTH_2, -1)) for n in C2], axis=2)
    arrays["rel_bias"] = i["rel_bias_2"].T
    arrays["const_tiles"] = const_tiles()
    arrays["bucket_onehot"] = bucket_onehot()
    nc = bacc.Bacc("TRN2", target_bir_lowering=False, num_devices=1)
    arrays = {n: np.ascontiguousarray(v) for n, v in arrays.items()}
    aps = {n: nc.dram_tensor("in_" + n, v.shape, F32, kind="ExternalInput").ap() for n, v in arrays.items()}
    out = nc.dram_tensor("out", (1, SEQ, D), F32, kind="ExternalOutput").ap()
    build(nc, aps, out)
    r = run_bass_kernel_spmd(nc, [{"in_" + n: v for n, v in arrays.items()}], core_ids=[0])
    return r.results[0]["out"]
```
